# Optimizing a Trainium2 kernel written in Bass

```python
import math
import jax, jax.numpy as jnp
from jax import lax
import numpy as np

D_MODEL = 1024
BATCH = 1
SEQ = 128
DEPTH = 2
DEC_BATCH = 1
DEC_SEQ = 512
PAST_LEN = 128

GRID_W = 64
N_HEADS = 16
N_KV_HEADS = 4
HEAD_DIM = D_MODEL // N_HEADS
Q_W = N_HEADS * HEAD_DIM
KV_W = N_KV_HEADS * HEAD_DIM
AXIS_DIM = HEAD_DIM // 2
ROPE_THETA = 10000.0
Q_BLOCK = 128
D_CONV = D_MODEL // 2
CONV_K = 31
N_EXPERTS = 16
N_GROUPS = 4
EXPERTS_PER_GROUP = N_EXPERTS // N_GROUPS
TOP_K = 2
D_EXPERT = D_MODEL // 4
IN_W = Q_W + 2 * KV_W + 2 * D_CONV + 2 * D_MODEL
EPS = 1e-6

kernel_name = "hybrid_prefix_diffusion_gqa_conformer_moe_step"

def rmsnorm(x, g):
    x32 = x.astype(jnp.float32)
    y = x32 * lax.rsqrt(jnp.mean(x32 * x32, axis=-1, keepdims=True) + EPS)
    return (y * g.astype(jnp.float32)).astype(x.dtype)

def layernorm(x, g, b):
    x32 = x.astype(jnp.float32)
    mu = jnp.mean(x32, axis=-1, keepdims=True)
    var = jnp.mean(jnp.square(x32 - mu), axis=-1, keepdims=True)
    y = (x32 - mu) * lax.rsqrt(var + EPS) * g.astype(jnp.float32) + b.astype(jnp.float32)
    return y.astype(x.dtype)

def axial_rope_tables(n_tokens):
    rows = n_tokens // GRID_W
    row = jnp.repeat(jnp.arange(rows), GRID_W).astype(jnp.float32)
    col = jnp.tile(jnp.arange(GRID_W), rows).astype(jnp.float32)
    inv = 1.0 / (ROPE_THETA ** (jnp.arange(0, AXIS_DIM, 2, dtype=jnp.float32) / AXIS_DIM))
    ar = row[:, None] * inv[None, :]
    ac = col[:, None] * inv[None, :]
    cos = jnp.concatenate([jnp.cos(ar), jnp.cos(ar), jnp.cos(ac), jnp.cos(ac)], axis=-1)
    sin = jnp.concatenate([jnp.sin(ar), jnp.sin(ar), jnp.sin(ac), jnp.sin(ac)], axis=-1)
    return cos, sin

def apply_rope(x, cos, sin):
    x32 = x.astype(jnp.float32)
    a1, a2, b1, b2 = jnp.split(x32, 4, axis=-1)
    rot = jnp.concatenate([-a2, a1, -b2, b1], axis=-1)
    y = x32 * cos[None, :, None, :] + rot * sin[None, :, None, :]
    return y.astype(x.dtype)

def block_attention(q, k, v):
    b, sq, _, dh = q.shape
    g = N_HEADS // N_KV_HEADS
    nb = sq // Q_BLOCK
    qb = q.reshape(b, nb, Q_BLOCK, N_KV_HEADS, g, dh).transpose(1, 0, 2, 3, 4, 5)
    scale = 1.0 / math.sqrt(dh)

    def one_block(qblk):
        s = jnp.einsum('bqkgd,bskd->bkgqs', qblk, k).astype(jnp.float32) * scale
        p = jax.nn.softmax(s, axis=-1).astype(v.dtype)
        return jnp.einsum('bkgqs,bskd->bqkgd', p, v)

    o = lax.map(one_block, qb)
    return o.transpose(1, 0, 2, 3, 4, 5).reshape(b, sq, N_HEADS * dh)

def depthwise_conv(x, w, bias):
    pad = CONV_K // 2
    y = lax.conv_general_dilated(
        x, w[:, None, :].astype(x.dtype), window_strides=(1,), padding=[(pad, pad)],
        dimension_numbers=('NWC', 'WIO', 'NWC'), feature_group_count=x.shape[-1])
    return y + bias

def grouped_moe(u, w_router, router_bias, w_gate, w_up, w_down):
    b, s, d = u.shape
    t = u.reshape(b * s, d)
    scores = jax.nn.softmax((t @ w_router).astype(jnp.float32), axis=-1)
    sel = scores + router_bias.astype(jnp.float32)[None, :]
    grp = sel.reshape(-1, N_GROUPS, EXPERTS_PER_GROUP)
    grp_score = jnp.sum(lax.top_k(grp, 2)[0], axis=-1)
    gidx = jnp.argmax(grp_score, axis=-1)
    in_grp = (jnp.arange(N_EXPERTS) // EXPERTS_PER_GROUP)[None, :] == gidx[:, None]
    masked = jnp.where(in_grp, sel, -jnp.inf)
    _, eidx = lax.top_k(masked, TOP_K)
    wsel = jnp.take_along_axis(scores, eidx, axis=-1)
    wsel = wsel / jnp.sum(wsel, axis=-1, keepdims=True)
    combine = jnp.sum(jax.nn.one_hot(eidx, N_EXPERTS, dtype=jnp.float32) * wsel[..., None], axis=1)
    hg = jnp.einsum('td,edf->tef', t, w_gate)
    hu = jnp.einsum('td,edf->tef', t, w_up)
    h = jax.nn.silu(hg) * hu * combine.astype(t.dtype)[..., None]
    y = jnp.einsum('tef,efd->td', h, w_down)
    return y.reshape(b, s, d)

def trunk_layer(h, cvec, rope, ctx_k, ctx_v, norm1_g, w_ada, b_ada, w_in, q_norm_g, k_norm_g,
                w_attn_o, conv_w, conv_b, conv_ln_g, conv_ln_b, w_conv_o, w_out, norm2_g,
                w_router, router_bias, w_gate, w_up, w_down):
    b, s, _ = h.shape
    mod = jax.nn.silu(cvec) @ w_ada + b_ada
    sh1, sc1, g1, sh2, sc2, g2 = jnp.split(mod, 6, axis=-1)
    u = rmsnorm(h, norm1_g) * (1.0 + sc1) + sh1
    proj = u @ w_in
    q, k, v, a_glu, gates = jnp.split(
        proj, np.cumsum([Q_W, KV_W, KV_W, 2 * D_CONV]).tolist(), axis=-1)
    q = rmsnorm(q.reshape(b, s, N_HEADS, HEAD_DIM), q_norm_g)
    k = rmsnorm(k.reshape(b, s, N_KV_HEADS, HEAD_DIM), k_norm_g)
    v = v.reshape(b, s, N_KV_HEADS, HEAD_DIM)
    if rope is not None:
        q = apply_rope(q, rope[0], rope[1])
        k_att = apply_rope(k, rope[0], rope[1])
    else:
        k_att = k
    if ctx_k is not None:
        keys = jnp.concatenate([ctx_k.astype(k_att.dtype), k_att], axis=1)
        vals = jnp.concatenate([ctx_v.astype(v.dtype), v], axis=1)
    else:
        keys, vals = k_att, v
    attn_br = block_attention(q, keys, vals) @ w_attn_o
    ga, gb = jnp.split(a_glu, 2, axis=-1)
    cv = depthwise_conv(ga * jax.nn.sigmoid(gb), conv_w, conv_b)
    cv = jax.nn.silu(layernorm(cv, conv_ln_g, conv_ln_b))
    conv_br = cv @ w_conv_o
    gate_a, gate_c = jnp.split(gates, 2, axis=-1)
    merged = jax.nn.sigmoid(gate_a) * attn_br + jax.nn.sigmoid(gate_c) * conv_br
    h = h + g1 * (merged @ w_out)
    u2 = rmsnorm(h, norm2_g) * (1.0 + sc2) + sh2
    h = h + g2 * grouped_moe(u2, w_router, router_bias, w_gate, w_up, w_down)
    return h, k, v

def setup_inputs(seed: int = 0) -> dict:
    key = jax.random.key(seed)
    ks = jax.random.split(key, 32)
    f32 = jnp.float32

    def nrm(k, shape, scale):
        return jax.random.normal(k, shape, f32) * scale

    D = D_MODEL
    return {
        'x_prompt': nrm(ks[0], (BATCH, SEQ, D), 1.0),
        'x_sample': nrm(ks[1], (DEC_BATCH, DEC_SEQ, D), 1.0),
        'cache_k': nrm(ks[2], (DEC_BATCH, DEPTH, PAST_LEN, N_KV_HEADS, HEAD_DIM), 1.0),
        'cache_v': nrm(ks[3], (DEC_BATCH, DEPTH, PAST_LEN, N_KV_HEADS, HEAD_DIM), 1.0),
        'c': nrm(ks[4], (DEC_BATCH, D), 1.0),
        'c_ctx': nrm(ks[5], (D,), 1.0),
        'norm1_g': 1.0 + nrm(ks[6], (DEPTH, D), 0.02),
        'w_ada': nrm(ks[7], (DEPTH, D, 6 * D), 0.5 * D ** -0.5),
        'b_ada': nrm(ks[8], (DEPTH, 6 * D), 0.02),
        'w_in': nrm(ks[9], (DEPTH, D, IN_W), D ** -0.5),
        'q_norm_g': 1.0 + nrm(ks[10], (DEPTH, HEAD_DIM), 0.02),
        'k_norm_g': 1.0 + nrm(ks[11], (DEPTH, HEAD_DIM), 0.02),
        'w_attn_o': nrm(ks[12], (DEPTH, Q_W, D), Q_W ** -0.5),
        'conv_w': nrm(ks[13], (DEPTH, CONV_K, D_CONV), CONV_K ** -0.5),
        'conv_b': nrm(ks[14], (DEPTH, D_CONV), 0.02),
        'conv_ln_g': 1.0 + nrm(ks[15], (DEPTH, D_CONV), 0.02),
        'conv_ln_b': nrm(ks[16], (DEPTH, D_CONV), 0.02),
        'w_conv_o': nrm(ks[17], (DEPTH, D_CONV, D), D_CONV ** -0.5),
        'w_out': nrm(ks[18], (DEPTH, D, D), D ** -0.5),
        'norm2_g': 1.0 + nrm(ks[19], (DEPTH, D), 0.02),
        'w_router': nrm(ks[20], (D, N_EXPERTS), D ** -0.5),
        'router_bias': nrm(ks[21], (N_EXPERTS,), 0.01),
        'w_gate': nrm(ks[22], (DEPTH, N_EXPERTS, D, D_EXPERT), D ** -0.5),
        'w_up': nrm(ks[23], (DEPTH, N_EXPERTS, D, D_EXPERT), D ** -0.5),
        'w_down': nrm(ks[24], (DEPTH, N_EXPERTS, D_EXPERT, D), D_EXPERT ** -0.5),
        'final_norm_g': 1.0 + nrm(ks[25], (D,), 0.02),
    }

def reference(x_prompt, x_sample, cache_k, cache_v, c, c_ctx, norm1_g, w_ada, b_ada, w_in,
              q_norm_g, k_norm_g, w_attn_o, conv_w, conv_b, conv_ln_g, conv_ln_b, w_conv_o,
              w_out, norm2_g, w_router, router_bias, w_gate, w_up, w_down, final_norm_g):
    n_lat = x_sample.shape[1]
    rope = axial_rope_tables(n_lat)
    c_ctx_vec = c_ctx[None, None, :]
    c_vec = c[:, None, :]

    hp = x_prompt
    hs = x_sample
    ks_list = []
    vs_list = []
    for l in range(DEPTH):
        shared = (norm1_g[l], w_ada[l], b_ada[l], w_in[l], q_norm_g[l], k_norm_g[l],
                  w_attn_o[l], conv_w[l], conv_b[l], conv_ln_g[l], conv_ln_b[l], w_conv_o[l],
                  w_out[l], norm2_g[l], w_router, router_bias, w_gate[l], w_up[l], w_down[l])
        hp, k_ctx, v_ctx = trunk_layer(hp, c_ctx_vec, None, None, None, *shared)
        ks_list.append(k_ctx)
        vs_list.append(v_ctx)
        hs, _, _ = trunk_layer(hs, c_vec, rope, cache_k[:, l], cache_v[:, l], *shared)

    y_prompt = rmsnorm(hp, final_norm_g)
    y_sample = rmsnorm(hs, final_norm_g)
    new_k = jnp.stack(ks_list, axis=1)
    new_v = jnp.stack(vs_list, axis=1)
    return (y_prompt, y_sample, new_k, new_v)


_drawn_inputs = setup_inputs


def setup_inputs(seed=0):
    import zlib

    import numpy as np

    out = dict(_drawn_inputs(seed))
    spreads = {}
    factors = {'cache_k': 3.371,
     'cache_v': 2.797,
     'q_norm_g': 3.439,
     'conv_ln_g': 3.364,
     'conv_ln_b': 6.157,
     'final_norm_g': 2.795}
    for name, (base, spread) in spreads.items():
        noise = np.random.default_rng([zlib.crc32(name.encode()), seed]).standard_normal(out[name].shape)
        drawn = base * np.exp(spread * noise) if base else spread * noise
        out[name] = __import__('jax').numpy.asarray(drawn.astype(out[name].dtype))
    for name, factor in factors.items():
        out[name] = (out[name] * factor).astype(out[name].dtype)
    return out
```

```python
from contextlib import ExitStack

import numpy as np
import concourse.bass as bass
from concourse import mybir

F32, F32R = mybir.dt.float32, mybir.dt.float32r
U32, I32 = mybir.dt.uint32, mybir.dt.int32
ALU, ACT, AX = mybir.AluOpType, mybir.ActivationFunctionType, mybir.AxisListType

P = 128
D = 1024
DEPTH = 2
KC = D // P
LT, NT = 4, 5
NLAT, NTOK = LT * P, NT * P
HALF = NTOK // 2
NH, NKV, DH = 16, 4, 64
GQ = NH // NKV
QW, KVW = NH * DH, NKV * DH
DC, CCH = 512, 4
TAPS, PAD = 31, 15
NE, NG, EPG, DE = 16, 4, 4, 256
EPS = 1e-6
UNIT = 2048
CW = PAD + NLAT + PAD + PAD + P + PAD
CO = CW - 2 * PAD
CTX0 = NLAT + 2 * PAD
MAXT = (2 * NTOK) // P + NE
SKIP = 1 << 20

Q0, K0, GA0, GB0 = 0, QW, QW + 2 * KVW, QW + 2 * KVW + DC
GATE0 = QW + 2 * KVW + 2 * DC
SH1, SC1, G1, SH2, SC2, G2 = (i * D for i in range(6))

N_ADA, N_QKV, N_GLU, N_GATE, N_CO, N_OUT = 24, 6, 4, 16, 4, 4
U_QKV = N_ADA
U_GLU = U_QKV + N_QKV
U_GATE = U_GLU + N_GLU
U_CO = U_GATE + N_GATE
U_OUT = U_CO + N_CO
U_MOE = U_OUT + N_OUT
N_UNITS = U_MOE + 3 * NE


class Ledger:

    def __init__(self, known=None):
        self.known = known
        self.section = "before"
        self.count = {"before": {}, "layer": {}, "after": {}}
        self.events = {}
        self.alias = {}
        self.banks = {}

    def raised(self, sem, event, by):
        n = self.count[self.section].get(sem, 0) + by
        self.count[self.section][sem] = n
        if event is not None:
            assert event not in self.events or self.section == "before", event
            self.events[event] = (sem, self.section, n)

    def order_drains(self):
        n = {}
        for name, b in self.banks.items():
            if ("drained", name) in self.events:
                n[b] = n.get(b, 0) + 1
                sem, section, _ = self.events["drained", name]
                self.events["drained", name] = (sem, section, n[b])

    def value(self, event, l, previous):
        event = self.known.alias.get(event, event)
        sem, section, n = self.known.events[event]
        before = self.known.count["before"].get(sem, 0)
        per = self.known.count["layer"].get(sem, 0)
        if section == "before":
            return sem, n
        if section == "after":
            return sem, before + DEPTH * per + n
        if l is None:
            return sem, before + (DEPTH - 1) * per + n
        n += before - (per if previous else 0)
        assert n > 0, event
        return sem, l * per + n


class Counts:

    def __init__(self, ledger, sems):
        self.led, self.sems, self.l, self.steps = ledger, sems, None, 0

    def at(self, *event, previous=False):
        if self.led.known is None:
            return self.sems("uncounted"), 1
        sem, value = self.led.value(event, self.l, previous)
        return self.sems(sem), value

    def up(self, sem, *event, by=1):
        self.led.raised(sem, event or None, by)
        return self.sems(sem), by

    def step(self):
        self.steps += 1
        return self.up("v_step", "v", self.steps)

    def bank(self, name):
        return self.led.banks.get(name, 0) if self.led.known is None else self.led.known.banks[name]

    def filled(self, name):
        return self.up(f"psum_full{self.bank(name)}", "filled", name)

    def drained(self, name):
        return self.up(f"psum_drained{self.bank(name)}", "drained", name)


def build(nc, io, out, ledger):
    ctx = ExitStack()
    with ctx:
        _build(nc, io, out, ledger, ctx)


def _build(nc, io, out, ledger, ctx):
    semd = {}

    def sems(name):
        if name not in semd:
            semd[name] = ctx.enter_context(nc.semaphore(name))
        return semd[name]

    base = (nc.sbuf_base + 63) // 64 * 64
    KB = 1024
    R_RAW = base
    R_W = R_RAW + 16 * KB
    R_Q = R_W + 32 * KB
    R_U = R_Q + 20 * KB
    R_A = R_U + 40 * KB
    R_G = R_A + 73 * KB
    R_C = R_G + 11 * KB
    top = [R_C]

    def at(name, shape, dt, offset):
        return nc.alloc_sbuf_tensor_at(name, shape, dt, offset=offset)

    def const(name, shape, dt=F32):
        n = int(np.prod(shape[1:])) * 4
        t = at(name, shape, dt, top[0])
        top[0] += (n + 31) // 32 * 32
        assert top[0] <= nc.sbuf_usable_end, name
        return t

    raw = at("raw", [P, 2, UNIT], F32, R_RAW)
    raw_x = [at(f"raw_x{i}", [P, UNIT], F32, R_A + (68 + 8 * i) * KB) for i in range(2)]
    w_hi = at("w_hi", [P, 2, UNIT], F32R, R_W)
    w_lo = at("w_lo", [P, 2, UNIT], F32R, R_W + 16 * KB)
    xn = at("xn", [P, NT, D], F32, R_Q)
    u_hi = at("u_hi", [P, KC, NTOK], F32R, R_U)
    u_lo = at("u_lo", [P, KC, NTOK], F32R, R_U + 20 * KB)
    u_tmp = at("u_tmp", [P, 2, NTOK], F32, R_A)
    q_tok = at("q_tok", [P, NT, QW], F32, R_Q)
    k_hi = at("k_hi", [P, NKV, 6 * P], F32R, R_A)
    k_lo = at("k_lo", [P, NKV, 6 * P], F32R, R_A + 12 * KB)
    v_hl = at("v_hl", [P, 6, NKV, 2 * DH], F32R, R_A + 24 * KB)
    q_st = at("q_st", [P, 2, NTOK], F32R, R_A + 36 * KB)
    probs = at("probs", [P, 2, LT, NTOK], F32, R_A + 41 * KB)
    pt_hi = at("pt_hi", [P, 3, NLAT], F32R, R_A + 61 * KB)
    pt_lo = at("pt_lo", [P, 3, NLAT], F32R, R_A + 67 * KB)
    kr = at("kr", [P, 6, KVW], F32, R_A + 41 * KB)
    vr = at("vr", [P, 6, KVW], F32, R_A + 47 * KB)
    sq = at("sq", [P, D], F32, R_A + 61 * KB)
    rot = at("rot", [P, D], F32, R_A + 65 * KB)
    glu = at("glu", [P, CCH, CW], F32, R_G)
    sgb = at("sgb", [P, 2, NTOK], F32, R_A + 53 * KB)
    o_hi = at("o_hi", [P, KC, NTOK], F32R, R_A)
    o_lo = at("o_lo", [P, KC, NTOK], F32R, R_A + 20 * KB)
    sgc = at("sgc", [P, KC, NTOK], F32, R_A + 40 * KB)
    cv = at("cv", [P, CCH, CO], F32, R_A + 60 * KB)
    sga = at("sga", [P, NTOK], F32, R_A + 60 * KB + 10752)
    o_t = at("o_t", [P, NT, KC, P], F32, R_Q)
    m_t = at("m_t", [P, KC, NTOK], F32, R_Q)
    cn = at("cn", [P, NT, DC], F32, R_U + 20 * KB)
    c_hi = at("c_hi", [P, CCH, NTOK], F32R, R_U)
    c_lo = at("c_lo", [P, CCH, NTOK], F32R, R_U + 10 * KB)
    c_f = at("c_f", [P, 2, NTOK], F32, R_U + 30 * KB)
    m_hi = at("m_hi", [P, KC, NTOK], F32R, R_A)
    m_lo = at("m_lo", [P, KC, NTOK], F32R, R_A + 20 * KB)
    m_tmp = at("m_tmp", [P, 2, NTOK], F32, R_U + 35 * KB)
    h_in = at("h_in", [P, NT, D], F32, R_U)
    g1_row = at("g1_row", [P, 2, D], F32, R_U + 20 * KB)
    h_a = at("h_a", [P, NT, D], F32, R_Q)
    a2_row = at("a2_row", [P, 2, D], F32, R_A + 40 * KB)
    b2_row = at("b2_row", [P, 2, D], F32, R_A + 48 * KB)
    n2_row = at("n2_row", [P, D], F32, R_A + 56 * KB)
    u2 = at("u2", [P, NT, D], F32, R_U)
    u2_t = at("u2_t", [P, 2, KC, P], F32, R_A)
    gu_hi = [at(f"gu_hi{i}", [P, KC, 2 * DE], F32R, R_U + 48 * i * KB) for i in range(2)]
    gu_lo = [at(f"gu_lo{i}", [P, KC, 2 * DE], F32R, R_U + (48 * i + 16) * KB) for i in range(2)]
    dn_hi = [at(f"dn_hi{i}", [P, 2, D], F32R, R_U + (48 * i + 32) * KB) for i in range(2)]
    dn_lo = [at(f"dn_lo{i}", [P, 2, D], F32R, R_U + (48 * i + 40) * KB) for i in range(2)]
    xe = at("xe", [P, D], F32, R_Q)
    xt_hi = at("xt_hi", [P, KC, P], F32R, R_Q + 4 * KB)
    xt_lo = at("xt_lo", [P, KC, P], F32R, R_Q + 8 * KB)
    sg = at("sg", [P, DE], F32, R_Q + 12 * KB)
    hx = at("hx", [P, DE], F32, R_Q + 13 * KB)
    ht_hi = at("ht_hi", [P, 2, P], F32R, R_Q + 14 * KB)
    ht_lo = at("ht_lo", [P, 2, P], F32R, R_Q + 15 * KB)
    ye = at("ye", [P, D], F32, R_W)
    tab = at("tab", [P, MAXT, 4], U32, R_W + 4 * KB)
    g2_row = at("g2_row", [P, 2, D], F32, R_W + 8 * KB)
    cmb = at("cmb", [P, 2, 3, D], F32, R_A)
    fin = at("fin", [P, NT, D], F32, R_Q)
    fin_row = at("fin_row", [P, D], F32, R_U)
    junk2 = at("junk2", [P, 2, D], F32, R_A + 60 * KB)

    late = [R_W + 16 * KB]

    def routed(name, shape, dt=F32):
        n = int(np.prod(shape[1:])) * 4
        t = at(name, shape, dt, late[0])
        late[0] += (n + 31) // 32 * 32
        assert late[0] <= R_Q, name
        return t

    ident = const("ident", [P, P])
    ones = const("ones", [P, P])
    tri = const("tri", [P, P])
    cs_hi = const("cs_hi", [P, 2, KC], F32R)
    cs_lo = const("cs_lo", [P, 2, KC], F32R)
    cs = const("cs", [P, 2, KC])
    craw = const("craw", [P, 2, KC])
    cosr = const("cosr", [P, LT, DH])
    sinr = const("sinr", [P, LT, DH])
    rq = at("rq", [P, 2, LT, DH], F32, R_A + 69 * KB)
    rk = at("rk", [P, 2, LT, DH], F32, R_A + 71 * KB)
    gq = const("gq", [P, 2, DH])
    gp = const("gp", [P, 2, DH])
    mcol = const("mcol", [P, 2, 2, KC])
    n1col = const("n1col", [P, KC])
    convw = const("convw", [P, CCH, TAPS])
    convb = const("convb", [P, CCH])
    lng = const("lng", [P, CCH])
    lnb = const("lnb", [P, CCH])
    ssq = const("ssq", [P, 8])
    std = const("std", [P, 8])
    rstd = const("rstd", [P, 8])
    hss = const("hss", [P, NT, NH + NKV])
    hrs = const("hrs", [P, NT, NH + NKV])
    nmax = const("nmax", [P, 2, LT])
    rsum = const("rsum", [P, 2, LT])
    cmax = const("cmax", [P, GQ])
    csum = const("csum", [P, GQ])
    bst = const("bst", [P, NT, 6])
    bag = const("bag", [P, NT, 2])
    adab = at("adab", [2, 2, 512], F32, R_A + 30 * KB)
    mrow = at("mrow", [2, 2, 512], F32, R_A + 34 * KB)
    osb = const("osb", [DH, NLAT])
    oscb = const("oscb", [DH, P])
    wr = const("wr", [P, KC, NE])
    rb = const("rb", [P, NE])
    eps = const("eps", [P, 1])
    iot = const("iot", [P, NE])
    grpof = const("grpof", [P, NE])
    tokid = const("tokid", [P, NT])
    lg = routed("lg", [P, NT, NE])
    sel = routed("sel", [P, NT, NE])
    msk = routed("msk", [P, 2, NT, NE])
    tmp16 = routed("tmp16", [P, NT, NE])
    pos = routed("pos", [P, NT, NE])
    cnt = routed("cnt", [P, NT, NE])
    pair = routed("pair", [P, NT, NG, 6])
    g8 = routed("g8", [P, NT, 8])
    top8 = routed("top8", [P, NT, 8])
    idx8 = routed("idx8", [P, NT, 8], U32)
    ef = routed("ef", [P, NT, 8])
    wsel = routed("wsel", [P, 2, NT])
    sca = routed("sca", [P, 4, NE])
    start = routed("start", [P, NE + 3])
    start_i = const("start_i", [P, NE + 3], I32)
    tbase = const("tbase", [P, 2])
    slot = routed("slot", [P, 2, NT])
    slot_u = routed("slot_u", [P, 2, NT], U32)
    rows = routed("rows", [P, 2, NT, 4], U32)
    blank = const("blank", [P, MAXT, 4], U32)
    gidx = routed("gidx", [P, 1], U32)
    sidx = routed("sidx", [P, 1], U32)
    wrow = routed("wrow", [P, 1], F32)
    ctxp = const("ctxp", [P, 2, P])
    cpt_hi = const("cpt_hi", [P, 2, P], F32R)
    cpt_lo = const("cpt_lo", [P, 2, P], F32R)
    mrt = const("mrt", [32, P])

    ps = ctx.enter_context(nc.psum_tensor("ps", [P, 8, 512], F32))

    def dram(name, shape, dt=F32):
        return nc.dram_tensor(name, shape, dt, kind="Internal").ap()

    mod_d = dram("mod_d", (2, 6 * D))
    h_d = dram("h_d", (NTOK, D))
    ha_d = dram("ha_d", (NTOK, D))
    u2_d = dram("u2_d", (NTOK, D))
    y_d = dram("y_d", (2 * NTOK, D))
    tab_d = dram("tab_d", (MAXT * P, 4), U32)

    class Banks:

        def __init__(self):
            self.at = 0
            self.of = ledger.banks

        def take(self, name, bank=None):
            b = self.at if bank is None else bank
            self.at = (b + 1) % 8
            self.of[name] = b
            return b

    fills = Banks()

    MM3 = ((0, 0), (0, 1), (1, 0))

    def ALIAS(event, of):
        ledger.alias[event] = of

    def u2t(eng, V, t):
        for i in range(2):
            eng.wait_ge(*V.at("filled", ("u2T", t, i)))
            b = V.bank(("u2T", t, i))
            if t >= 2 and i == 0:
                eng.wait_ge(*V.at("u2t_used", t - 2))
            nc.vector.tensor_copy(u2_t[:, t % 2, 4 * i:4 * i + 4, :].rearrange("p c n -> p (c n)"), ps[:, b, :]).then_inc(*V.drained(("u2T", t, i)))

    def slot_of(n):
        return n % 2 if n < U_MOE else (n - U_MOE + 2) % 4

    def raw_of(n):
        s = slot_of(n)
        return raw[:, s, :] if s < 2 else raw_x[s - 2][:, :]

    def gate_units(b):
        return U_GATE + 2 * b, U_GATE + 2 * b + 1

    block = ctx.enter_context(nc.Block())

    @block.tensor
    def _(eng):
        T = Counts(ledger, sems)
        last = {}

        def fill(name, bank=None):
            b = fills.take(name, bank)
            if b in last:
                eng.wait_ge(*T.at("drained", last[b]))
            last[b] = name
            return b

        ledger.section = "before"
        eng.wait_ge(*T.at("ident"))
        eng.wait_ge(*T.at("cs"))
        eng.wait_ge(*T.at("wr_loaded"))
        eng.sem_inc(sems("y_full"), 1)
        ledger.section = "layer"
        mm = nc.tensor.matmul
        with eng.Fori(0, DEPTH) as l:
            T.l = l

            for j in range(N_ADA // 2):
                b = fill(("ada", j))
                for kh in range(2):
                    eng.wait_ge(*T.at("w_lo", 2 * j + kh))
                    s = (2 * j + kh) % 2
                    for c in range(4):
                        for w, x in MM3:
                            k = kh * 4 + c
                            ins = mm(ps[0:2, b, :], (cs_hi, cs_lo)[x][:, :, k],
                                     (w_hi, w_lo)[w][:, s, c * 512:(c + 1) * 512],
                                     start=(k == 0 and w + x == 0), stop=(k == 7 and w == 1))
                    if kh == 0:
                        ins.then_inc(*T.up("w_used", "w_used", 2 * j))
                ins.then_inc(*T.filled(("ada", j)))

            b = fill(("mcol",))
            eng.wait_ge(*T.at("mrt"))
            eng.sem_inc(sems("passed_T"), 1)
            ins = nc.tensor.transpose(ps[:, b, 0:32], mrt[:, :], ident[0:32, 0:32])
            ins.then_inc(*T.filled(("mcol",)))

            eng.wait_ge(*T.at("xn"))
            for c in range(KC):
                for part, tiles in ((0, range(LT)), (1, (LT,))):
                    b = fill(("uT", c, part))
                    for i, t in enumerate(tiles):
                        ins = nc.tensor.transpose(ps[:, b, i * P:(i + 1) * P], xn[:, t, c * P:(c + 1) * P], ident[:, :])
                    ins.then_inc(*T.filled(("uT", c, part)))

            eng.wait_ge(*T.at("drained", ("uT", KC - 1, 1)))
            eng.wait_ge(*T.at("u_lo_all"))
            for nu in range(3):
                bs = [fill(("qkv", nu, t)) for t in range(NT)]
                for kh in range(2):
                    n = U_QKV + 2 * nu + kh
                    eng.wait_ge(*T.at("w_lo", n))
                    s = (n) % 2
                    for t in range(NT):
                        for c in range(4):
                            k = kh * 4 + c
                            for w, x in MM3:
                                ins = mm(ps[:, bs[t], :], (u_hi, u_lo)[x][:, k, t * P:(t + 1) * P],
                                         (w_hi, w_lo)[w][:, s, c * 512:(c + 1) * 512],
                                         start=(k == 0 and w + x == 0), stop=(k == 7 and w == 1))
                        if kh == 1:
                            ins.then_inc(*T.filled(("qkv", nu, t)))
                    if kh == 0:
                        ins.then_inc(*T.up("w_used", "w_used", n))

            def feature_rows(names, s, cols, nk, xs, last_used=None):
                for half in range(2):
                    b = fill(names[half])
                    for k in range(nk):
                        for w, x in MM3:
                            ins = mm(ps[:, b, 0:HALF], (w_hi, w_lo)[w][:, s, cols(k):cols(k) + P],
                                     xs[x][:, k, half * HALF:(half + 1) * HALF],
                                     start=(k == 0 and w + x == 0), stop=(k == nk - 1 and w == 1))
                    ins.then_inc(*T.filled(names[half]))

            for j in range(CCH):
                eng.wait_ge(*T.at("w_lo", U_GLU + j))
                s = (U_GLU + j) % 2
                feature_rows([("gb", j, i) for i in range(2)], s, lambda k: k * 256 + 128, KC, (u_hi, u_lo))
                feature_rows([("ga", j, i) for i in range(2)], s, lambda k: k * 256, KC, (u_hi, u_lo))

            eng.wait_ge(*T.at("k_ready"))
            for g2 in range(NKV // 2):
                for part, blocks in ((0, range(4)), (1, range(4, 6))):
                    b = fill(("kT", g2, part))
                    for i, blk in enumerate(blocks):
                        ins = nc.tensor.transpose(ps[:, b, i * P:(i + 1) * P], kr[:, blk, g2 * P:(g2 + 1) * P], ident[:, :])
                    ins.then_inc(*T.filled(("kT", g2, part)))

            eng.wait_ge(*T.at("q_ready"))

            def q_transposes(h2):
                b = fill(("qT", h2, 0), 0)
                for t in range(LT):
                    ins = nc.tensor.transpose(ps[:, b, t * P:(t + 1) * P], q_tok[:, t, h2 * P:(h2 + 1) * P], ident[:, :])
                ins.then_inc(*T.filled(("qT", h2, 0)))
                b = fill(("qT", h2, 1), 1)
                ins = nc.tensor.transpose(ps[:, b, 0:P], q_tok[:, LT, h2 * P:(h2 + 1) * P], ident[:, :])
                ins.then_inc(*T.filled(("qT", h2, 1)))

            def scores(h, t):
                if h >= NH:
                    return
                g = h // GQ
                if t == 0:
                    eng.wait_ge(*T.at("q_st", h))
                for i in range(2):
                    b = fill(("S", h, t, i), 2 * (t % 2) + i)
                    mm(ps[:, b, 0:HALF], q_st[:, h % 2, t * P:(t + 1) * P], k_hi[:, g, i * HALF:(i + 1) * HALF],
                       start=True, stop=False)
                    ins = mm(ps[:, b, 0:HALF], q_st[:, h % 2, t * P:(t + 1) * P], k_lo[:, g, i * HALF:(i + 1) * HALF],
                             start=False, stop=True)
                    ins.then_inc(*T.filled(("S", h, t, i)))

            def ctx_scores(h):
                if h >= NH:
                    return
                g = h // GQ
                b = fill(("Sc", h), 7)
                mm(ps[:, b, 0:P], q_st[:, h % 2, NLAT:NTOK], k_hi[:, g, NTOK:NTOK + P], start=True, stop=False)
                ins = mm(ps[:, b, 0:P], q_st[:, h % 2, NLAT:NTOK], k_lo[:, g, NTOK:NTOK + P], start=False, stop=True)
                ins.then_inc(*T.filled(("Sc", h)))

            def p_transposes(h, kc):
                b = fill(("PT", h, kc), 4 + (h * NT + kc) % 2)
                for t in range(LT):
                    ins = nc.tensor.transpose(ps[:, b, t * P:(t + 1) * P], probs[:, h % 2, t, kc * P:(kc + 1) * P], ident[:, :])
                ins.then_inc(*T.filled(("PT", h, kc)))

            def values(h, k):
                g = h // GQ
                ob = fill(("O", h), 6) if k == 0 else fills.of["O", h]
                eng.wait_ge(*T.at("drained", ("PT", h, k)))
                for x in range(2):
                    ins = mm(ps[:, ob, :], v_hl[:, k, g, :], (pt_hi, pt_lo)[x][:, (h * NT + k) % 3, :],
                             start=(k == 0 and x == 0), stop=(k == NT - 1 and x == 1))
                if k == NT - 1:
                    ins.then_inc(*T.filled(("O", h)))
                else:
                    ins.then_inc(*T.up("pt_used", "pt_used", h, k))

            def ctx_transpose(h):
                eng.wait_ge(*T.at("ctx_probs", h))
                b = fill(("PTc", h), 7)
                ins = nc.tensor.transpose(ps[:, b, 0:P], ctxp[:, h % 2, :], ident[:, :])
                ins.then_inc(*T.filled(("PTc", h)))

            def ctx_values(h):
                b = fill(("Oc", h), 7)
                eng.wait_ge(*T.at("drained", ("PTc", h)))
                for x in range(2):
                    ins = mm(ps[:, b, 0:P], v_hl[:, 5, h // GQ, :], (cpt_hi, cpt_lo)[x][:, h % 2, :], start=(x == 0), stop=(x == 1))
                ins.then_inc(*T.filled(("Oc", h)))

            q_transposes(0)
            for t in range(LT):
                scores(0, t)
            ctx_scores(0)
            for h in range(NH):
                if h + 1 < NH and (h + 1) % 2 == 0:
                    q_transposes((h + 1) // 2)
                eng.wait_ge(*T.at("probs", h))
                p_transposes(h, 0)
                p_transposes(h, 1)
                ctx_transpose(h)
                scores(h + 1, 0)
                p_transposes(h, 2)
                values(h, 0)
                scores(h + 1, 1)
                p_transposes(h, 3)
                values(h, 1)
                ctx_values(h)
                scores(h + 1, 2)
                p_transposes(h, 4)
                values(h, 2)
                scores(h + 1, 3)
                ctx_scores(h + 1)
                values(h, 3)
                values(h, 4)

            eng.wait_ge(*T.at("o_split"))
            for b8 in range(KC):
                eng.wait_ge(*T.at("w_lo", gate_units(b8)[0]))
                s = (gate_units(b8)[0]) % 2
                feature_rows([("gta", b8, i) for i in range(2)], s, lambda k: k * 256, KC, (u_hi, u_lo))
                feature_rows([("gtc", b8, i) for i in range(2)], s, lambda k: k * 256 + 128, KC, (u_hi, u_lo))
                eng.wait_ge(*T.at("w_lo", gate_units(b8)[1]))
                s = (gate_units(b8)[1]) % 2
                feature_rows([("ao", b8, i) for i in range(2)], s, lambda k: k * P, KC, (o_hi, o_lo))

            eng.wait_ge(*T.at("cv"))
            for t in range(NT):
                b = fill(("cvT", t))
                c0 = t * P if t < LT else CTX0
                for c in range(CCH):
                    ins = nc.tensor.transpose(ps[:, b, c * P:(c + 1) * P], cv[:, c, c0:c0 + P], ident[:, :])
                ins.then_inc(*T.filled(("cvT", t)))
            eng.wait_ge(*T.at("cn"))
            for c in range(CCH):
                for part, tiles in ((0, range(LT)), (1, (LT,))):
                    b = fill(("cT", c, part))
                    for i, t in enumerate(tiles):
                        ins = nc.tensor.transpose(ps[:, b, i * P:(i + 1) * P], cn[:, t, c * P:(c + 1) * P], ident[:, :])
                    ins.then_inc(*T.filled(("cT", c, part)))
            eng.wait_ge(*T.at("c_lo", CCH - 1))
            for b8 in range(KC):
                if b8 % 2 == 0:
                    eng.wait_ge(*T.at("w_lo", U_CO + b8 // 2))
                    s = (U_CO + b8 // 2) % 2
                feature_rows([("co", b8, i) for i in range(2)], s, lambda k, b8=b8: k * 256 + b8 % 2 * P, CCH, (c_hi, c_lo))

            eng.wait_ge(*T.at("m_lo", KC - 1))
            for nh in range(2):
                bs = [fill(("wo", nh, t)) for t in range(NT)]
                for kh in range(2):
                    n = U_OUT + 2 * nh + kh
                    eng.wait_ge(*T.at("w_lo", n))
                    s = (n) % 2
                    for t in range(NT):
                        for c in range(4):
                            k = kh * 4 + c
                            for w, x in MM3:
                                ins = mm(ps[:, bs[t], :], (m_hi, m_lo)[x][:, k, t * P:(t + 1) * P],
                                         (w_hi, w_lo)[w][:, s, c * 512:(c + 1) * 512],
                                         start=(k == 0 and w + x == 0), stop=(k == 7 and w == 1))
                        if kh == 1:
                            ins.then_inc(*T.filled(("wo", nh, t)))
                    if kh == 0:
                        ins.then_inc(*T.up("w_used", "w_used", n))

            def u2_transposes(t):
                eng.wait_ge(*T.at("u2", t))
                for i in range(2):
                    b = fill(("u2T", t, i))
                    for c in range(4):
                        k = i * 4 + c
                        ins = nc.tensor.transpose(ps[:, b, c * P:(c + 1) * P], u2[:, t, k * P:(k + 1) * P], ident[:, :])
                    ins.then_inc(*T.filled(("u2T", t, i)))

            rbank = None
            for t in range(NT + 1):
                if t < NT:
                    u2_transposes(t)
                if t >= 1:
                    if rbank is None:
                        rbank = fill(("router",))
                    eng.wait_ge(*T.at("drained", ("u2T", t - 1, 1)))
                    eng.wait_ge(*T.at("drained", ("u2T", t - 1, 0)))
                    for k in range(KC):
                        ins = mm(ps[:, rbank, (t - 1) * NE:t * NE], u2_t[:, (t - 1) % 2, k, :], wr[:, k, :],
                                 start=(k == 0), stop=(k == KC - 1))
                    if t == NT:
                        ins.then_inc(*T.filled(("router",)))
                    else:
                        ins.then_inc(*T.up("u2t_used", "u2t_used", t - 1))
            eng.wait_ge(*T.at("mask"))
            b = fill(("place",))
            mm(ps[:, b, 0:NT * NE], tri[:, :], cnt[:, :, :].rearrange("p t e -> p (t e)"), start=True, stop=True)
            ins = mm(ps[:, b, 256:256 + NT * NE], ones[:, :], cnt[:, :, :].rearrange("p t e -> p (t e)"), start=True, stop=True)
            ins.then_inc(*T.filled(("place",)))

            for b in range(8):
                eng.wait_ge(*T.at("drained", last[b]))
            eng.wait_ge(*T.at("starts"))
            eng.sem_inc(sems("passed_T"), 1)
            g0 = eng.value_load(start_i[0:1, NE + 1:NE + 2], min_val=1, max_val=DEPTH * MAXT)
            n0 = eng.value_load(start_i[0:1, NE + 2:NE + 3], min_val=0, max_val=DEPTH * MAXT)

            def xe_transposes(g):
                eng.wait_ge(sems("xe_landed"), 16 * g)
                for k in range(KC):
                    ins = nc.tensor.transpose(ps[:, k // 4, (k % 4) * P:(k % 4 + 1) * P], xe[:, k * P:(k + 1) * P], ident[:, :])
                ins.then_inc(sems("xt_full"), 1)

            xe_transposes(g0)
            for e in range(NE):
                eng.wait_ge(*T.at("w_lo", U_MOE + 3 * e + 1))
                eng.sem_inc(sems("passed_T"), 1)
                i = (e + 1) % 2
                lo = eng.value_load(start_i[0:1, e:e + 1], min_val=0, max_val=MAXT - 1)
                hi = eng.value_load(start_i[0:1, e + 1:e + 2], min_val=0, max_val=MAXT - 1)
                with eng.Fori(lo, hi) as j:
                    g, n = g0 + j, n0 + j + 1
                    eng.wait_ge(sems("xt_split"), g)
                    for k in range(KC):
                        for w, x in MM3:
                            ins = mm(ps[:, 2, :], (xt_hi, xt_lo)[x][:, k, :], (gu_hi, gu_lo)[w][i][:, k, :],
                                     start=(k == 0 and w + x == 0), stop=(k == 7 and w == 1))
                    ins.then_inc(sems("gu_full"), 1)
                    xe_transposes(g + 1)
                    eng.wait_ge(sems("h_ready"), n)
                    for c in range(2):
                        ins = nc.tensor.transpose(ps[:, 3, c * P:(c + 1) * P], hx[:, c * P:(c + 1) * P], ident[:, :])
                    ins.then_inc(sems("ht_full"), 1)
                    eng.wait_ge(sems("ht_split"), n)
                    eng.wait_ge(*T.at("w_lo", U_MOE + 3 * e + 2))
                    for half in range(2):
                        for c in range(2):
                            for w, x in MM3:
                                ins = mm(ps[:, 4 + half, :], (ht_hi, ht_lo)[x][:, c, :], (dn_hi, dn_lo)[w][i][:, c, half * 512:(half + 1) * 512],
                                         start=(c == 0 and w + x == 0), stop=(c == 1 and w == 1))
                    ins.then_inc(sems("y_full"), 1)
            eng.wait_ge(sems("y_drained"), n0 + hi)
            eng.wait_ge(sems("xt_split"), g0 + hi)

    def used(n):
        if n < U_QKV:
            return ("w_used", n) if n % 2 == 0 else ("filled", ("ada", n // 2))
        if n < U_GLU:
            i = n - U_QKV
            return ("w_used", n) if i % 2 == 0 else ("filled", ("qkv", i // 2, NT - 1))
        if n < U_GATE:
            return ("filled", ("ga", n - U_GLU, 1))
        if n < U_CO:
            i = n - U_GATE
            return ("filled", (("gtc", "ao")[i % 2], i // 2, 1))
        if n < U_OUT:
            return ("filled", ("co", 2 * (n - U_CO) + 1, 1))
        i = n - U_OUT
        return ("w_used", n) if i % 2 == 0 else ("filled", ("wo", i // 2, NT - 1))

    def size(n):
        if U_GATE <= n < U_CO and (n - U_GATE) % 2 == 1:
            return KC * P
        if U_CO <= n < U_OUT:
            return CCH * 256
        return UNIT

    A_hs = h_d.rearrange("(t p) d -> p t d", p=P)

    @block.sync
    def _(eng):
        S = Counts(ledger, sems)
        ledger.section = "layer"
        with eng.Fori(0, DEPTH) as l:
            S.l = l

            def load(n, *pieces):
                if n < 2:
                    eng.wait_ge(*S.at("w_lo", N_UNITS - 2 + n, previous=True))
                elif n < U_MOE:
                    eng.wait_ge(*S.at("w_lo", n - 2))
                elif n < U_MOE + 2:
                    eng.wait_ge(*S.at("filled", ("cvT", NT - 1)))
                    eng.wait_ge(*S.at("drained", ("ao", KC - 1, 1)))
                elif n < U_MOE + 4:
                    eng.wait_ge(*S.at("w_lo", n - 4))
                else:
                    eng.wait_ge(*S.at("w_lo", n - 4))
                for i, (dst, src) in enumerate(pieces):
                    eng.dma_start(dst, src).then_inc(*S.up(f"w_raw{slot_of(n)}", *(("w_raw", n) if i == len(pieces) - 1 else ()), by=16))

            def r(n, c):
                return raw_of(n)[:, 0:size(n) if n < U_MOE else UNIT].rearrange("p (c n) -> p c n", c=c)

            for j in range(N_ADA // 2):
                for kh in range(2):
                    n = 2 * j + kh
                    load(n, (r(n, 4), io["w_ada"][l, kh * 512:(kh + 1) * 512, j * 512:(j + 1) * 512].rearrange("(c p) n -> p c n", p=P)))
            for nu in range(3):
                for kh in range(2):
                    n = U_QKV + 2 * nu + kh
                    load(n, (r(n, 4), io["w_in"][l, kh * 512:(kh + 1) * 512, nu * 512:(nu + 1) * 512].rearrange("(c p) n -> p c n", p=P)))
            for j in range(CCH):
                n = U_GLU + j
                load(n, *((r(n, KC)[:, :, i * P:(i + 1) * P],
                           io["w_in"][l, :, c0 + j * P:c0 + (j + 1) * P].rearrange("(c p) n -> p c n", p=P))
                          for i, c0 in enumerate((GA0, GB0))))
            for b8 in range(KC):
                n = gate_units(b8)[0]
                load(n, *((r(n, KC)[:, :, i * P:(i + 1) * P],
                           io["w_in"][l, :, c0 + b8 * P:c0 + (b8 + 1) * P].rearrange("(c p) n -> p c n", p=P))
                          for i, c0 in enumerate((GATE0, GATE0 + D))))
                n = gate_units(b8)[1]
                load(n, (r(n, KC), io["w_attn_o"][l, :, b8 * P:(b8 + 1) * P].rearrange("(c p) n -> p c n", p=P)))
            for j in range(N_CO):
                n = U_CO + j
                load(n, (r(n, CCH), io["w_conv_o"][l, :, j * 256:(j + 1) * 256].rearrange("(c p) n -> p c n", p=P)))
            for nh in range(2):
                for kh in range(2):
                    n = U_OUT + 2 * nh + kh
                    load(n, (r(n, 4), io["w_out"][l, kh * 512:(kh + 1) * 512, nh * 512:(nh + 1) * 512].rearrange("(c p) n -> p c n", p=P)))
            for e in range(NE):
                for kh in range(2):
                    n = U_MOE + 3 * e + kh
                    load(n, *((r(n, 4)[:, :, i * DE:(i + 1) * DE],
                               io[w][l, e, kh * 512:(kh + 1) * 512, :].rearrange("(c p) n -> p c n", p=P))
                              for i, w in enumerate(("w_gate", "w_up"))))
                n = U_MOE + 3 * e + 2
                load(n, (r(n, 2), io["w_down"][l, e, :, :].rearrange("(c p) n -> p c n", p=P)))

    def expert_half(n, hi):
        e, k = (n - U_MOE) // 3, (n - U_MOE) % 3
        i = (e + 1) % 2
        if k == 2:
            return (dn_lo, dn_hi)[hi][i][:, :, :].rearrange("p c n -> p (c n)")
        return (gu_lo, gu_hi)[hi][i][:, 4 * k:4 * k + 4, :].rearrange("p c n -> p (c n)")

    @block.scalar
    def _(eng):
        A = Counts(ledger, sems)
        act = nc.scalar.activation
        ledger.section = "before"
        eng.wait_ge(*A.at("eps"))
        eng.wait_ge(*A.at("c_loaded"))
        act(cs[:, :, :], craw[:, :, :], ACT.Silu).then_inc(*A.up("a_pre", "cs_f"))
        eng.wait_ge(*A.at("cs_f"))
        act(cs_hi[:, :, :], cs[:, :, :], ACT.Copy).then_inc(*A.up("a_pre", "cs_hi"))
        ledger.section = "layer"
        with eng.Fori(0, DEPTH) as l:
            A.l = l

            def hi(n):
                if n >= U_MOE:
                    return
                eng.wait_ge(*A.at("w_raw", n))
                if n >= 2:
                    eng.wait_ge(*A.at(*used(n - 2)))
                k = size(n)
                act(w_hi[:, n % 2, 0:k], raw[:, n % 2, 0:k], ACT.Copy).then_inc(*A.up("a_hi", "w_hi", n))

            def hi_expert(n):
                eng.wait_ge(*A.at("w_raw", n))
                act(expert_half(n, 1), raw_of(n), ACT.Copy).then_inc(*A.up("a_hi", "w_hi", n))

            eng.wait_ge(*A.at("h_loaded"))
            for t in range(NT):
                if t >= 2:
                    eng.wait_ge(*A.at("ss1", t - 2))
                act(junk2[:, t % 2, :], xn[:, t, :], ACT.Square, accum_out=ssq[:, t:t + 1]).then_inc(*A.up("a_ss", "ss1", t))
            eng.wait_ge(*A.at("ss1", NT - 1))
            act(std[:, 0:NT], ssq[:, 0:NT], ACT.Sqrt, bias=eps[:, :], scale=1.0 / D).then_inc(*A.up("a_ss", "std1"))
            for n in range(U_QKV + 2):
                hi(n)
            eng.wait_ge(*A.at("acol"))
            for c in range(KC):
                for part, (c0, n) in enumerate(((0, NLAT), (NLAT, P))):
                    eng.wait_ge(*A.at("filled", ("uT", c, part)))
                    b = A.bank(("uT", c, part))
                    act(u_hi[:, c, c0:c0 + n], ps[:, b, 0:n], ACT.Identity,
                              bias=mcol[:, part, 0, c:c + 1], scale=mcol[:, part, 1, c:c + 1]).then_inc(*A.up("a_u", "u_hi", c, part))
            for nu in range(3):
                hi(U_QKV + 2 * nu + 2)
                hi(U_QKV + 2 * nu + 3)
                for t in range(NT):
                    eng.wait_ge(*A.at("filled", ("qkv", nu, t)))
                    b = A.bank(("qkv", nu, t))
                    if nu < 2:
                        act(q_tok[:, t, nu * 512:(nu + 1) * 512], ps[:, b, :], ACT.Copy).then_inc(*A.drained(("qkv", nu, t)))
                    else:
                        act(kr[:, t + 1, :], ps[:, b, 0:KVW], ACT.Copy).then_inc(*A.up("a_kv", "k_raw", t))
                        act(vr[:, t + 1, :], ps[:, b, KVW:2 * KVW], ACT.Copy).then_inc(*A.drained(("qkv", nu, t)))
            eng.wait_ge(*A.at("hss"))
            act(hrs[:, :, :], hss[:, :, :], ACT.Sqrt, bias=eps[:, :], scale=1.0 / DH).then_inc(*A.up("a_ss", "hstd"))
            eng.wait_ge(*A.at("cache_loaded"))
            eng.wait_ge(*A.at("drained", ("qkv", 2, NT - 1)))
            act(v_hl[:, :, :, 0:DH], vr[:, :, :].rearrange("p b (g d) -> p b g d", g=NKV), ACT.Copy).then_inc(*A.up("a_v", "v_hi"))
            for j in range(CCH):
                hi(U_GLU + j + 2)
                if j >= 2:
                    eng.wait_ge(*A.at("glu", j - 2))
                for i in range(2):
                    eng.wait_ge(*A.at("filled", ("gb", j, i)))
                    b = A.bank(("gb", j, i))
                    act(sgb[:, j % 2, i * HALF:(i + 1) * HALF], ps[:, b, 0:HALF], ACT.Sigmoid).then_inc(*A.drained(("gb", j, i)))
            for g2 in range(NKV // 2):
                for part, (c0, n) in enumerate(((0, 512), (512, 256))):
                    eng.wait_ge(*A.at("filled", ("kT", g2, part)))
                    b = A.bank(("kT", g2, part))
                    for x in range(2):
                        for y in range(2):
                            act(k_hi[y * DH:(y + 1) * DH, 2 * g2 + x, c0:c0 + n], ps[x * DH:(x + 1) * DH, b, 0:n], ACT.Copy).then_inc(*A.up("a_k", "k_hi", g2, part, x, y))

            def q_hi(h2):
                for part, (c0, n) in enumerate(((0, NLAT), (NLAT, P))):
                    eng.wait_ge(*A.at("filled", ("qT", h2, part)))
                    b = A.bank(("qT", h2, part))
                    for x in range(2):
                        if h2 >= 1 and part == 0:
                            eng.wait_ge(*A.at("filled", ("Sc", 2 * h2 - 2 + x)))
                        act(q_st[0:DH, x, c0:c0 + n], ps[x * DH:(x + 1) * DH, b, 0:n], ACT.Copy, scale=DH ** -0.5).then_inc(*A.up("a_q", "q_hi", h2, part, x))

            def exps(h, t):
                if h >= NH:
                    return
                eng.wait_ge(*A.at("nmax", h, t))
                eng.wait_ge(*A.at("filled", ("S", h, t, 0)))
                b0 = A.bank(("S", h, t, 0))
                eng.wait_ge(*A.at("filled", ("S", h, t, 1)))
                if h >= 2 and t == 0:
                    eng.wait_ge(*A.at("filled", ("PT", h - 2, NT - 1)))
                ins = act(probs[:, h % 2, t, :].rearrange("p (a b) -> p a b", a=2), ps[:, b0:b0 + 2, 0:HALF], ACT.Exp,
                          bias=nmax[:, h % 2, t:t + 1], accum_out=rsum[:, h % 2, t:t + 1])
                ins.then_inc(*A.drained(("S", h, t, 0)))
                ALIAS(("drained", ("S", h, t, 1)), ("drained", ("S", h, t, 0)))

            def ctx_exp(h):
                if h >= NH:
                    return
                eng.wait_ge(*A.at("cmax", h))
                eng.wait_ge(*A.at("filled", ("Sc", h)))
                b = A.bank(("Sc", h))
                if h >= 2:
                    eng.wait_ge(*A.at("filled", ("PTc", h - 2)))
                act(ctxp[:, h % 2, :], ps[:, b, 0:P], ACT.Exp, bias=cmax[:, h % 2:h % 2 + 1],
                    accum_out=csum[:, h % 2:h % 2 + 1]).then_inc(*A.drained(("Sc", h)))

            def probs_hi(h, kc):
                k = h * NT + kc
                eng.wait_ge(*A.at("filled", ("PT", h, kc)))
                b = A.bank(("PT", h, kc))
                if k >= 3:
                    hh, kk = divmod(k - 3, NT)
                    eng.wait_ge(*A.at(*(("pt_used", hh, kk) if kk < NT - 1 else ("filled", ("O", hh)))))
                act(pt_hi[:, k % 3, :], ps[:, b, :], ACT.Copy).then_inc(*A.up("a_pt", "pt_hi", h, kc))

            def ctx_hi(h):
                eng.wait_ge(*A.at("filled", ("PTc", h)))
                b = A.bank(("PTc", h))
                if h >= 2:
                    eng.wait_ge(*A.at("filled", ("Oc", h - 2)))
                act(cpt_hi[:, h % 2, :], ps[:, b, 0:P], ACT.Copy).then_inc(*A.up("a_pt", "cpt_hi", h))

            def out_half(h):
                eng.wait_ge(*A.at("filled", ("O", h)))
                b = A.bank(("O", h))
                if h >= 1:
                    eng.wait_ge(*A.at("drained", ("O", h - 1)))
                act(osb[:, :], ps[DH:P, b, :], ACT.Copy).then_inc(*A.up("a_o", "o_half", h))

            def ctx_out_half(h):
                eng.wait_ge(*A.at("filled", ("Oc", h)))
                b = A.bank(("Oc", h))
                if h >= 1:
                    eng.wait_ge(*A.at("drained", ("Oc", h - 1)))
                act(oscb[:, :], ps[DH:P, b, 0:P], ACT.Copy).then_inc(*A.up("a_o", "oc_half", h))

            q_hi(0)
            for t in range(LT):
                exps(0, t)
            ctx_exp(0)
            for h in range(NH):
                if h + 1 < NH and (h + 1) % 2 == 0:
                    q_hi((h + 1) // 2)
                probs_hi(h, 0)
                probs_hi(h, 1)
                ctx_hi(h)
                probs_hi(h, 2)
                exps(h + 1, 0)
                probs_hi(h, 3)
                exps(h + 1, 1)
                ctx_out_half(h)
                probs_hi(h, 4)
                exps(h + 1, 2)
                exps(h + 1, 3)
                ctx_exp(h + 1)
                out_half(h)
            eng.wait_ge(*A.at("drained", ("O", NH - 1)))
            for k in range(KC):
                act(o_hi[:, k, :].rearrange("p (t n) -> p t n", t=NT), o_t[:, :, k, :], ACT.Copy).then_inc(*A.up("a_oh", "o_hi", k))
            for b8 in range(KC):
                if b8 >= 1:
                    eng.wait_ge(*A.at("drained", ("ao", b8 - 1, 1)))
                for i in range(2):
                    eng.wait_ge(*A.at("filled", ("gta", b8, i)))
                    b = A.bank(("gta", b8, i))
                    act(sga[:, i * HALF:(i + 1) * HALF], ps[:, b, 0:HALF], ACT.Sigmoid).then_inc(*A.drained(("gta", b8, i)))
                if b8 == 0:
                    eng.wait_ge(*A.at("o_split"))
                for i in range(2):
                    eng.wait_ge(*A.at("filled", ("gtc", b8, i)))
                    b = A.bank(("gtc", b8, i))
                    act(sgc[:, b8, i * HALF:(i + 1) * HALF], ps[:, b, 0:HALF], ACT.Sigmoid).then_inc(*A.drained(("gtc", b8, i)))
                hi(gate_units(b8)[0] + 2)
                hi(gate_units(b8)[1] + 2)
            eng.wait_ge(*A.at("cv_var"))
            act(std[:, 0:NT], bag[:, :, 1], ACT.Sqrt, bias=eps[:, :]).then_inc(*A.up("a_ss", "cstd"))
            for c in range(CCH):
                if c >= 2:
                    eng.wait_ge(*A.at("c_lo", c - 2))
                for part, (c0, n) in enumerate(((0, NLAT), (NLAT, P))):
                    eng.wait_ge(*A.at("filled", ("cT", c, part)))
                    b = A.bank(("cT", c, part))
                    act(c_f[:, c % 2, c0:c0 + n], ps[:, b, 0:n], ACT.Silu, bias=lnb[:, c:c + 1], scale=lng[:, c:c + 1]).then_inc(*A.drained(("cT", c, part)))
                eng.wait_ge(*A.at("drained", ("cT", c, 1)))
                act(c_hi[:, c, :], c_f[:, c % 2, :], ACT.Copy).then_inc(*A.up("a_c", "c_hi", c))
            for j in range(N_CO):
                hi(U_CO + j + 2)
                for b8 in (2 * j, 2 * j + 1):
                    eng.wait_ge(*A.at("merged", b8))
                    act(m_hi[:, b8, :], m_t[:, b8, :], ACT.Copy).then_inc(*A.up("a_m", "m_hi", b8))
            eng.wait_ge(*A.at("filled", ("co", KC - 1, 1)))
            eng.wait_ge(*A.at("m_lo", KC - 1))
            for i in range(2):
                eng.dma_start(g1_row[:, i, :], mod_d[i:i + 1, G1:G1 + D].broadcast_to([P, D])).then_inc(*A.up("rows_in", by=16))
            eng.dma_start(h_in[:, :, :], A_hs).then_inc(*A.up("rows_in", "h_in", by=16))
            for i in range(2):
                eng.dma_start(a2_row[:, i, :], mod_d[i:i + 1, SC2:SC2 + D].broadcast_to([P, D])).then_inc(*A.up("rows_in", by=16))
                eng.dma_start(b2_row[:, i, :], mod_d[i:i + 1, SH2:SH2 + D].broadcast_to([P, D])).then_inc(*A.up("rows_in", by=16))
            eng.dma_start(n2_row[:, :], io["norm2_g"][bass.ds(l, 1), :].broadcast_to([P, D])).then_inc(*A.up("rows_in", "n2_in", by=16))
            for nh in range(2):
                hi(U_OUT + 2 * nh + 2)
                hi(U_OUT + 2 * nh + 3)
            for t in range(NT):
                eng.wait_ge(*A.at("h_a", t))
                if t >= 2:
                    eng.wait_ge(*A.at("ss2", t - 2))
                act(junk2[:, t % 2, :], h_a[:, t, :], ACT.Square, accum_out=ssq[:, t:t + 1]).then_inc(*A.up("a_ss", "ss2", t))
            eng.wait_ge(*A.at("ss2", NT - 1))
            act(std[:, 0:NT], ssq[:, 0:NT], ACT.Sqrt, bias=eps[:, :], scale=1.0 / D).then_inc(*A.up("a_ss", "std2"))
            eng.dma_start(ha_d.rearrange("(t p) d -> p t d", p=P), h_a[:, :, :]).then_inc(*A.up("ha_out", "ha_out", by=16))
            for k in range(2):
                hi_expert(U_MOE + k)
            eng.wait_ge(*A.at("u2", NT - 1))
            hi_expert(U_MOE + 2)
            eng.dma_start(u2_d.rearrange("(t p) d -> p t d", p=P), u2[:, :, :]).then_inc(*A.up("u2_st", "u2_out", by=16))
            for i in range(2):
                eng.dma_start(g2_row[:, i, :], mod_d[i:i + 1, G2:G2 + D].broadcast_to([P, D])).then_inc(*A.up("g2_in", "g2_in", i, by=16))
            eng.wait_ge(*A.at("lg_shift"))
            act(lg[:, :, :], lg[:, :, :], ACT.Exp).then_inc(*A.up("a_rt", "lg_exp"))
            eng.wait_ge(*A.at("starts"))
            eng.wait_ge(*A.at("u2_out"))
            eng.wait_ge(*A.at("filled", ("router",)))
            eng.wait_ge(*A.at("rank"))
            eng.sem_inc(sems("passed_A"), 1)
            g0 = eng.value_load(start_i[0:1, NE + 1:NE + 2], min_val=1, max_val=DEPTH * MAXT)
            n0 = eng.value_load(start_i[0:1, NE + 2:NE + 3], min_val=0, max_val=DEPTH * MAXT)

            def xt_hi_of(g):
                eng.wait_ge(sems("xt_full"), g)
                act(xt_hi[:, :, :].rearrange("p (a c) n -> p a (c n)", a=2), ps[:, 0:2, :], ACT.Copy).then_inc(sems("xt_hi"), 1)

            eng.wait_ge(*A.at("ha_out"))
            xt_hi_of(g0)
            for e in range(NE):
                lo = eng.value_load(start_i[0:1, e:e + 1], min_val=0, max_val=MAXT - 1)
                hi_g = eng.value_load(start_i[0:1, e + 1:e + 2], min_val=0, max_val=MAXT - 1)
                if e + 1 < NE:
                    if e >= 1:
                        eng.wait_ge(sems("y_full"), n0 + lo + 1)
                    for k in range(3):
                        hi_expert(U_MOE + 3 * (e + 1) + k)
                with eng.Fori(lo, hi_g) as j:
                    g, n = g0 + j, n0 + j + 1
                    eng.wait_ge(sems("gu_full"), n)
                    act(sg[:, :], ps[:, 2, 0:DE], ACT.Silu).then_inc(sems("sg_ready"), 1)
                    xt_hi_of(g + 1)
                    eng.wait_ge(sems("ht_full"), n)
                    act(ht_hi[:, :, :].rearrange("p c n -> p (c n)"), ps[:, 3, 0:2 * P], ACT.Copy).then_inc(sems("ht_hi"), 1)
                    eng.wait_ge(sems("y_full"), n + 1)
                    eng.wait_ge(sems("y_sent"), 16 * n)
                    act(ye[:, :].rearrange("p (a n) -> p a n", a=2), ps[:, 4:6, :], ACT.Copy).then_inc(sems("y_drained"), 1)

    @block.vector
    def _(eng):
        V = Counts(ledger, sems)
        v = nc.vector
        ledger.section = "before"
        eng.wait_ge(*V.at("cs_hi"))
        v.tensor_tensor(cs_lo[:, :, :], cs[:, :, :], cs_hi[:, :, :].bitcast(F32), ALU.subtract).then_inc(*V.up("v_pre", "cs"))
        v.memset(tbase[:, 0:1], 1.0).then_inc(*V.up("v_pre"))
        v.memset(tbase[:, 1:2], 0.0).then_inc(*V.up("v_pre", "tbase"))
        eng.sem_inc(*V.up("v_lo", by=2))
        ledger.section = "layer"
        with eng.Fori(0, DEPTH) as l:
            V.l = l

            def lo(n):
                eng.wait_ge(*V.at("w_hi", n))
                if n < U_MOE:
                    k = size(n)
                    ins = v.tensor_tensor(w_lo[:, n % 2, 0:k], raw[:, n % 2, 0:k], w_hi[:, n % 2, 0:k].bitcast(F32), ALU.subtract)
                else:
                    ins = v.tensor_tensor(expert_half(n, 0), raw_of(n), expert_half(n, 1).bitcast(F32), ALU.subtract)
                ins.then_inc(*V.up("v_lo", "w_lo", n))

            eng.wait_ge(*V.at("std1"))
            v.reciprocal(rstd[:, 0:NT], std[:, 0:NT]).then_inc(*V.step())
            eng.wait_ge(*V.at("v", V.steps))
            for t in range(NT):
                ins = v.tensor_scalar(xn[:, t, :], xn[:, t, :], rstd[:, t:t + 1], None, ALU.mult)
                ins.then_inc(*V.up("v_xn", *(("xn",) if t == NT - 1 else ())))
            for j in range(N_ADA // 2):
                lo(2 * j)
                lo(2 * j + 1)
                eng.wait_ge(*V.at("filled", ("ada", j)))
                b = V.bank(("ada", j))
                eng.wait_ge(*V.at("ada_bias", j))
                if j >= 2:
                    eng.wait_ge(*V.at("mod_out", j - 2))
                v.tensor_tensor(mrow[:, j % 2, :], ps[0:2, b, :], adab[:, j % 2, :], ALU.add).then_inc(*V.drained(("ada", j)))
            eng.wait_ge(*V.at("filled", ("mcol",)))
            b = V.bank(("mcol",))
            eng.wait_ge(*V.at("small_loaded"))
            v.tensor_copy(mcol[:, :, :, :].rearrange("p a b c -> p (a b c)"), ps[:, b, 0:32]).then_inc(*V.drained(("mcol",)))
            eng.wait_ge(*V.at("drained", ("mcol",)))
            v.tensor_scalar(mcol[:, :, 1, :], mcol[:, :, 1, :], 1.0, None, ALU.add).then_inc(*V.step())
            eng.wait_ge(*V.at("v", V.steps))
            for i in range(2):
                ins = v.tensor_tensor(mcol[:, i, 1, :], mcol[:, i, 1, :], n1col[:, :], ALU.mult)
                ins.then_inc(*V.up("v_acol", *(("acol",) if i == 1 else ())))
            eng.wait_ge(*V.at("acol"))
            for x in range(2):
                for a in range(2):
                    for y in range(2):
                        v.tensor_copy(gp[:, x, a * 32 + y * 16:a * 32 + y * 16 + 16],
                                             gq[:, x, a * 32 + (1 - y) * 16:a * 32 + (1 - y) * 16 + 16]).then_inc(*V.step())
                        k = V.steps
            eng.wait_ge(*V.at("v", k))
            for x, rr in ((0, rq), (1, rk)):
                v.tensor_tensor(rr[:, 0, :, :], cosr[:, :, :], gq[:, x:x + 1, :].broadcast_to([P, LT, DH]), ALU.mult).then_inc(*V.step())
                v.tensor_tensor(rr[:, 1, :, :], sinr[:, :, :], gp[:, x:x + 1, :].broadcast_to([P, LT, DH]), ALU.mult).then_inc(*V.step())
                k_rope = V.steps
            for c in range(KC):
                for part, (c0, n) in enumerate(((0, NLAT), (NLAT, P))):
                    eng.wait_ge(*V.at("u_hi", c, part))
                    eng.wait_ge(*V.at("filled", ("uT", c, part)))
                    b = V.bank(("uT", c, part))
                    if c >= 2:
                        eng.wait_ge(*V.at("u_lo", c - 2, part))
                    v.tensor_scalar(u_tmp[:, c % 2, c0:c0 + n], ps[:, b, 0:n], mcol[:, part, 1, c:c + 1],
                                               mcol[:, part, 0, c:c + 1], ALU.mult, ALU.add).then_inc(*V.drained(("uT", c, part)))
                    eng.wait_ge(*V.at("drained", ("uT", c, part)))
                    ins = v.tensor_tensor(u_lo[:, c, c0:c0 + n], u_tmp[:, c % 2, c0:c0 + n],
                                          u_hi[:, c, c0:c0 + n].bitcast(F32), ALU.subtract)
                    ins.then_inc(*V.up("v_u", "u_lo", c, part))
            ALIAS(("u_lo_all",), ("u_lo", KC - 1, 1))

            last = None
            for t in range(NT):
                for nu in range(2):
                    eng.wait_ge(*V.at("drained", ("qkv", nu, t)))
                if last:
                    eng.wait_ge(*V.at("v", last))
                v.tensor_tensor(sq[:, :], q_tok[:, t, :], q_tok[:, t, :], ALU.mult).then_inc(*V.step())
                eng.wait_ge(*V.at("v", V.steps))
                v.tensor_reduce(hss[:, t, 0:NH], sq[:, :].rearrange("p (h d) -> p h d", d=DH), axis=AX.X, op=ALU.add).then_inc(*V.step())
                last = V.steps
            for t in range(NT):
                eng.wait_ge(*V.at("drained", ("qkv", 2, t)))
                eng.wait_ge(*V.at("v", last))
                v.tensor_tensor(sq[:, 0:KVW], kr[:, t + 1, :], kr[:, t + 1, :], ALU.mult).then_inc(*V.step())
                eng.wait_ge(*V.at("v", V.steps))
                v.tensor_reduce(hss[:, t, NH:NH + NKV], sq[:, 0:KVW].rearrange("p (h d) -> p h d", d=DH), axis=AX.X, op=ALU.add).then_inc(*V.step())
                last = V.steps
            ALIAS(("hss",), ("v", last))
            eng.wait_ge(*V.at("v", last))
            eng.wait_ge(*V.at("hstd"))
            v.reciprocal(hrs[:, :, :], hrs[:, :, :]).then_inc(*V.step())
            eng.wait_ge(*V.at("v", V.steps))
            k_inv = V.steps
            eng.wait_ge(*V.at("v_hi"))
            v.tensor_tensor(v_hl[:, :, :, DH:2 * DH], vr[:, :, :].rearrange("p b (g d) -> p b g d", g=NKV),
                                  v_hl[:, :, :, 0:DH].bitcast(F32), ALU.subtract).then_inc(*V.up("v_v", "v_lo_half"))

            def normed(x3, t, h0, nh, rr, gain, name):
                n = nh * DH
                v.tensor_tensor(x3, x3, hrs[:, t, h0:h0 + nh].unsqueeze(2).broadcast_to([P, nh, DH]), ALU.mult).then_inc(*V.step())
                eng.wait_ge(*V.at("v", V.steps))
                if t == LT:
                    v.tensor_tensor(x3, x3, gq[:, gain:gain + 1, :].broadcast_to([P, nh, DH]), ALU.mult).then_inc(*V.up("v_rope", name, t))
                    return
                x4 = x3.rearrange("p h (a y i) -> p h a y i", a=2, y=2)
                r4 = rot[:, 0:n].rearrange("p (h a y i) -> p h a y i", h=nh, a=2, y=2)
                s4 = rr[:, 1, t, :].rearrange("p (a y i) -> p a y i", a=2, y=2)
                for a in range(2):
                    for y in range(2):
                        v.tensor_tensor(r4[:, :, a, y, :], x4[:, :, a, 1 - y, :],
                                               s4[:, a, y, :].unsqueeze(1).broadcast_to([P, nh, 16]), ALU.mult).then_inc(*V.step())
                        k = V.steps
                eng.wait_ge(*V.at("v", k))
                v.tensor_tensor(x3, x3, rr[:, 0, t:t + 1, :].broadcast_to([P, nh, DH]), ALU.mult).then_inc(*V.step())
                eng.wait_ge(*V.at("v", V.steps))
                v.tensor_tensor(x3, x3, rot[:, 0:n].rearrange("p (h d) -> p h d", h=nh), ALU.add).then_inc(*V.up("v_rope", name, t))

            eng.wait_ge(*V.at("v", k_rope))
            for t in range(NT):
                if t >= 1:
                    eng.wait_ge(*V.at("k_done", t - 1))
                normed(kr[:, t + 1, :].rearrange("p (h d) -> p h d", d=DH), t, NH, NKV, rk, 1, "k_done")
            ALIAS(("k_ready",), ("k_done", LT))
            for t in range(NT):
                eng.wait_ge(*V.at(*(("q_done", t - 1) if t else ("k_done", LT))))
                normed(q_tok[:, t, :].rearrange("p (h d) -> p h d", d=DH), t, 0, NH, rq, 0, "q_done")
            ALIAS(("q_ready",), ("q_done", LT))
            v.memset(glu[:, :, 0:PAD], 0.0).then_inc(*V.step())
            v.memset(glu[:, :, PAD + NLAT:PAD + NLAT + 2 * PAD], 0.0).then_inc(*V.step())
            v.memset(glu[:, :, CW - PAD:CW], 0.0).then_inc(*V.step())
            k_pad = V.steps
            for j in range(CCH):
                for i in range(2):
                    eng.wait_ge(*V.at("filled", ("ga", j, i)))
                    b = V.bank(("ga", j, i))
                    eng.wait_ge(*V.at("drained", ("gb", j, i)))
                    if i == 0:
                        v.tensor_tensor(glu[:, j, PAD:PAD + HALF], ps[:, b, 0:HALF], sgb[:, j % 2, 0:HALF], ALU.mult).then_inc(*V.drained(("ga", j, i)))
                    else:
                        n = NLAT - HALF
                        v.tensor_tensor(glu[:, j, PAD + HALF:PAD + NLAT], ps[:, b, 0:n], sgb[:, j % 2, HALF:NLAT], ALU.mult).then_inc(*V.step())
                        v.tensor_tensor(glu[:, j, PAD + CTX0:PAD + CTX0 + P], ps[:, b, n:HALF], sgb[:, j % 2, NLAT:NTOK], ALU.mult).then_inc(*V.drained(("ga", j, i)))
                ALIAS(("glu", j), ("drained", ("ga", j, 1)))
            for g2 in range(NKV // 2):
                for part, (c0, n) in enumerate(((0, 512), (512, 256))):
                    eng.wait_ge(*V.at("filled", ("kT", g2, part)))
                    b = V.bank(("kT", g2, part))
                    for x in range(2):
                        for y in range(2):
                            eng.wait_ge(*V.at("k_hi", g2, part, 1, 1))
                            ins = v.tensor_tensor(k_lo[y * DH:(y + 1) * DH, 2 * g2 + x, c0:c0 + n], ps[x * DH:(x + 1) * DH, b, 0:n],
                                                  k_hi[y * DH:(y + 1) * DH, 2 * g2 + x, c0:c0 + n].bitcast(F32), ALU.subtract)
                            if x == 1 and y == 1:
                                ins.then_inc(*V.drained(("kT", g2, part)))
                            else:
                                ins.then_inc(*V.step())

            def q_lo(h2):
                for part, (c0, n) in enumerate(((0, NLAT), (NLAT, P))):
                    eng.wait_ge(*V.at("filled", ("qT", h2, part)))
                    b = V.bank(("qT", h2, part))
                    eng.wait_ge(*V.at("q_hi", h2, part, 1))
                    for x in range(2):
                        ins = v.scalar_tensor_tensor(out=q_st[DH:P, x, c0:c0 + n], in0=ps[x * DH:(x + 1) * DH, b, 0:n], scalar=DH ** -0.5,
                                                     in1=q_st[0:DH, x, c0:c0 + n].bitcast(F32), op0=ALU.mult, op1=ALU.subtract)
                        if x == 1:
                            ins.then_inc(*V.drained(("qT", h2, part)))
                        else:
                            ins.then_inc(*V.step())
                for x in range(2):
                    ALIAS(("q_st", 2 * h2 + x), ("drained", ("qT", h2, 1)))

            def maxima(h, t):
                if h >= NH:
                    return
                eng.wait_ge(*V.at("filled", ("S", h, t, 0)))
                b0 = V.bank(("S", h, t, 0))
                eng.wait_ge(*V.at("filled", ("S", h, t, 1)))
                v.tensor_reduce(nmax[:, h % 2, t:t + 1], ps[:, b0:b0 + 2, 0:HALF], axis=AX.XY, op=ALU.max, negate=True).then_inc(*V.up("v_max", "nmax", h, t))

            def ctx_maximum(h):
                if h >= NH:
                    return
                eng.wait_ge(*V.at("filled", ("Sc", h)))
                b = V.bank(("Sc", h))
                v.tensor_reduce(cmax[:, h % 2:h % 2 + 1], ps[:, b, 0:P], axis=AX.X, op=ALU.max, negate=True).then_inc(*V.up("v_max", "cmax", h))

            def normalise(h, tiles):
                if h >= NH:
                    return
                t0, t1 = tiles[0], tiles[-1] + 1
                eng.wait_ge(*V.at("drained", ("S", h, t1 - 1, 0)))
                v.reciprocal(rsum[:, h % 2, t0:t1], rsum[:, h % 2, t0:t1]).then_inc(*V.step())
                eng.wait_ge(*V.at("v", V.steps))
                for t in tiles:
                    ins = v.tensor_scalar(probs[:, h % 2, t, :], probs[:, h % 2, t, :], rsum[:, h % 2, t:t + 1], None, ALU.mult)
                    ins.then_inc(*V.up("v_p", *(("probs", h) if t == LT - 1 else ())))

            def ctx_normalise(h):
                if h >= NH:
                    return
                eng.wait_ge(*V.at("drained", ("Sc", h)))
                v.reciprocal(csum[:, h % 2:h % 2 + 1], csum[:, h % 2:h % 2 + 1]).then_inc(*V.step())
                eng.wait_ge(*V.at("v", V.steps))
                v.tensor_scalar(ctxp[:, h % 2, :], ctxp[:, h % 2, :], csum[:, h % 2:h % 2 + 1], None, ALU.mult).then_inc(*V.up("v_p", "ctx_probs", h))

            def probs_lo(h, kc):
                eng.wait_ge(*V.at("pt_hi", h, kc))
                eng.wait_ge(*V.at("filled", ("PT", h, kc)))
                b = V.bank(("PT", h, kc))
                k = (h * NT + kc) % 3
                v.tensor_tensor(pt_lo[:, k, :], ps[:, b, :], pt_hi[:, k, :].bitcast(F32), ALU.subtract).then_inc(*V.drained(("PT", h, kc)))

            def ctx_lo(h):
                eng.wait_ge(*V.at("cpt_hi", h))
                eng.wait_ge(*V.at("filled", ("PTc", h)))
                b = V.bank(("PTc", h))
                v.tensor_tensor(cpt_lo[:, h % 2, :], ps[:, b, 0:P], cpt_hi[:, h % 2, :].bitcast(F32), ALU.subtract).then_inc(*V.drained(("PTc", h)))

            def ctx_output(h):
                x = h % 2
                eng.wait_ge(*V.at("oc_half", h))
                eng.wait_ge(*V.at("filled", ("Oc", h)))
                b = V.bank(("Oc", h))
                v.tensor_tensor(o_t[x * DH:(x + 1) * DH, LT, h // 2, :], ps[0:DH, b, 0:P], oscb[:, :], ALU.add).then_inc(*V.drained(("Oc", h)))

            def output(h):
                x = h % 2
                eng.wait_ge(*V.at("o_half", h))
                eng.wait_ge(*V.at("filled", ("O", h)))
                b = V.bank(("O", h))
                v.tensor_tensor(o_t[x * DH:(x + 1) * DH, 0:LT, h // 2, :],
                                ps[0:DH, b, :].rearrange("p (t n) -> p t n", t=LT), osb[:, :].rearrange("p (t n) -> p t n", t=LT), ALU.add).then_inc(*V.drained(("O", h)))

            q_lo(0)
            for t in range(LT):
                maxima(0, t)
            ctx_maximum(0)
            normalise(0, range(LT))
            ctx_normalise(0)
            for h in range(NH):
                if h + 1 < NH and (h + 1) % 2 == 0:
                    q_lo((h + 1) // 2)
                probs_lo(h, 0)
                probs_lo(h, 1)
                ctx_lo(h)
                maxima(h + 1, 0)
                probs_lo(h, 2)
                maxima(h + 1, 1)
                probs_lo(h, 3)
                ctx_output(h)
                maxima(h + 1, 2)
                probs_lo(h, 4)
                maxima(h + 1, 3)
                ctx_maximum(h + 1)
                normalise(h + 1, range(0, 2))
                normalise(h + 1, range(2, LT))
                ctx_normalise(h + 1)
                output(h)
            for k in range(KC):
                eng.wait_ge(*V.at("o_hi", k))
                v.tensor_tensor(o_lo[:, k, :].rearrange("p (t n) -> p t n", t=NT), o_t[:, :, k, :],
                                      o_hi[:, k, :].rearrange("p (t n) -> p t n", t=NT).bitcast(F32), ALU.subtract).then_inc(*V.up("v_oh", *(("o_split",) if k == KC - 1 else ())))
            eng.wait_ge(*V.at("o_split"))
            eng.wait_ge(*V.at("drained", ("ga", CCH - 1, 1)))
            eng.wait_ge(*V.at("v", k_pad))
            taps = [(k, c) for k in range(TAPS) for c in range(CCH)]
            tap_step = {}
            share = -(-len(taps) // KC)
            for b8 in range(KC):
                for k, c in taps[b8 * share:(b8 + 1) * share]:
                    src = glu[:, c, k:k + CO]
                    if k == 0:
                        ins = v.tensor_scalar(cv[:, c, :], src, convw[:, c, 0:1], convb[:, c:c + 1], ALU.mult, ALU.add)
                    else:
                        eng.wait_ge(*V.at("v", tap_step[(k - 1, c)]))
                        ins = v.scalar_tensor_tensor(out=cv[:, c, :], in0=src, scalar=convw[:, c, k:k + 1], in1=cv[:, c, :],
                                                     op0=ALU.mult, op1=ALU.add)
                    ins.then_inc(*V.step())
                    tap_step[(k, c)] = V.steps
                for i in range(2):
                    eng.wait_ge(*V.at("filled", ("ao", b8, i)))
                    b = V.bank(("ao", b8, i))
                    eng.wait_ge(*V.at("drained", ("gta", b8, i)))
                    v.tensor_tensor(m_t[:, b8, i * HALF:(i + 1) * HALF], ps[:, b, 0:HALF], sga[:, i * HALF:(i + 1) * HALF], ALU.mult).then_inc(*V.drained(("ao", b8, i)))
            ALIAS(("cv",), ("v", tap_step[(TAPS - 1, CCH - 1)]))
            for t in range(NT):
                eng.wait_ge(*V.at("filled", ("cvT", t)))
                b = V.bank(("cvT", t))
                v.bn_stats(bst[:, t, :], ps[:, b, :]).then_inc(*V.step())
                k = V.steps
            eng.wait_ge(*V.at("v", k))
            eng.sem_inc(sems("passed_V"), 1)
            for t in range(NT):
                v.bn_aggr(bag[:, t, :], bst[:, t, :]).then_inc(*V.up("v_bn", *(("cv_var",) if t == NT - 1 else ())))
            eng.wait_ge(*V.at("cstd"))
            v.reciprocal(rstd[:, 0:NT], std[:, 0:NT]).then_inc(*V.step())
            eng.wait_ge(*V.at("v", V.steps))
            for t in range(NT):
                eng.wait_ge(*V.at("filled", ("cvT", t)))
                b = V.bank(("cvT", t))
                v.tensor_scalar(cn[:, t, :], ps[:, b, :], bag[:, t, 0:1], rstd[:, t:t + 1], ALU.subtract, ALU.mult).then_inc(*V.drained(("cvT", t)))
            for t in range(NT):
                eng.wait_ge(*V.at("drained", ("cvT", t)))
            ins = v.memset(ssq[:, 7:8], 0.0)
            ins.then_inc(*V.up("v_cn", "cn"))
            for c in range(CCH):
                eng.wait_ge(*V.at("c_hi", c))
                v.tensor_tensor(c_lo[:, c, :], c_f[:, c % 2, :], c_hi[:, c, :].bitcast(F32), ALU.subtract).then_inc(*V.up("v_c", "c_lo", c))
            def m_lo_of(b8):
                eng.wait_ge(*V.at("m_hi", b8))
                v.tensor_tensor(m_lo[:, b8, :], m_t[:, b8, :], m_hi[:, b8, :].bitcast(F32), ALU.subtract).then_inc(*V.up("v_m", "m_lo", b8))

            for b8 in range(KC):
                for i in range(2):
                    h0 = i * HALF
                    eng.wait_ge(*V.at("filled", ("co", b8, i)))
                    b = V.bank(("co", b8, i))
                    if b8 >= 2:
                        eng.wait_ge(*V.at("merged", b8 - 2))
                    v.tensor_tensor(m_tmp[:, b8 % 2, h0:h0 + HALF], ps[:, b, 0:HALF], sgc[:, b8, h0:h0 + HALF], ALU.mult).then_inc(*V.drained(("co", b8, i)))
                eng.wait_ge(*V.at("drained", ("co", b8, 0)))
                eng.wait_ge(*V.at("drained", ("co", b8, 1)))
                v.tensor_tensor(m_t[:, b8, :], m_t[:, b8, :], m_tmp[:, b8 % 2, :], ALU.add).then_inc(*V.up("v_m2", "merged", b8))
                if b8 >= 1:
                    m_lo_of(b8 - 1)
            m_lo_of(KC - 1)
            eng.wait_ge(*V.at("n2_in"))
            eng.wait_ge(*V.at("m_lo", KC - 1))
            for i in range(2):
                v.scalar_tensor_tensor(out=a2_row[:, i, :], in0=a2_row[:, i, :], scalar=1.0, in1=n2_row[:, :], op0=ALU.add, op1=ALU.mult).then_inc(*V.step())
                k = V.steps
            for nh in range(2):
                cols = slice(nh * 512, (nh + 1) * 512)
                for t in range(NT):
                    eng.wait_ge(*V.at("filled", ("wo", nh, t)))
                    b = V.bank(("wo", nh, t))
                    v.tensor_tensor(h_a[:, t, cols], ps[:, b, :], g1_row[:, t // LT, cols], ALU.mult).then_inc(*V.drained(("wo", nh, t)))
                for t in range(NT):
                    eng.wait_ge(*V.at("drained", ("wo", nh, t)))
                    v.tensor_tensor(h_a[:, t, cols], h_a[:, t, cols], h_in[:, t, cols], ALU.add).then_inc(*V.up("v_ha", *(("h_a", t) if nh else ("h_a0", t))))
            eng.wait_ge(*V.at("std2"))
            v.reciprocal(rstd[:, 0:NT], std[:, 0:NT]).then_inc(*V.step())
            eng.wait_ge(*V.at("v", V.steps))
            eng.wait_ge(*V.at("h_a", NT - 1))
            for t in range(NT):
                v.scalar_tensor_tensor(out=u2[:, t, :], in0=h_a[:, t, :], scalar=rstd[:, t:t + 1], in1=a2_row[:, t // LT, :],
                                                     op0=ALU.mult, op1=ALU.mult).then_inc(*V.step())
                eng.wait_ge(*V.at("v", V.steps))
                v.tensor_tensor(u2[:, t, :], u2[:, t, :], b2_row[:, t // LT, :], ALU.add).then_inc(*V.up("v_u2", "u2", t))
                if t >= 1:
                    u2t(eng, V, t - 1)
            u2t(eng, V, NT - 1)
            eng.wait_ge(*V.at("filled", ("router",)))
            b = V.bank(("router",))
            lgp = ps[:, b, 0:NT * NE].rearrange("p (t e) -> p t e", e=NE)
            bc = lambda x: x.unsqueeze(2).broadcast_to([P, NT, NE])
            v.tensor_reduce(ssq[:, 0:NT], lgp, axis=AX.X, op=ALU.max).then_inc(*V.step())
            eng.wait_ge(*V.at("v", V.steps))
            v.tensor_tensor(lg[:, :, :], lgp, bc(ssq[:, 0:NT]), ALU.subtract).then_inc(*V.drained(("router",)))
            ALIAS(("lg_shift",), ("drained", ("router",)))
            eng.wait_ge(*V.at("lg_exp"))
            v.tensor_reduce(ssq[:, 0:NT], lg[:, :, :], axis=AX.X, op=ALU.add).then_inc(*V.step())
            eng.wait_ge(*V.at("v", V.steps))
            v.reciprocal(ssq[:, 0:NT], ssq[:, 0:NT]).then_inc(*V.step())
            eng.wait_ge(*V.at("v", V.steps))
            v.tensor_tensor(lg[:, :, :], lg[:, :, :], bc(ssq[:, 0:NT]), ALU.mult).then_inc(*V.step())
            eng.wait_ge(*V.at("v", V.steps))
            v.tensor_tensor(sel[:, :, :], lg[:, :, :], rb[:, :].unsqueeze(1).broadcast_to([P, NT, NE]), ALU.add).then_inc(*V.step())
            eng.wait_ge(*V.at("v", V.steps))
            s4 = sel[:, :, :].rearrange("p t (g e) -> p t g e", e=EPG)
            for t in range(NT):
                v.tensor_tensor(pair[:, t, :, 0:3], s4[:, t, :, 0:3], s4[:, t, :, 1:4], ALU.add).then_inc(*V.step())
                v.tensor_tensor(pair[:, t, :, 3:5], s4[:, t, :, 0:2], s4[:, t, :, 2:4], ALU.add).then_inc(*V.step())
                v.tensor_tensor(pair[:, t, :, 5:6], s4[:, t, :, 0:1], s4[:, t, :, 3:4], ALU.add).then_inc(*V.step())
            v.memset(g8[:, :, NG:8], -1e30).then_inc(*V.step())
            k = V.steps
            eng.wait_ge(*V.at("v", k))
            v.tensor_reduce(g8[:, :, 0:NG], pair[:, :, :, :], axis=AX.X, op=ALU.max).then_inc(*V.step())
            eng.wait_ge(*V.at("v", V.steps))
            eng.sem_inc(sems("passed_V"), 1)
            for t in range(NT):
                v.max(top8[:, t, :], g8[:, t, :]).then_inc(*V.step())
                k = V.steps
            eng.wait_ge(*V.at("v", k))
            eng.sem_inc(sems("passed_V"), 1)
            for t in range(NT):
                v.max_index(idx8[:, t, :], top8[:, t, :], g8[:, t, :]).then_inc(*V.step())
                k = V.steps
            eng.wait_ge(*V.at("v", k))
            v.tensor_copy(ef[:, :, 0:1], idx8[:, :, 0:1]).then_inc(*V.step())
            eng.wait_ge(*V.at("v", V.steps))
            v.tensor_tensor(tmp16[:, :, :], grpof[:, :].unsqueeze(1).broadcast_to([P, NT, NE]),
                                          bc(ef[:, :, 0]), ALU.is_equal).then_inc(*V.step())
            eng.wait_ge(*V.at("v", V.steps))
            v.tensor_scalar(tmp16[:, :, :], tmp16[:, :, :], 1e30, -1e30, ALU.mult, ALU.add).then_inc(*V.step())
            eng.wait_ge(*V.at("v", V.steps))
            v.tensor_tensor(sel[:, :, :], sel[:, :, :], tmp16[:, :, :], ALU.add).then_inc(*V.step())
            eng.wait_ge(*V.at("v", V.steps))
            eng.wait_ge(*V.at("v", V.steps))
            eng.sem_inc(sems("passed_V"), 1)
            for t in range(NT):
                v.max(top8[:, t, :], sel[:, t, :]).then_inc(*V.step())
                k = V.steps
            eng.wait_ge(*V.at("v", k))
            eng.sem_inc(sems("passed_V"), 1)
            for t in range(NT):
                v.max_index(idx8[:, t, :], top8[:, t, :], sel[:, t, :]).then_inc(*V.step())
                k = V.steps
            eng.wait_ge(*V.at("v", k))
            v.tensor_copy(ef[:, :, :], idx8[:, :, :]).then_inc(*V.step())
            eng.wait_ge(*V.at("v", V.steps))
            iot3 = iot[:, :].unsqueeze(1).broadcast_to([P, NT, NE])
            for x in range(2):
                v.tensor_tensor(msk[:, x, :, :], iot3, bc(ef[:, :, x]), ALU.is_equal).then_inc(*V.step())
                k = V.steps
            eng.wait_ge(*V.at("v", k))
            v.tensor_tensor(cnt[:, :, :], msk[:, 0, :, :], msk[:, 1, :, :], ALU.add).then_inc(*V.up("v_mask", "mask"))
            for x in range(2):
                v.tensor_tensor(tmp16[:, :, :], msk[:, x, :, :], lg[:, :, :], ALU.mult).then_inc(*V.step())
                eng.wait_ge(*V.at("v", V.steps))
                v.tensor_reduce(wsel[:, x, :], tmp16[:, :, :], axis=AX.X, op=ALU.add).then_inc(*V.step())
                eng.wait_ge(*V.at("v", V.steps))
            v.tensor_tensor(ssq[:, 0:NT], wsel[:, 0, :], wsel[:, 1, :], ALU.add).then_inc(*V.step())
            eng.wait_ge(*V.at("v", V.steps))
            v.reciprocal(ssq[:, 0:NT], ssq[:, 0:NT]).then_inc(*V.step())
            eng.wait_ge(*V.at("v", V.steps))
            v.tensor_tensor(wsel[:, :, :], wsel[:, :, :], ssq[:, 0:NT].unsqueeze(1).broadcast_to([P, 2, NT]), ALU.mult).then_inc(*V.step())
            eng.wait_ge(*V.at("v", V.steps))
            eng.wait_ge(*V.at("filled", ("place",)))
            b = V.bank(("place",))
            v.tensor_copy(pos[:, :, :].rearrange("p t e -> p (t e)"), ps[:, b, 0:NT * NE]).then_inc(*V.step())
            eng.wait_ge(*V.at("filled", ("place",)))
            v.tensor_copy(cnt[:, :, :].rearrange("p t e -> p (t e)"), ps[:, b, 256:256 + NT * NE]).then_inc(*V.drained(("place",)))
            eng.wait_ge(*V.at("drained", ("place",)))
            for t in range(1, NT):
                if t == 1:
                    v.tensor_copy(sca[:, 0, :], cnt[:, 0, :]).then_inc(*V.step())
                    eng.wait_ge(*V.at("v", V.steps))
                else:
                    v.tensor_tensor(sca[:, 0, :], sca[:, 0, :], cnt[:, t - 1, :], ALU.add).then_inc(*V.step())
                    eng.wait_ge(*V.at("v", V.steps))
                v.tensor_tensor(pos[:, t, :], pos[:, t, :], sca[:, 0, :], ALU.add).then_inc(*V.step())
                eng.wait_ge(*V.at("v", V.steps))
            v.tensor_tensor(sca[:, 0, :], sca[:, 0, :], cnt[:, NT - 1, :], ALU.add).then_inc(*V.step())
            eng.wait_ge(*V.at("v", V.steps))
            v.tensor_scalar(sca[:, 1, :], sca[:, 0, :], float(P), 1.0, ALU.is_gt, ALU.add).then_inc(*V.step())
            eng.wait_ge(*V.at("v", V.steps))
            for k in range(2, NT):
                v.tensor_scalar(sca[:, 2, :], sca[:, 0, :], float(k * P), None, ALU.is_gt).then_inc(*V.step())
                eng.wait_ge(*V.at("v", V.steps))
                v.tensor_tensor(sca[:, 1, :], sca[:, 1, :], sca[:, 2, :], ALU.add).then_inc(*V.step())
                eng.wait_ge(*V.at("v", V.steps))
            src = 1
            for d in (1, 2, 4, 8):
                dst = 3 if src != 3 else 2
                v.tensor_copy(sca[:, dst, 0:d], sca[:, src, 0:d]).then_inc(*V.step())
                v.tensor_tensor(sca[:, dst, d:NE], sca[:, src, d:NE], sca[:, src, 0:NE - d], ALU.add).then_inc(*V.step())
                eng.wait_ge(*V.at("v", V.steps))
                src = dst
            v.memset(start[:, 0:1], 0.0).then_inc(*V.step())
            v.tensor_copy(start[:, NE + 1:NE + 3], tbase[:, :]).then_inc(*V.step())
            v.tensor_copy(start[:, 1:NE + 1], sca[:, src, :]).then_inc(*V.step())
            eng.wait_ge(*V.at("v", V.steps))
            v.tensor_copy(start_i[:, :], start[:, :]).then_inc(*V.up("v_start", "starts"))
            v.tensor_scalar(sca[:, 0, :], start[:, 0:NE], float(P), None, ALU.mult).then_inc(*V.step())
            eng.wait_ge(*V.at("v", V.steps))
            v.tensor_tensor(pos[:, :, :], pos[:, :, :], sca[:, 0:1, :].broadcast_to([P, NT, NE]), ALU.add).then_inc(*V.step())
            eng.wait_ge(*V.at("v", V.steps))
            for x in range(2):
                v.tensor_tensor(tmp16[:, :, :], msk[:, x, :, :], pos[:, :, :], ALU.mult).then_inc(*V.step())
                eng.wait_ge(*V.at("v", V.steps))
                v.tensor_reduce(slot[:, x, :], tmp16[:, :, :], axis=AX.X, op=ALU.add).then_inc(*V.step())
                eng.wait_ge(*V.at("v", V.steps))
            v.tensor_copy(slot_u[:, :, :], slot[:, :, :]).then_inc(*V.step())
            for x in range(2):
                v.tensor_copy(rows[:, x, :, 0], tokid[:, :]).then_inc(*V.step())
                v.tensor_scalar(rows[:, x, :, 1], tokid[:, :], float(x * NTOK), None, ALU.add).then_inc(*V.step())
                v.tensor_copy(rows[:, x, :, 2].bitcast(F32), wsel[:, x, :]).then_inc(*V.step())
                v.memset(rows[:, x, :, 3], 0).then_inc(*V.step())
                k = V.steps
            v.tensor_tensor(tbase[:, 1:2], start[:, NE:NE + 1], start[:, NE + 2:NE + 3], ALU.add).then_inc(*V.step())
            v.scalar_tensor_tensor(out=tbase[:, 0:1], in0=start[:, NE:NE + 1], scalar=1.0, in1=start[:, NE + 1:NE + 2], op0=ALU.add, op1=ALU.add).then_inc(*V.step())
            k2 = V.steps
            ALIAS(("rank",), ("v", k2))
            eng.wait_ge(*V.at("v", k2))

            eng.wait_ge(*V.at("u2_out"))
            eng.sem_inc(sems("passed_V"), 1)
            g0 = eng.value_load(start_i[0:1, NE + 1:NE + 2], min_val=1, max_val=DEPTH * MAXT)
            n0 = eng.value_load(start_i[0:1, NE + 2:NE + 3], min_val=0, max_val=DEPTH * MAXT)

            def xt_lo_of(g):
                eng.wait_ge(sems("xt_hi"), g)
                v.tensor_tensor(xt_lo[:, :, :].rearrange("p (a c) n -> p a (c n)", a=2), ps[:, 0:2, :],
                                xt_hi[:, :, :].rearrange("p (a c) n -> p a (c n)", a=2).bitcast(F32), ALU.subtract).then_inc(sems("xt_split"), 1)

            eng.wait_ge(*V.at("tab_in"))
            xt_lo_of(g0)
            for e in range(NE):
                s = eng.value_load(start_i[0:1, e:e + 1], min_val=0, max_val=MAXT - 1)
                s2 = eng.value_load(start_i[0:1, e + 1:e + 2], min_val=0, max_val=MAXT - 1)
                if e + 1 < NE:
                    for k in range(2):
                        lo(U_MOE + 3 * (e + 1) + k)
                with eng.Fori(s, s2) as j:
                    g, n = g0 + j, n0 + j + 1
                    eng.wait_ge(sems("gu_full"), n)
                    v.tensor_copy(wrow[:, :], tab[:, bass.ds(j, 1), 2].bitcast(F32)).then_inc(sems("w_row"), 1)
                    eng.wait_ge(sems("w_row"), n)
                    eng.wait_ge(sems("sg_ready"), n)
                    v.scalar_tensor_tensor(out=hx[:, :], in0=ps[:, 2, DE:2 * DE], scalar=wrow[:, :], in1=sg[:, :],
                                           op0=ALU.mult, op1=ALU.mult).then_inc(sems("h_ready"), 1)
                    xt_lo_of(g + 1)
                    eng.wait_ge(sems("ht_hi"), n)
                    v.tensor_tensor(ht_lo[:, :, :].rearrange("p c n -> p (c n)"), ps[:, 3, 0:2 * P],
                                    ht_hi[:, :, :].rearrange("p c n -> p (c n)").bitcast(F32), ALU.subtract).then_inc(sems("ht_split"), 1)
                if e + 1 < NE:
                    lo(U_MOE + 3 * (e + 1) + 2)
            eng.wait_ge(*V.at("g2_in", 1))
            for t in range(NT):
                eng.wait_ge(*V.at("cmb_in", t))
                i = t % 2
                v.tensor_tensor(cmb[:, i, 1, :], cmb[:, i, 1, :], cmb[:, i, 2, :], ALU.add).then_inc(*V.step())
                eng.wait_ge(*V.at("v", V.steps))
                v.tensor_tensor(cmb[:, i, 1, :], cmb[:, i, 1, :], g2_row[:, t // LT, :], ALU.mult).then_inc(*V.step())
                eng.wait_ge(*V.at("v", V.steps))
                v.tensor_tensor(cmb[:, i, 0, :], cmb[:, i, 0, :], cmb[:, i, 1, :], ALU.add).then_inc(*V.up("v_h", "h", t))
        V.l = None
        ledger.section = "after"
        eng.wait_ge(*V.at("fin_std"))
        v.reciprocal(rstd[:, 0:NT], std[:, 0:NT]).then_inc(*V.up("v_fin", "fin_rstd"))
        eng.wait_ge(*V.at("fin_rstd"))
        for t in range(NT):
            v.scalar_tensor_tensor(out=fin[:, t, :], in0=fin[:, t, :], scalar=rstd[:, t:t + 1], in1=fin_row[:, :],
                                         op0=ALU.mult, op1=ALU.mult).then_inc(*V.up("v_fin", "y", t))

    @block.scalar
    def _(eng):
        A = Counts(ledger, sems)
        ledger.section = "after"
        eng.wait_ge(*A.at("fin_in"))
        for t in range(NT):
            if t >= 2:
                eng.wait_ge(*A.at("fin_ss", t - 2))
            nc.scalar.activation(junk2[:, t % 2, :], fin[:, t, :], ACT.Square, accum_out=ssq[:, t:t + 1]).then_inc(*A.up("a_fin", "fin_ss", t))
        eng.wait_ge(*A.at("fin_ss", NT - 1))
        nc.scalar.activation(std[:, 0:NT], ssq[:, 0:NT], ACT.Sqrt, bias=eps[:, :], scale=1.0 / D).then_inc(*A.up("a_fin", "fin_std"))

    @block.gpsimd
    def _(eng):
        G = Counts(ledger, sems)
        g_ = nc.gpsimd
        ledger.section = "before"
        def dma(dst, src, sem, *event):
            eng.dma_start(dst, src).then_inc(*G.up(sem, *event, by=16))
        dma(craw[:, :, :], io["c_cols"], "g_in", "c_loaded")
        dma(h_d, io["x_all"], "h_st", "h0")
        dma(wr[:, :, :], io["w_router"].rearrange("(c p) e -> p c e", p=P), "g_in2")
        dma(rb[:, :], io["router_bias"].rearrange("(a e) -> a e", a=1).broadcast_to([P, NE]), "g_in2")
        dma(cosr[:, :, :], io["cos"].rearrange("(t p) d -> p t d", p=P), "g_in2")
        dma(sinr[:, :, :], io["sin"].rearrange("(t p) d -> p t d", p=P), "g_in2", "wr_loaded")
        g_.memset(eps[:, :], EPS).then_inc(*G.up("g_c", "eps"))
        g_.memset(ident[:, :], 0.0).then_inc(*G.up("g_c", "id0"))
        g_.memset(ones[:, :], 1.0).then_inc(*G.up("g_c", "ones"))
        g_.memset(tri[:, :], 1.0).then_inc(*G.up("g_c", "tri0"))
        g_.memset(ye[:, :], 0.0).then_inc(*G.up("g_c"))
        eng.wait_ge(*G.at("tri0"))
        eng.sem_inc(sems("passed_G"), 1)
        g_.affine_select(out=tri[:, :], in_=tri[:, :], compare_op=ALU.is_ge, fill=0.0, base=-1, pattern=[[1, P]], channel_multiplier=-1).then_inc(*G.up("g_c", "tri"))
        g_.affine_select(out=ident[:, :], in_=ident[:, :], compare_op=ALU.not_equal, fill=1.0, base=0, pattern=[[-1, P]], channel_multiplier=1).then_inc(*G.up("g_c", "ident_g"))
        g_.iota(iot[:, :], pattern=[[1, NE]], base=0, channel_multiplier=0, allow_small_or_imprecise_dtypes=True).then_inc(*G.up("g_c"))
        g_.iota(grpof[:, :], pattern=[[1, NG], [0, EPG]], base=0, channel_multiplier=0, allow_small_or_imprecise_dtypes=True).then_inc(*G.up("g_c"))
        g_.iota(tokid[:, :], pattern=[[P, NT]], base=0, channel_multiplier=1, allow_small_or_imprecise_dtypes=True).then_inc(*G.up("g_c"))
        g_.memset(blank[:, :, :], 0).then_inc(*G.up("g_c", "blank0"))
        eng.wait_ge(*G.at("blank0"))
        eng.sem_inc(sems("passed_G"), 1)
        g_.memset(blank[:, :, 1:2], SKIP).then_inc(*G.up("g_c", "blank1"))
        eng.wait_ge(*G.at("blank1"))
        eng.sem_inc(sems("passed_G"), 1)
        g_.memset(mrt[:, :], 0.0).then_inc(*G.up("g_c", "ident"))
        eng.dma_start(tab_d.rearrange("(p g) f -> p g f", p=P), blank[:, :, :]).then_inc(sems("y_sent"), 16)
        eng.wait_ge(sems("y_sent"), 16)
        eng.wait_ge(*G.at("h0"))
        eng.sem_inc(sems("passed_G"), 1)
        ledger.section = "layer"
        with eng.Fori(0, DEPTH) as l:
            G.l = l
            dma(xn[:, :, :], A_hs, "h_ld", "h_loaded")
            for x, name in enumerate(("q_norm_g", "k_norm_g")):
                dma(gq[:, x, :], io[name][bass.ds(l, 1), :].broadcast_to([P, DH]), "g_small")
            dma(n1col[:, :], io["n1_cols"][l], "g_small")
            dma(convw[:, :, :], io["conv_w_t"][l], "g_small")
            dma(convb[:, :], io["conv_b_cols"][l], "g_small")
            dma(lng[:, :], io["ln_g_cols"][l], "g_small")
            dma(lnb[:, :], io["ln_b_cols"][l], "g_small", "small_loaded")
            dma(tab_d.rearrange("(p g) f -> p g f", p=P), blank[:, :, :], "g_blank", "blanked")
            for j in range(N_ADA // 2):
                if j >= 2:
                    eng.wait_ge(*G.at("drained", ("ada", j - 2)))
                    eng.sem_inc(sems("passed_G"), 1)
                    dma(mod_d[:, (j - 2) * 512:(j - 1) * 512], mrow[:, j % 2, :], f"mod_st{j % 2}", "mod_out", j - 2)
                for i in range(2):
                    dma(adab[i:i + 1, j % 2, :], io["b_ada"][bass.ds(l, 1), j * 512:(j + 1) * 512], f"ada_b{j % 2}", *(("ada_bias", j) if i else ()))
            for j in (10, 11):
                eng.wait_ge(*G.at("drained", ("ada", j)))
                eng.sem_inc(sems("passed_G"), 1)
                dma(mod_d[:, j * 512:(j + 1) * 512], mrow[:, j % 2, :], f"mod_st{j % 2}", "mod_out", j)
            eng.wait_ge(*G.at("mod_out", 10))
            eng.sem_inc(sems("passed_G"), 1)
            eng.wait_ge(*G.at("mod_out", 11))
            eng.sem_inc(sems("passed_G"), 1)
            for i in range(2):
                dma(mrt[i * 16:(i + 1) * 16, :], mod_d[i, 0:2 * D].rearrange("(r p) -> r p", p=P), "mrt", *(("mrt",) if i else ()))
            eng.wait_ge(*G.at("u_lo", KC - 1, 1))
            eng.sem_inc(sems("passed_G"), 1)
            eng.wait_ge(*G.at("std1"))
            eng.sem_inc(sems("passed_G"), 1)
            dma(kr[:, 0, :], io["cache_k"][0, l].rearrange("s h d -> s (h d)"), "cache")
            dma(vr[:, 0, :], io["cache_v"][0, l].rearrange("s h d -> s (h d)"), "cache", "cache_loaded")

            def lo(n):
                eng.wait_ge(*G.at("w_hi", n))
                if n >= U_MOE:
                    g_.tensor_tensor(expert_half(n, 0), raw_of(n), expert_half(n, 1).bitcast(F32), ALU.subtract).then_inc(*G.up("g_lo", "w_lo", n))
                    return
                k = size(n)
                g_.tensor_tensor(w_lo[:, n % 2, 0:k], raw[:, n % 2, 0:k], w_hi[:, n % 2, 0:k].bitcast(F32), ALU.subtract).then_inc(*G.up("g_lo", "w_lo", n))

            for n in range(U_QKV, U_GLU + 2):
                lo(n)
            eng.wait_ge(*G.at("k_done", LT))
            eng.sem_inc(sems("passed_G"), 1)
            dma(out["new_k"][0, l].rearrange("s h d -> s (h d)"), kr[:, 5, :], "out_kv")
            dma(out["new_v"][0, l].rearrange("s h d -> s (h d)"), vr[:, 5, :], "out_kv", "kv_out")
            eng.wait_ge(*G.at("kv_out"))
            eng.sem_inc(sems("passed_G"), 1)
            g_.memset(ssq[:, 6:7], 0.0).then_inc(*G.up("g_c", "kv_free"))
            for n in range(U_GLU + 2, U_MOE + 3):
                lo(n)
            eng.wait_ge(*G.at("rank"))
            eng.sem_inc(sems("passed_G"), 1)
            eng.wait_ge(*G.at("blanked"))
            eng.sem_inc(sems("passed_G"), 1)
            for x in range(2):
                for t in range(NT):
                    eng.indirect_dma_start(out=tab_d, out_offset=bass.IndirectOffsetOnAxis(ap=slot_u[:, x, t:t + 1], axis=0),
                                                 in_=rows[:, x, t, :], in_offset=None, bounds_check=MAXT * P - 1, oob_is_err=False).then_inc(*G.up("tab_st", "tab_row", x, t, by=16))
            eng.wait_ge(*G.at("tab_row", 1, NT - 1))
            eng.sem_inc(sems("passed_G"), 1)
            dma(tab[:, :, :], tab_d.rearrange("(g p) f -> p g f", p=P), "tab_ld", "tab_in")
            eng.wait_ge(*G.at("tab_in"))
            eng.sem_inc(sems("passed_G"), 1)
            eng.wait_ge(*G.at("u2_out"))
            eng.sem_inc(sems("passed_G"), 1)
            eng.wait_ge(*G.at("ha_out"))
            eng.sem_inc(sems("passed_G"), 1)
            g0 = eng.value_load(start_i[0:1, NE + 1:NE + 2], min_val=1, max_val=DEPTH * MAXT)
            n0 = eng.value_load(start_i[0:1, NE + 2:NE + 3], min_val=0, max_val=DEPTH * MAXT)

            def wait_apart(sem, value):
                eng.wait_ge(sems(sem), value)
                eng.sem_inc(sems("passed_G"), 1)

            def gather(j):
                at_j = tab[:, bass.ds(j, 1), 0] if not isinstance(j, int) else tab[:, j:j + 1, 0]
                g_.tensor_copy(gidx[:, :], at_j).then_inc(sems("g_idx"), 1)
                wait_apart("g_idx", g0 + j)
                eng.indirect_dma_start(out=xe[:, :], out_offset=None, in_=u2_d,
                                       in_offset=bass.IndirectOffsetOnAxis(ap=gidx[:, :], axis=0),
                                       bounds_check=NTOK - 1, oob_is_err=False).then_inc(sems("xe_landed"), 16)

            gather(0)
            for e in range(NE):
                s = eng.value_load(start_i[0:1, e:e + 1], min_val=0, max_val=MAXT - 1)
                s2 = eng.value_load(start_i[0:1, e + 1:e + 2], min_val=0, max_val=MAXT - 1)
                with eng.Fori(s, s2) as j:
                    g, n = g0 + j, n0 + j + 1
                    wait_apart("xt_full", g)
                    gather(j + 1)
                    eng.wait_ge(sems("y_sent"), 16 * n)
                    g_.tensor_copy(sidx[:, :], tab[:, bass.ds(j, 1), 1]).then_inc(sems("s_idx"), 1)
                    eng.wait_ge(sems("s_idx"), n)
                    wait_apart("y_drained", n)
                    eng.indirect_dma_start(out=y_d, out_offset=bass.IndirectOffsetOnAxis(ap=sidx[:, :], axis=0),
                                           in_=ye[:, :], in_offset=None,
                                           bounds_check=2 * NTOK - 1, oob_is_err=False).then_inc(sems("y_sent"), 16)
            wait_apart("xt_split", g0 + s2)
            wait_apart("y_sent", 16 * (n0 + s2 + 1))
            for t in range(NT):
                rs = slice(t * P, (t + 1) * P)
                if t >= 2:
                    eng.wait_ge(*G.at("h_stored", t - 2))
                    eng.sem_inc(sems("passed_G"), 1)
                dma(cmb[:, t % 2, 0, :], ha_d[rs, :], f"cmb{t % 2}")
                dma(cmb[:, t % 2, 1, :], y_d[rs, :], f"cmb{t % 2}")
                dma(cmb[:, t % 2, 2, :], y_d[NTOK + t * P:NTOK + (t + 1) * P, :], f"cmb{t % 2}", "cmb_in", t)
                if t >= 1:
                    eng.wait_ge(*G.at("h", t - 1))
                    eng.sem_inc(sems("passed_G"), 1)
                    dma(h_d[(t - 1) * P:t * P, :], cmb[:, (t - 1) % 2, 0, :], f"h_st{(t - 1) % 2}", "h_stored", t - 1)
            eng.wait_ge(*G.at("h", NT - 1))
            eng.sem_inc(sems("passed_G"), 1)
            dma(h_d[(NT - 1) * P:NT * P, :], cmb[:, (NT - 1) % 2, 0, :], f"h_st{(NT - 1) % 2}", "h_stored", NT - 1)
            eng.wait_ge(*G.at("h_stored", NT - 2))
            eng.sem_inc(sems("passed_G"), 1)
            eng.wait_ge(*G.at("h_stored", NT - 1))
            eng.sem_inc(sems("passed_G"), 1)
        ledger.section = "after"
        G.l = None
        dma(fin[:, :, :], A_hs, "fin_ld")
        dma(fin_row[:, :], io["final_norm_g"].rearrange("(a e) -> a e", a=1).broadcast_to([P, D]), "fin_ld", "fin_in")
        for t in range(NT):
            eng.wait_ge(*G.at("y", t))
            eng.sem_inc(sems("passed_G"), 1)
            if t < LT:
                dma(out["y_sample"][0, t * P:(t + 1) * P, :], fin[:, t, :], "out_y", "y_out", t)
            else:
                dma(out["y_prompt"][0, :, :], fin[:, t, :], "out_y", "y_out", t)
        eng.wait_ge(*G.at("y_out", NT - 1))
        eng.sem_inc(sems("passed_G"), 1)
        eng.wait_ge(*G.at("kv_out"))
        eng.sem_inc(sems("passed_G"), 1)


_OUTS = [("y_prompt", (1, P, D)), ("y_sample", (1, NLAT, D)), ("new_k", (1, DEPTH, P, NKV, DH)), ("new_v", (1, DEPTH, P, NKV, DH))]


def tables():
    f = np.float32
    grid_w, axis = 64, DH // 2
    row = np.repeat(np.arange(NLAT // grid_w), grid_w).astype(f)
    col = np.tile(np.arange(grid_w), NLAT // grid_w).astype(f)
    inv = (f(1.0) / (f(10000.0) ** (np.arange(0, axis, 2, dtype=f) / f(axis)))).astype(f)
    ar, ac = row[:, None] * inv[None, :], col[:, None] * inv[None, :]
    cos = np.concatenate([np.cos(ar), np.cos(ar), np.cos(ac), np.cos(ac)], axis=-1).astype(f)
    sin = np.concatenate([-np.sin(ar), np.sin(ar), -np.sin(ac), np.sin(ac)], axis=-1).astype(f)
    return cos, sin


def kernel(**inputs):
    from concourse import bacc
    from concourse.bass_utils import run_bass_kernel_spmd

    a = {k: np.asarray(v) for k, v in inputs.items()}

    def cols(x):
        return np.ascontiguousarray(np.swapaxes(x.reshape(*x.shape[:-1], -1, P), -1, -2))

    cos, sin = tables()
    arrays = {
        "x_all": np.concatenate([a["x_sample"][0], a["x_prompt"][0]], axis=0),
        "c_cols": np.ascontiguousarray(np.stack([cols(a["c"][0]), cols(a["c_ctx"])], axis=1)),
        "n1_cols": cols(a["norm1_g"]),
        "conv_w_t": np.ascontiguousarray(a["conv_w"].reshape(DEPTH, TAPS, CCH, P).transpose(0, 3, 2, 1)),
        "conv_b_cols": cols(a["conv_b"]), "ln_g_cols": cols(a["conv_ln_g"]), "ln_b_cols": cols(a["conv_ln_b"]),
        "cos": cos, "sin": sin,
    }
    for name in ("cache_k", "cache_v", "w_ada", "b_ada", "w_in", "q_norm_g", "k_norm_g", "w_attn_o", "w_conv_o", "w_out",
                 "norm2_g", "w_router", "router_bias", "w_gate", "w_up", "w_down", "final_norm_g"):
        arrays[name] = np.ascontiguousarray(a[name])

    def program(ledger):
        nc = bacc.Bacc("TRN2", target_bir_lowering=False, num_devices=1)
        io = {k: nc.dram_tensor(f"in_{k}", x.shape, mybir.dt.from_np(x.dtype), kind="ExternalInput").ap() for k, x in arrays.items()}
        out = {k: nc.dram_tensor(f"out_{k}", s, F32, kind="ExternalOutput").ap() for k, s in _OUTS}
        build(nc, io, out, ledger)
        return nc

    counted = Ledger()
    program(counted)
    counted.order_drains()
    nc = program(Ledger(counted))
    r = run_bass_kernel_spmd(nc, [{f"in_{k}": x for k, x in arrays.items()}], core_ids=[0])
    return tuple(r.results[0][f"out_{k}"] for k, _ in _OUTS)
```

```python
from contextlib import ExitStack

import numpy as np
import concourse.bass as bass
from concourse import mybir

F32, F32R = mybir.dt.float32, mybir.dt.float32r
U32, I32 = mybir.dt.uint32, mybir.dt.int32
ALU, ACT, AX = mybir.AluOpType, mybir.ActivationFunctionType, mybir.AxisListType

P = 128
D = 1024
DEPTH = 2
KC = D // P
LT, NT = 4, 5
NLAT, NTOK = LT * P, NT * P
HALF = NTOK // 2
NH, NKV, DH = 16, 4, 64
GQ = NH // NKV
QW, KVW = NH * DH, NKV * DH
DC, CCH = 512, 4
TAPS, PAD = 31, 15
NE, NG, EPG, DE = 16, 4, 4, 256
EPS = 1e-6
UNIT = 2048
CW = PAD + NLAT + PAD + PAD + P + PAD
CO = CW - 2 * PAD
CTX0 = NLAT + 2 * PAD
MAXT = (2 * NTOK) // P + NE + 1
SKIP = 1 << 20

Q0, K0, GA0, GB0 = 0, QW, QW + 2 * KVW, QW + 2 * KVW + DC
GATE0 = QW + 2 * KVW + 2 * DC
SH1, SC1, G1, SH2, SC2, G2 = (i * D for i in range(6))

N_ADA1, N_QKV, N_GLU, N_ADA2, N_GATE, N_CO, N_OUT, N_ADA3 = 8, 6, 4, 12, 16, 4, 4, 4
U_QKV = N_ADA1
U_GLU = U_QKV + N_QKV
U_ADA2 = U_GLU + N_GLU
U_GATE = U_ADA2 + N_ADA2
U_CO = U_GATE + N_GATE
U_OUT = U_CO + N_CO
U_ADA3 = U_OUT + N_OUT
U_MOE = U_ADA3 + N_ADA3
N_UNITS = U_MOE + 3 * NE


class Ledger:

    def __init__(self, known=None):
        self.known = known
        self.section = "before"
        self.count = {"before": {}, "layer": {}, "after": {}}
        self.events = {}
        self.alias = {}
        self.banks = {}

    def raised(self, sem, event, by):
        n = self.count[self.section].get(sem, 0) + by
        self.count[self.section][sem] = n
        if event is not None:
            assert event not in self.events or self.section == "before", event
            self.events[event] = (sem, self.section, n)

    def order_drains(self):
        n = {}
        for name, b in self.banks.items():
            if ("drained", name) in self.events:
                n[b] = n.get(b, 0) + 1
                sem, section, _ = self.events["drained", name]
                self.events["drained", name] = (sem, section, n[b])

    def value(self, event, l, previous):
        event = self.known.alias.get(event, event)
        sem, section, n = self.known.events[event]
        before = self.known.count["before"].get(sem, 0)
        per = self.known.count["layer"].get(sem, 0)
        if section == "before":
            return sem, n
        if section == "after":
            return sem, before + DEPTH * per + n
        if l is None:
            return sem, before + (DEPTH - 1) * per + n
        n += before - (per if previous else 0)
        assert n > 0, event
        return sem, l * per + n


class Counts:

    def __init__(self, ledger, sems):
        self.led, self.sems, self.l, self.steps = ledger, sems, None, 0

    def at(self, *event, previous=False):
        if self.led.known is None:
            return self.sems("uncounted"), 1
        sem, value = self.led.value(event, self.l, previous)
        return self.sems(sem), value

    def up(self, sem, *event, by=1):
        self.led.raised(sem, event or None, by)
        return self.sems(sem), by

    def step(self):
        self.steps += 1
        return self.up("v_step", "v", self.steps)

    def bank(self, name):
        return self.led.banks.get(name, 0) if self.led.known is None else self.led.known.banks[name]

    def filled(self, name):
        return self.up(f"psum_full{self.bank(name)}", "filled", name)

    def drained(self, name):
        return self.up(f"psum_drained{self.bank(name)}", "drained", name)


def build(nc, io, out, ledger):
    ctx = ExitStack()
    with ctx:
        _build(nc, io, out, ledger, ctx)


def _build(nc, io, out, ledger, ctx):
    semd = {}

    def sems(name):
        if name not in semd:
            semd[name] = ctx.enter_context(nc.semaphore(name))
        return semd[name]

    base = (nc.sbuf_base + 63) // 64 * 64
    KB = 1024
    R_RAW = base
    R_W = R_RAW + 16 * KB
    R_Q = R_W + 32 * KB
    R_U = R_Q + 20 * KB
    R_A = R_U + 40 * KB
    R_G = R_A + 73 * KB
    R_C = R_G + 11 * KB
    top = [R_C]

    def at(name, shape, dt, offset):
        return nc.alloc_sbuf_tensor_at(name, shape, dt, offset=offset)

    def const(name, shape, dt=F32):
        n = int(np.prod(shape[1:])) * 4
        t = at(name, shape, dt, top[0])
        top[0] += (n + 31) // 32 * 32
        assert top[0] <= nc.sbuf_usable_end, name
        return t

    raw = at("raw", [P, 2, UNIT], F32, R_RAW)
    raw_x = [at(f"raw_x{i}", [P, UNIT], F32, R_A + (68 + 8 * i) * KB) for i in range(2)]
    w_hi = at("w_hi", [P, 2, UNIT], F32R, R_W)
    w_lo = at("w_lo", [P, 2, UNIT], F32R, R_W + 16 * KB)
    h_cur = at("h_cur", [P, NT, D], F32, R_Q)
    xn = at("xn", [P, NT, D], F32, R_A + 40 * KB)
    u_hi = at("u_hi", [P, KC, NTOK], F32R, R_U)
    u_lo = at("u_lo", [P, KC, NTOK], F32R, R_U + 20 * KB)
    u_tmp = at("u_tmp", [P, 2, NTOK], F32, R_A)
    q_tok = at("q_tok", [P, NT, QW], F32, R_Q)
    k_hi = at("k_hi", [P, NKV, 6 * P], F32R, R_A)
    k_lo = at("k_lo", [P, NKV, 6 * P], F32R, R_A + 12 * KB)
    v_hl = at("v_hl", [P, 6, NKV, 2 * DH], F32R, R_A + 24 * KB)
    q_st = at("q_st", [P, 2, NTOK], F32R, R_A + 36 * KB)
    probs = at("probs", [P, 2, LT, NTOK], F32, R_A + 41 * KB)
    pt_hi = at("pt_hi", [P, 3, NLAT], F32R, R_A + 61 * KB)
    pt_lo = at("pt_lo", [P, 3, NLAT], F32R, R_A + 67 * KB)
    kr = at("kr", [P, 6, KVW], F32, R_A + 41 * KB)
    vr = at("vr", [P, 6, KVW], F32, R_A + 47 * KB)
    sq = at("sq", [P, D], F32, R_A + 61 * KB)
    rot = at("rot", [P, D], F32, R_A + 65 * KB)
    glu = at("glu", [P, CCH, CW], F32, R_G)
    sgb = at("sgb", [P, 2, NTOK], F32, R_A + 53 * KB)
    o_hi = at("o_hi", [P, KC, NTOK], F32R, R_A)
    o_lo = at("o_lo", [P, KC, NTOK], F32R, R_A + 20 * KB)
    sgc = at("sgc", [P, KC, NTOK], F32, R_A + 40 * KB)
    cv = at("cv", [P, CCH, CO], F32, R_A + 60 * KB)
    sga = at("sga", [P, NTOK], F32, R_A + 60 * KB + 10752)
    o_t = at("o_t", [P, NT, KC, P], F32, R_Q)
    m_t = at("m_t", [P, KC, NTOK], F32, R_Q)
    cn = at("cn", [P, NT, DC], F32, R_G)
    c_hi = at("c_hi", [P, CCH, NTOK], F32R, R_U)
    c_lo = at("c_lo", [P, CCH, NTOK], F32R, R_U + 10 * KB)
    c_f = at("c_f", [P, 2, NTOK], F32, R_U + 30 * KB)
    m_hi = at("m_hi", [P, KC, NTOK], F32R, R_A)
    m_lo = at("m_lo", [P, KC, NTOK], F32R, R_A + 20 * KB)
    m_tmp = at("m_tmp", [P, 2, NTOK], F32, R_U + 35 * KB)
    h_in = at("h_in", [P, NT, D], F32, R_U)
    g1_row = at("g1_row", [P, 2, D], F32, R_U + 20 * KB)
    h_a = at("h_a", [P, NT, D], F32, R_Q)
    a2_row = at("a2_row", [P, 2, D], F32, R_A + 40 * KB)
    b2_row = at("b2_row", [P, 2, D], F32, R_A + 48 * KB)
    n2_row = at("n2_row", [P, D], F32, R_A + 56 * KB)
    u2 = at("u2", [P, NT, D], F32, R_U)
    u2_t = at("u2_t", [P, 2, KC, P], F32, R_A)
    gu_hi = [at(f"gu_hi{i}", [P, KC, 2 * DE], F32R, R_U + 48 * i * KB) for i in range(2)]
    gu_lo = [at(f"gu_lo{i}", [P, KC, 2 * DE], F32R, R_U + (48 * i + 16) * KB) for i in range(2)]
    dn_hi = [at(f"dn_hi{i}", [P, 2, D], F32R, R_U + (48 * i + 32) * KB) for i in range(2)]
    dn_lo = [at(f"dn_lo{i}", [P, 2, D], F32R, R_U + (48 * i + 40) * KB) for i in range(2)]
    xe = at("xe", [P, D], F32, R_Q)
    xt_hi = at("xt_hi", [P, KC, P], F32R, R_Q + 4 * KB)
    xt_lo = at("xt_lo", [P, KC, P], F32R, R_Q + 8 * KB)
    sg = at("sg", [P, DE], F32, R_Q + 12 * KB)
    hx = at("hx", [P, DE], F32, R_Q + 13 * KB)
    ht_hi = at("ht_hi", [P, 2, P], F32R, R_Q + 14 * KB)
    ht_lo = at("ht_lo", [P, 2, P], F32R, R_Q + 15 * KB)
    ye = at("ye", [P, D], F32, R_W)
    tab = at("tab", [P, MAXT, 4], U32, R_W + 4 * KB)
    g2_row = at("g2_row", [P, 2, D], F32, R_W + 8 * KB)
    ha_in = at("ha_in", [P, NT, D], F32, R_A + 8 * KB)
    y_in = at("y_in", [P, NT, 2, D], F32, R_U)
    fin_row = at("fin_row", [P, D], F32, R_A + 30 * KB)
    junk2 = at("junk2", [P, 2, D], F32, R_A + 60 * KB)

    late = [R_W + 16 * KB]

    def routed(name, shape, dt=F32):
        n = int(np.prod(shape[1:])) * 4
        t = at(name, shape, dt, late[0])
        late[0] += (n + 31) // 32 * 32
        assert late[0] <= R_Q, name
        return t

    ident = const("ident", [P, P])
    ones = const("ones", [P, P])
    tri = const("tri", [P, P])
    cs = const("cs", [P, 2, KC])
    craw = const("craw", [P, 2, KC])
    cosr = const("cosr", [P, LT, DH])
    sinr = const("sinr", [P, LT, DH])
    rq = at("rq", [P, 2, LT, DH], F32, R_A + 69 * KB)
    rk = at("rk", [P, 2, LT, DH], F32, R_A + 71 * KB)
    gq = const("gq", [P, 2, DH])
    gp = const("gp", [P, 2, DH])
    mcol = const("mcol", [P, 2, 2, KC])
    n1col = const("n1col", [P, KC])
    convw = const("convw", [P, CCH, TAPS])
    convb = const("convb", [P, CCH])
    lng = const("lng", [P, CCH])
    lnb = const("lnb", [P, CCH])
    ssq = const("ssq", [P, 8])
    std = const("std", [P, 8])
    rstd = const("rstd", [P, 8])
    hss = const("hss", [P, NT, NH + NKV])
    hrs = const("hrs", [P, NT, NH + NKV])
    nmax = const("nmax", [P, 2, LT])
    rsum = const("rsum", [P, 2, LT])
    cmax = const("cmax", [P, GQ])
    csum = const("csum", [P, GQ])
    bst = const("bst", [P, NT, 6])
    bag = const("bag", [P, NT, 2])
    adab = at("adab", [2, 2, 512], F32, R_W + 24 * KB)
    mrow = at("mrow", [2, 2, 512], F32, R_W + 28 * KB)
    osb = const("osb", [DH, NLAT])
    oscb = const("oscb", [DH, P])
    wr = const("wr", [P, KC, NE])
    rb = const("rb", [P, NE])
    eps = const("eps", [P, 1])
    iot = const("iot", [P, NE])
    grpof = const("grpof", [P, NE])
    tokid = const("tokid", [P, NT])
    lg = routed("lg", [P, NT, NE])
    sel = routed("sel", [P, NT, NE])
    msk = routed("msk", [P, 2, NT, NE])
    tmp16 = routed("tmp16", [P, NT, NE])
    pos = routed("pos", [P, NT, NE])
    cnt = routed("cnt", [P, NT, NE])
    pair = routed("pair", [P, NT, NG, 6])
    g8 = routed("g8", [P, NT, 8])
    top8 = routed("top8", [P, NT, 8])
    idx8 = routed("idx8", [P, NT, 8], U32)
    ef = routed("ef", [P, NT, 8])
    wsel = routed("wsel", [P, 2, NT])
    sca = routed("sca", [P, 4, NE])
    start = routed("start", [P, NE + 3])
    start_i = const("start_i", [P, NE + 3], I32)
    tbase = const("tbase", [P, 2])
    slot = routed("slot", [P, 2, NT])
    slot_u = routed("slot_u", [P, 2, NT], U32)
    rows = routed("rows", [P, 2, NT, 4], U32)
    blank = const("blank", [P, MAXT, 4], U32)
    gidx = routed("gidx", [P, 1], U32)
    sidx = routed("sidx", [P, 1], U32)
    wrow = routed("wrow", [P, 1], F32)
    ctxp = const("ctxp", [P, 2, P])
    cpt_hi = const("cpt_hi", [P, 2, P], F32R)
    cpt_lo = const("cpt_lo", [P, 2, P], F32R)
    mrt = const("mrt", [32, P])

    ps = ctx.enter_context(nc.psum_tensor("ps", [P, 8, 512], F32))

    def dram(name, shape, dt=F32):
        return nc.dram_tensor(name, shape, dt, kind="Internal").ap()

    mod_d = dram("mod_d", (2, 6 * D))
    h_d = dram("h_d", (NTOK, D))
    ha_d = dram("ha_d", (NTOK, D))
    u2_d = dram("u2_d", (NTOK, D))
    y_d = dram("y_d", (2 * NTOK, D))
    tab_d = dram("tab_d", (MAXT * P, 4), U32)

    class Banks:

        def __init__(self):
            self.at = 0
            self.of = ledger.banks

        def take(self, name, bank=None):
            b = self.at if bank is None else bank
            self.at = (b + 1) % 8
            self.of[name] = b
            return b

    fills = Banks()

    MM3 = ((0, 0), (0, 1), (1, 0))

    def ALIAS(event, of):
        ledger.alias[event] = of

    def slot_of(n):
        return (n + 2) % 4 if n < U_QKV else n % 2 if n < U_MOE else (n - U_MOE + 2) % 4

    def raw_of(n):
        s = slot_of(n)
        return raw[:, s, :] if s < 2 else raw_x[s - 2][:, :]

    def ada_unit(u):
        if u < N_ADA1:
            return u
        return U_ADA2 + u - N_ADA1 if u < N_ADA1 + N_ADA2 else U_ADA3 + u - N_ADA1 - N_ADA2

    def gate_units(b):
        return U_GATE + 2 * b, U_GATE + 2 * b + 1

    block = ctx.enter_context(nc.Block())

    @block.tensor
    def _(eng):
        T = Counts(ledger, sems)
        last = {}

        def fill(name, bank=None):
            b = fills.take(name, bank)
            if b in last:
                eng.wait_ge(*T.at("drained", last[b]))
            last[b] = name
            return b

        ledger.section = "before"
        eng.wait_ge(*T.at("ident"))
        eng.wait_ge(*T.at("cs"))
        for name in ("y_full", "gu_full"):
            eng.sem_inc(sems(name), 1)
        ledger.section = "layer"
        mm = nc.tensor.matmul
        with eng.Fori(0, DEPTH) as l:
            T.l = l

            def ada(u, rows, bank=None):
                j, kh = divmod(u, 2)
                b = fill(("ada", j), bank) if kh == 0 and rows[0] == 0 else fills.of["ada", j]
                if rows[0] == 0:
                    eng.wait_ge(*T.at("w_raw", ada_unit(u)))
                for c in rows:
                    k = kh * 4 + c
                    ins = mm(ps[0:2, b, :], cs[:, :, k], raw_of(ada_unit(u))[:, c * 512:(c + 1) * 512], start=(k == 0), stop=(k == 7))
                if rows[-1] == 3:
                    if kh == 0:
                        ins.then_inc(*T.up("ada_used", "ada_used", u))
                    else:
                        ins.then_inc(*T.filled(("ada", j)))

            for u in range(N_ADA1):
                ada(u, range(4))

            b = fill(("mcol",))
            eng.wait_ge(*T.at("mrt"))
            eng.sem_inc(sems("passed_T"), 1)
            ins = nc.tensor.transpose(ps[:, b, 0:32], mrt[:, :], ident[0:32, 0:32])
            ins.then_inc(*T.filled(("mcol",)))

            eng.wait_ge(*T.at("xn"))
            for c in range(KC):
                for part, tiles in ((0, range(LT)), (1, (LT,))):
                    b = fill(("uT", c, part))
                    for i, t in enumerate(tiles):
                        ins = nc.tensor.transpose(ps[:, b, i * P:(i + 1) * P], xn[:, t, c * P:(c + 1) * P], ident[:, :])
                    ins.then_inc(*T.filled(("uT", c, part)))

            eng.wait_ge(*T.at("drained", ("uT", KC - 1, 1)))
            eng.wait_ge(*T.at("u_lo_all"))
            for nu in range(3):
                bs = [fill(("qkv", nu, t)) for t in range(NT)]
                for kh in range(2):
                    n = U_QKV + 2 * nu + kh
                    eng.wait_ge(*T.at("w_lo", n))
                    s = (n) % 2
                    for t in range(NT):
                        for c in range(4):
                            k = kh * 4 + c
                            for w, x in MM3:
                                ins = mm(ps[:, bs[t], :], (u_hi, u_lo)[x][:, k, t * P:(t + 1) * P],
                                         (w_hi, w_lo)[w][:, s, c * 512:(c + 1) * 512],
                                         start=(k == 0 and w + x == 0), stop=(k == 7 and w == 1))
                        if kh == 1:
                            ins.then_inc(*T.filled(("qkv", nu, t)))
                    if kh == 0:
                        ins.then_inc(*T.up("w_used", "w_used", n))

            def feature_rows(names, s, cols, nk, xs, last_used=None):
                for half in range(2):
                    b = fill(names[half])
                    for k in range(nk):
                        for w, x in MM3:
                            ins = mm(ps[:, b, 0:HALF], (w_hi, w_lo)[w][:, s, cols(k):cols(k) + P],
                                     xs[x][:, k, half * HALF:(half + 1) * HALF],
                                     start=(k == 0 and w + x == 0), stop=(k == nk - 1 and w == 1))
                    ins.then_inc(*T.filled(names[half]))

            for j in range(CCH):
                eng.wait_ge(*T.at("w_lo", U_GLU + j))
                s = (U_GLU + j) % 2
                feature_rows([("gb", j, i) for i in range(2)], s, lambda k: k * 256 + 128, KC, (u_hi, u_lo))
                feature_rows([("ga", j, i) for i in range(2)], s, lambda k: k * 256, KC, (u_hi, u_lo))

            eng.wait_ge(*T.at("k_ready"))
            for g2 in range(NKV // 2):
                for part, blocks in ((0, range(4)), (1, range(4, 6))):
                    b = fill(("kT", g2, part))
                    for i, blk in enumerate(blocks):
                        ins = nc.tensor.transpose(ps[:, b, i * P:(i + 1) * P], kr[:, blk, g2 * P:(g2 + 1) * P], ident[:, :])
                    ins.then_inc(*T.filled(("kT", g2, part)))

            eng.wait_ge(*T.at("q_ready"))

            def q_transposes(h2):
                b = fill(("qT", h2, 0), 2)
                for t in range(LT):
                    ins = nc.tensor.transpose(ps[:, b, t * P:(t + 1) * P], q_tok[:, t, h2 * P:(h2 + 1) * P], ident[:, :])
                ins.then_inc(*T.filled(("qT", h2, 0)))
                b = fill(("qT", h2, 1), 3)
                ins = nc.tensor.transpose(ps[:, b, 0:P], q_tok[:, LT, h2 * P:(h2 + 1) * P], ident[:, :])
                ins.then_inc(*T.filled(("qT", h2, 1)))

            def scores(h, t):
                if h >= NH:
                    return
                g = h // GQ
                if t == 0:
                    eng.wait_ge(*T.at("q_st", h))
                for i in range(2):
                    b = fill(("S", h, t, i), 2 * ((t + 1) % 2) + i)
                    mm(ps[:, b, 0:HALF], q_st[:, h % 2, t * P:(t + 1) * P], k_hi[:, g, i * HALF:(i + 1) * HALF],
                       start=True, stop=False)
                    ins = mm(ps[:, b, 0:HALF], q_st[:, h % 2, t * P:(t + 1) * P], k_lo[:, g, i * HALF:(i + 1) * HALF],
                             start=False, stop=True)
                    ins.then_inc(*T.filled(("S", h, t, i)))

            def ctx_scores(h):
                if h >= NH:
                    return
                g = h // GQ
                b = fill(("Sc", h), 2)
                mm(ps[:, b, 0:P], q_st[:, h % 2, NLAT:NTOK], k_hi[:, g, NTOK:NTOK + P], start=True, stop=False)
                ins = mm(ps[:, b, 0:P], q_st[:, h % 2, NLAT:NTOK], k_lo[:, g, NTOK:NTOK + P], start=False, stop=True)
                ins.then_inc(*T.filled(("Sc", h)))

            def p_transposes(h, kc):
                b = fill(("PT", h, kc), 4 + (h * NT + kc) % 2)
                for t in range(LT):
                    ins = nc.tensor.transpose(ps[:, b, t * P:(t + 1) * P], probs[:, h % 2, t, kc * P:(kc + 1) * P], ident[:, :])
                ins.then_inc(*T.filled(("PT", h, kc)))

            def values(h, k):
                g = h // GQ
                ob = fill(("O", h), 6) if k == 0 else fills.of["O", h]
                eng.wait_ge(*T.at("drained", ("PT", h, k)))
                for x in range(2):
                    ins = mm(ps[:, ob, :], v_hl[:, k, g, :], (pt_hi, pt_lo)[x][:, (h * NT + k) % 3, :],
                             start=(k == 0 and x == 0), stop=(k == NT - 1 and x == 1))
                if k == NT - 1:
                    ins.then_inc(*T.filled(("O", h)))
                else:
                    ins.then_inc(*T.up("pt_used", "pt_used", h, k))

            def ctx_transpose(h):
                eng.wait_ge(*T.at("ctx_probs", h))
                b = fill(("PTc", h), 3)
                ins = nc.tensor.transpose(ps[:, b, 0:P], ctxp[:, h % 2, :], ident[:, :])
                ins.then_inc(*T.filled(("PTc", h)))

            def ctx_values(h):
                b = fill(("Oc", h), 0)
                eng.wait_ge(*T.at("drained", ("PTc", h)))
                for x in range(2):
                    ins = mm(ps[:, b, 0:P], v_hl[:, 5, h // GQ, :], (cpt_hi, cpt_lo)[x][:, h % 2, :], start=(x == 0), stop=(x == 1))
                ins.then_inc(*T.filled(("Oc", h)))

            q_transposes(0)
            for t in range(LT):
                scores(0, t)
            ctx_scores(0)
            for h in range(NH):
                if h + 1 < NH and (h + 1) % 2 == 0:
                    q_transposes((h + 1) // 2)
                eng.wait_ge(*T.at("probs", h))
                p_transposes(h, 0)
                p_transposes(h, 1)
                if h:
                    ctx_values(h - 1)
                u = N_ADA1 + h
                modulating = u < N_ADA1 + N_ADA2
                if modulating:
                    ada(u, (0,), 7)
                scores(h + 1, 0)
                p_transposes(h, 2)
                values(h, 0)
                scores(h + 1, 1)
                if modulating:
                    ada(u, (1,))
                p_transposes(h, 3)
                values(h, 1)
                scores(h + 1, 2)
                if modulating:
                    ada(u, (2,))
                p_transposes(h, 4)
                values(h, 2)
                scores(h + 1, 3)
                ctx_scores(h + 1)
                ctx_transpose(h)
                values(h, 3)
                values(h, 4)
                if modulating:
                    ada(u, (3,))
            ctx_values(NH - 1)

            def conv_tokens():
                eng.wait_ge(*T.at("cv"))
                for t in range(NT):
                    b = fill(("cvT", t))
                    c0 = t * P if t < LT else CTX0
                    for c in range(CCH):
                        ins = nc.tensor.transpose(ps[:, b, c * P:(c + 1) * P], cv[:, c, c0:c0 + P], ident[:, :])
                    ins.then_inc(*T.filled(("cvT", t)))

            for b8 in range(KC):
                if b8 == KC - 1:
                    conv_tokens()
                eng.wait_ge(*T.at("w_lo", gate_units(b8)[0]))
                s = (gate_units(b8)[0]) % 2
                feature_rows([("gta", b8, i) for i in range(2)], s, lambda k: k * 256, KC, (u_hi, u_lo))
                feature_rows([("gtc", b8, i) for i in range(2)], s, lambda k: k * 256 + 128, KC, (u_hi, u_lo))
                if b8 == 0:
                    eng.wait_ge(*T.at("o_split"))
                eng.wait_ge(*T.at("w_lo", gate_units(b8)[1]))
                s = (gate_units(b8)[1]) % 2
                feature_rows([("ao", b8, i) for i in range(2)], s, lambda k: k * P, KC, (o_hi, o_lo))

            eng.wait_ge(*T.at("cn"))
            for c in range(CCH):
                for part, tiles in ((0, range(LT)), (1, (LT,))):
                    b = fill(("cT", c, part))
                    for i, t in enumerate(tiles):
                        ins = nc.tensor.transpose(ps[:, b, i * P:(i + 1) * P], cn[:, t, c * P:(c + 1) * P], ident[:, :])
                    ins.then_inc(*T.filled(("cT", c, part)))
            eng.wait_ge(*T.at("c_lo", CCH - 1))
            for b8 in range(KC):
                if b8 % 2 == 0:
                    eng.wait_ge(*T.at("w_lo", U_CO + b8 // 2))
                    s = (U_CO + b8 // 2) % 2
                feature_rows([("co", b8, i) for i in range(2)], s, lambda k, b8=b8: k * 256 + b8 % 2 * P, CCH, (c_hi, c_lo))

            eng.wait_ge(*T.at("m_lo", KC - 1))
            for nh in range(2):
                bs = [fill(("wo", nh, t)) for t in range(NT)]
                for kh in range(2):
                    n = U_OUT + 2 * nh + kh
                    eng.wait_ge(*T.at("w_lo", n))
                    s = (n) % 2
                    for t in range(NT):
                        for c in range(4):
                            k = kh * 4 + c
                            for w, x in MM3:
                                ins = mm(ps[:, bs[t], :], (m_hi, m_lo)[x][:, k, t * P:(t + 1) * P],
                                         (w_hi, w_lo)[w][:, s, c * 512:(c + 1) * 512],
                                         start=(k == 0 and w + x == 0), stop=(k == 7 and w == 1))
                        if kh == 1:
                            ins.then_inc(*T.filled(("wo", nh, t)))
                    if kh == 0:
                        ins.then_inc(*T.up("w_used", "w_used", n))

            for u in range(N_ADA1 + N_ADA2, N_ADA1 + N_ADA2 + 2):
                ada(u, range(4), 7)

            def u2_transposes(t):
                eng.wait_ge(*T.at("u2", t))
                for i in range(2):
                    b = fill(("u2T", t, i), (2 * t + i) % 6)
                    for c in range(4):
                        k = i * 4 + c
                        ins = nc.tensor.transpose(ps[:, b, c * P:(c + 1) * P], u2[:, t, k * P:(k + 1) * P], ident[:, :])
                    ins.then_inc(*T.filled(("u2T", t, i)))

            rbank = None
            for t in range(NT + 1):
                if t < NT:
                    u2_transposes(t)
                if t >= 1:
                    if rbank is None:
                        rbank = fill(("router",), 6)
                        eng.wait_ge(*T.at("wr_loaded"))
                    eng.wait_ge(*T.at("drained", ("u2T", t - 1, 1)))
                    eng.wait_ge(*T.at("drained", ("u2T", t - 1, 0)))
                    for k in range(KC):
                        ins = mm(ps[:, rbank, (t - 1) * NE:t * NE], u2_t[:, (t - 1) % 2, k, :], wr[:, k, :],
                                 start=(k == 0), stop=(k == KC - 1))
                    if t == NT:
                        ins.then_inc(*T.filled(("router",)))
                    else:
                        ins.then_inc(*T.up("u2t_used", "u2t_used", t - 1))
            ada(N_ADA1 + N_ADA2 + 2, range(4), 0)
            eng.wait_ge(*T.at("mask"))
            b = fill(("place",))
            mm(ps[:, b, 0:NT * NE], tri[:, :], cnt[:, :, :].rearrange("p t e -> p (t e)"), start=True, stop=True)
            ins = mm(ps[:, b, 256:256 + NT * NE], ones[:, :], cnt[:, :, :].rearrange("p t e -> p (t e)"), start=True, stop=True)
            ins.then_inc(*T.filled(("place",)))
            ada(N_ADA1 + N_ADA2 + 3, range(4), 0)

            for b in range(8):
                eng.wait_ge(*T.at("drained", last[b]))
            eng.wait_ge(*T.at("starts"))
            eng.sem_inc(sems("passed_T"), 1)
            g0 = eng.value_load(start_i[0:1, NE + 1:NE + 2], min_val=1, max_val=DEPTH * MAXT)
            n0 = eng.value_load(start_i[0:1, NE + 2:NE + 3], min_val=0, max_val=DEPTH * MAXT)

            def xe_transposes(g):
                eng.wait_ge(sems("xe_landed"), 16 * (g + l))
                for k in range(KC):
                    ins = nc.tensor.transpose(ps[:, k // 4, (k % 4) * P:(k % 4 + 1) * P], xe[:, k * P:(k + 1) * P], ident[:, :])
                ins.then_inc(sems("xt_full"), 1)

            xe_transposes(g0)
            for e in range(NE):
                eng.wait_ge(*T.at("w_lo", U_MOE + 3 * e + 1))
                eng.sem_inc(sems("passed_T"), 1)
                i = (e + 1) % 2
                lo = eng.value_load(start_i[0:1, e:e + 1], min_val=0, max_val=MAXT - 2)
                hi = eng.value_load(start_i[0:1, e + 1:e + 2], min_val=0, max_val=MAXT - 2)
                with eng.Fori(lo, hi) as j:
                    g, n = g0 + j, n0 + j + 1
                    eng.wait_ge(sems("xt_split"), g)
                    for k in range(KC):
                        for w, x in MM3:
                            ins = mm(ps[:, 2, :], (xt_hi, xt_lo)[x][:, k, :], (gu_hi, gu_lo)[w][i][:, k, :],
                                     start=(k == 0 and w + x == 0), stop=(k == 7 and w == 1))
                    ins.then_inc(sems("gu_full"), 1)
                    eng.wait_ge(sems("h_ready"), n)
                    for c in range(2):
                        ins = nc.tensor.transpose(ps[:, 3, c * P:(c + 1) * P], hx[:, c * P:(c + 1) * P], ident[:, :])
                    ins.then_inc(sems("ht_full"), 1)
                    xe_transposes(g + 1)
                    eng.wait_ge(sems("y_drained"), g)
                    eng.wait_ge(sems("ht_split"), n)
                    eng.wait_ge(*T.at("w_lo", U_MOE + 3 * e + 2))
                    for half in range(2):
                        for c in range(2):
                            for w, x in MM3:
                                ins = mm(ps[:, 4 + half, :], (ht_hi, ht_lo)[x][:, c, :], (dn_hi, dn_lo)[w][i][:, c, half * 512:(half + 1) * 512],
                                         start=(c == 0 and w + x == 0), stop=(c == 1 and w == 1))
                    ins.then_inc(sems("y_full"), 1)
            eng.wait_ge(sems("y_drained"), g0 + hi)
            eng.wait_ge(sems("xt_split"), g0 + hi)

    def used(n):
        if n < U_GLU:
            i = n - U_QKV
            return ("w_used", n) if i % 2 == 0 else ("filled", ("qkv", i // 2, NT - 1))
        if n < U_ADA2:
            return ("filled", ("ga", n - U_GLU, 1))
        if n < U_CO:
            i = n - U_GATE
            return ("filled", (("gtc", "ao")[i % 2], i // 2, 1))
        if n < U_OUT:
            return ("filled", ("co", 2 * (n - U_CO) + 1, 1))
        i = n - U_OUT
        return ("w_used", n) if i % 2 == 0 else ("filled", ("wo", i // 2, NT - 1))

    def raw_free(n):
        if n < U_QKV or U_ADA2 <= n < U_GATE or U_ADA3 <= n < U_MOE:
            u = [ada_unit(u) for u in range(N_ADA1 + N_ADA2 + N_ADA3)].index(n)
            return ("ada_used", u) if u % 2 == 0 else ("filled", ("ada", u // 2))
        return ("w_lo", n)

    def size(n):
        if U_GATE <= n < U_CO and (n - U_GATE) % 2 == 1:
            return KC * P
        if U_CO <= n < U_OUT:
            return CCH * 256
        return UNIT

    A_hs = h_d.rearrange("(t p) d -> p t d", p=P)

    @block.sync
    def _(eng):
        S = Counts(ledger, sems)
        ledger.section = "layer"
        with eng.Fori(0, DEPTH) as l:
            S.l = l

            def load(n, *pieces):
                if n < 4:
                    eng.wait_ge(*S.at("w_lo", N_UNITS - 4 + n, previous=True))
                elif n < U_QKV:
                    eng.wait_ge(*S.at(*raw_free(n - 4)))
                elif n < U_MOE:
                    eng.wait_ge(*S.at(*raw_free(n - 2)))
                elif n < U_MOE + 2:
                    eng.wait_ge(*S.at("filled", ("cT", CCH - 1, 1)))
                    eng.sem_inc(sems("passed_S"), 1)
                    eng.wait_ge(*S.at("drained", ("ao", KC - 1, 1)))
                else:
                    eng.wait_ge(*S.at(*raw_free(n - 4)))
                for i, (dst, src) in enumerate(pieces):
                    eng.dma_start(dst, src).then_inc(*S.up(f"w_raw{slot_of(n)}", *(("w_raw", n) if i == len(pieces) - 1 else ()), by=16))

            def r(n, c):
                return raw_of(n)[:, 0:size(n) if n < U_MOE else UNIT].rearrange("p (c n) -> p c n", c=c)

            def load_ada(u):
                j, kh = divmod(u, 2)
                n = ada_unit(u)
                load(n, (r(n, 4), io["w_ada"][l, kh * 512:(kh + 1) * 512, j * 512:(j + 1) * 512].rearrange("(c p) n -> p c n", p=P)))

            for u in range(N_ADA1):
                load_ada(u)
            for nu in range(3):
                for kh in range(2):
                    n = U_QKV + 2 * nu + kh
                    load(n, (r(n, 4), io["w_in"][l, kh * 512:(kh + 1) * 512, nu * 512:(nu + 1) * 512].rearrange("(c p) n -> p c n", p=P)))
            for j in range(CCH):
                n = U_GLU + j
                load(n, *((r(n, KC)[:, :, i * P:(i + 1) * P],
                           io["w_in"][l, :, c0 + j * P:c0 + (j + 1) * P].rearrange("(c p) n -> p c n", p=P))
                          for i, c0 in enumerate((GA0, GB0))))
            for u in range(N_ADA1, N_ADA1 + N_ADA2):
                load_ada(u)
            for b8 in range(KC):
                n = gate_units(b8)[0]
                load(n, *((r(n, KC)[:, :, i * P:(i + 1) * P],
                           io["w_in"][l, :, c0 + b8 * P:c0 + (b8 + 1) * P].rearrange("(c p) n -> p c n", p=P))
                          for i, c0 in enumerate((GATE0, GATE0 + D))))
                n = gate_units(b8)[1]
                load(n, (r(n, KC), io["w_attn_o"][l, :, b8 * P:(b8 + 1) * P].rearrange("(c p) n -> p c n", p=P)))
            for j in range(N_CO):
                n = U_CO + j
                load(n, (r(n, CCH), io["w_conv_o"][l, :, j * 256:(j + 1) * 256].rearrange("(c p) n -> p c n", p=P)))
            for nh in range(2):
                for kh in range(2):
                    n = U_OUT + 2 * nh + kh
                    load(n, (r(n, 4), io["w_out"][l, kh * 512:(kh + 1) * 512, nh * 512:(nh + 1) * 512].rearrange("(c p) n -> p c n", p=P)))

            def load_gate_up(e):
                for kh in range(2):
                    n = U_MOE + 3 * e + kh
                    load(n, *((r(n, 4)[:, :, i * DE:(i + 1) * DE],
                               io[w][l, e, kh * 512:(kh + 1) * 512, :].rearrange("(c p) n -> p c n", p=P))
                              for i, w in enumerate(("w_gate", "w_up"))))

            load_gate_up(0)
            for u in range(N_ADA1 + N_ADA2, N_ADA1 + N_ADA2 + N_ADA3):
                load_ada(u)
            for e in range(NE):
                if e > 0:
                    load_gate_up(e)
                n = U_MOE + 3 * e + 2
                load(n, (r(n, 2), io["w_down"][l, e, :, :].rearrange("(c p) n -> p c n", p=P)))

    def expert_half(n, hi):
        e, k = (n - U_MOE) // 3, (n - U_MOE) % 3
        i = (e + 1) % 2
        if k == 2:
            return (dn_lo, dn_hi)[hi][i][:, :, :].rearrange("p c n -> p (c n)")
        return (gu_lo, gu_hi)[hi][i][:, 4 * k:4 * k + 4, :].rearrange("p c n -> p (c n)")

    @block.scalar
    def _(eng):
        A = Counts(ledger, sems)
        act = nc.scalar.activation
        ledger.section = "before"
        eng.wait_ge(*A.at("eps"))
        eng.wait_ge(*A.at("c_loaded"))
        act(cs[:, :, :], craw[:, :, :], ACT.Silu).then_inc(*A.up("a_pre", "cs"))
        ledger.section = "layer"
        with eng.Fori(0, DEPTH) as l:
            A.l = l

            def hi(n):
                if n >= U_ADA3:
                    return
                eng.wait_ge(*A.at("w_raw", n))
                if n >= U_QKV + 2:
                    eng.wait_ge(*A.at(*used(n - 2 if n >= U_GATE + 2 or n < U_GATE else n - 2 - N_ADA2)))
                k = size(n)
                act(w_hi[:, n % 2, 0:k], raw[:, n % 2, 0:k], ACT.Copy).then_inc(*A.up("a_hi", "w_hi", n))

            def hi_expert(n):
                eng.wait_ge(*A.at("w_raw", n))
                act(expert_half(n, 1), raw_of(n), ACT.Copy).then_inc(*A.up("a_hi", "w_hi", n))

            for t in range(NT):
                eng.wait_ge(*A.at("h", t, previous=True))
                if t >= 2:
                    eng.wait_ge(*A.at("ss1", t - 2))
                act(junk2[:, t % 2, :], h_cur[:, t, :], ACT.Square, accum_out=ssq[:, t:t + 1]).then_inc(*A.up("a_ss", "ss1", t))
            eng.wait_ge(*A.at("ss1", NT - 1))
            act(std[:, 0:NT], ssq[:, 0:NT], ACT.Sqrt, bias=eps[:, :], scale=1.0 / D).then_inc(*A.up("a_ss", "std1"))
            for n in range(U_QKV, U_QKV + 2):
                hi(n)
            eng.wait_ge(*A.at("acol"))
            for c in range(KC):
                for part, (c0, n) in enumerate(((0, NLAT), (NLAT, P))):
                    eng.wait_ge(*A.at("filled", ("uT", c, part)))
                    b = A.bank(("uT", c, part))
                    act(u_hi[:, c, c0:c0 + n], ps[:, b, 0:n], ACT.Identity,
                              bias=mcol[:, part, 0, c:c + 1], scale=mcol[:, part, 1, c:c + 1]).then_inc(*A.up("a_u", "u_hi", c, part))
            eng.wait_ge(*A.at("h_stored", NT - 1, previous=True))
            for nu in range(3):
                if nu == 2:
                    eng.wait_ge(*A.at("q_hss"))
                    act(hrs[:, :, 0:NH], hss[:, :, 0:NH], ACT.Sqrt, bias=eps[:, :], scale=1.0 / DH).then_inc(*A.up("a_ss", "q_hstd"))
                hi(U_QKV + 2 * nu + 2)
                hi(U_QKV + 2 * nu + 3)
                for t in range(NT):
                    eng.wait_ge(*A.at("filled", ("qkv", nu, t)))
                    b = A.bank(("qkv", nu, t))
                    if nu < 2:
                        act(q_tok[:, t, nu * 512:(nu + 1) * 512], ps[:, b, :], ACT.Copy).then_inc(*A.drained(("qkv", nu, t)))
                    else:
                        act(kr[:, t + 1, :], ps[:, b, 0:KVW], ACT.Copy).then_inc(*A.up("a_kv", "k_raw", t))
                        act(vr[:, t + 1, :], ps[:, b, KVW:2 * KVW], ACT.Copy).then_inc(*A.drained(("qkv", nu, t)))
            eng.wait_ge(*A.at("cache_loaded"))
            eng.wait_ge(*A.at("drained", ("qkv", 2, NT - 1)))
            act(v_hl[:, :, :, 0:DH], vr[:, :, :].rearrange("p b (g d) -> p b g d", g=NKV), ACT.Copy).then_inc(*A.up("a_v", "v_hi"))
            eng.wait_ge(*A.at("k_hss"))
            act(hrs[:, :, NH:NH + NKV], hss[:, :, NH:NH + NKV], ACT.Sqrt, bias=eps[:, :], scale=1.0 / DH).then_inc(*A.up("a_ss", "k_hstd"))
            for j in range(CCH):
                if j + 2 < N_GLU:
                    hi(U_GLU + j + 2)
                if j >= 2:
                    eng.wait_ge(*A.at("glu", j - 2))
                for i in range(2):
                    eng.wait_ge(*A.at("filled", ("gb", j, i)))
                    b = A.bank(("gb", j, i))
                    act(sgb[:, j % 2, i * HALF:(i + 1) * HALF], ps[:, b, 0:HALF], ACT.Sigmoid).then_inc(*A.drained(("gb", j, i)))
            for g2 in range(NKV // 2):
                for part, (c0, n) in enumerate(((0, 512), (512, 256))):
                    eng.wait_ge(*A.at("filled", ("kT", g2, part)))
                    b = A.bank(("kT", g2, part))
                    for x in range(2):
                        for y in range(2):
                            act(k_hi[y * DH:(y + 1) * DH, 2 * g2 + x, c0:c0 + n], ps[x * DH:(x + 1) * DH, b, 0:n], ACT.Copy).then_inc(*A.up("a_k", "k_hi", g2, part, x, y))

            def q_hi(h2):
                for part, (c0, n) in enumerate(((0, NLAT), (NLAT, P))):
                    eng.wait_ge(*A.at("filled", ("qT", h2, part)))
                    b = A.bank(("qT", h2, part))
                    for x in range(2):
                        if h2 >= 1 and part == 0:
                            eng.wait_ge(*A.at("filled", ("Sc", 2 * h2 - 2 + x)))
                        act(q_st[0:DH, x, c0:c0 + n], ps[x * DH:(x + 1) * DH, b, 0:n], ACT.Copy, scale=DH ** -0.5).then_inc(*A.up("a_q", "q_hi", h2, part, x))

            def exps(h, t):
                if h >= NH:
                    return
                eng.wait_ge(*A.at("nmax", h, t))
                eng.wait_ge(*A.at("filled", ("S", h, t, 0)))
                b0 = A.bank(("S", h, t, 0))
                eng.wait_ge(*A.at("filled", ("S", h, t, 1)))
                if h >= 2 and t == 0:
                    eng.wait_ge(*A.at("filled", ("PT", h - 2, NT - 1)))
                ins = act(probs[:, h % 2, t, :].rearrange("p (a b) -> p a b", a=2), ps[:, b0:b0 + 2, 0:HALF], ACT.Exp,
                          bias=nmax[:, h % 2, t:t + 1], accum_out=rsum[:, h % 2, t:t + 1])
                ins.then_inc(*A.drained(("S", h, t, 0)))
                ALIAS(("drained", ("S", h, t, 1)), ("drained", ("S", h, t, 0)))

            def ctx_exp(h):
                if h >= NH:
                    return
                eng.wait_ge(*A.at("cmax", h))
                eng.wait_ge(*A.at("filled", ("Sc", h)))
                b = A.bank(("Sc", h))
                if h >= 2:
                    eng.wait_ge(*A.at("filled", ("PTc", h - 2)))
                act(ctxp[:, h % 2, :], ps[:, b, 0:P], ACT.Exp, bias=cmax[:, h % 2:h % 2 + 1],
                    accum_out=csum[:, h % 2:h % 2 + 1]).then_inc(*A.drained(("Sc", h)))

            def probs_hi(h, kc):
                k = h * NT + kc
                eng.wait_ge(*A.at("filled", ("PT", h, kc)))
                b = A.bank(("PT", h, kc))
                if k >= 3:
                    hh, kk = divmod(k - 3, NT)
                    eng.wait_ge(*A.at(*(("pt_used", hh, kk) if kk < NT - 1 else ("filled", ("O", hh)))))
                act(pt_hi[:, k % 3, :], ps[:, b, :], ACT.Copy).then_inc(*A.up("a_pt", "pt_hi", h, kc))

            def ctx_hi(h):
                eng.wait_ge(*A.at("filled", ("PTc", h)))
                b = A.bank(("PTc", h))
                if h >= 2:
                    eng.wait_ge(*A.at("filled", ("Oc", h - 2)))
                act(cpt_hi[:, h % 2, :], ps[:, b, 0:P], ACT.Copy).then_inc(*A.up("a_pt", "cpt_hi", h))

            def out_half(h):
                eng.wait_ge(*A.at("filled", ("O", h)))
                b = A.bank(("O", h))
                if h >= 1:
                    eng.wait_ge(*A.at("drained", ("O", h - 1)))
                act(osb[:, :], ps[DH:P, b, :], ACT.Copy).then_inc(*A.up("a_o", "o_half", h))

            def ctx_out_half(h):
                eng.wait_ge(*A.at("filled", ("Oc", h)))
                b = A.bank(("Oc", h))
                if h >= 1:
                    eng.wait_ge(*A.at("drained", ("Oc", h - 1)))
                act(oscb[:, :], ps[DH:P, b, 0:P], ACT.Copy).then_inc(*A.up("a_o", "oc_half", h))

            q_hi(0)
            eng.wait_ge(*A.at("kv_free"))
            for t in range(LT):
                exps(0, t)
            ctx_exp(0)
            for h in range(NH):
                if h + 1 < NH and (h + 1) % 2 == 0:
                    q_hi((h + 1) // 2)
                probs_hi(h, 0)
                probs_hi(h, 1)
                if h:
                    ctx_out_half(h - 1)
                probs_hi(h, 2)
                exps(h + 1, 0)
                probs_hi(h, 3)
                exps(h + 1, 1)
                probs_hi(h, 4)
                exps(h + 1, 2)
                exps(h + 1, 3)
                ctx_exp(h + 1)
                ctx_hi(h)
                out_half(h)
                if h == NH - 3:
                    hi(U_GATE)
                    hi(U_GATE + 1)
            ctx_out_half(NH - 1)
            eng.wait_ge(*A.at("drained", ("O", NH - 1)))
            eng.wait_ge(*A.at("drained", ("Oc", NH - 1)))
            for k in range(KC):
                act(o_hi[:, k, :].rearrange("p (t n) -> p t n", t=NT), o_t[:, :, k, :], ACT.Copy).then_inc(*A.up("a_oh", "o_hi", k))
            for b8 in range(KC):
                if b8 == KC - 1:
                    eng.wait_ge(*A.at("cv_var"))
                    act(std[:, 0:NT], bag[:, :, 1], ACT.Sqrt, bias=eps[:, :]).then_inc(*A.up("a_ss", "cstd"))
                if b8 >= 1:
                    eng.wait_ge(*A.at("drained", ("ao", b8 - 1, 1)))
                for i in range(2):
                    eng.wait_ge(*A.at("filled", ("gta", b8, i)))
                    b = A.bank(("gta", b8, i))
                    act(sga[:, i * HALF:(i + 1) * HALF], ps[:, b, 0:HALF], ACT.Sigmoid).then_inc(*A.drained(("gta", b8, i)))
                if b8 == 0:
                    eng.wait_ge(*A.at("o_split"))
                for i in range(2):
                    eng.wait_ge(*A.at("filled", ("gtc", b8, i)))
                    b = A.bank(("gtc", b8, i))
                    act(sgc[:, b8, i * HALF:(i + 1) * HALF], ps[:, b, 0:HALF], ACT.Sigmoid).then_inc(*A.drained(("gtc", b8, i)))
                hi(gate_units(b8)[0] + 2)
                hi(gate_units(b8)[1] + 2)
            for c in range(CCH):
                if c >= 2:
                    eng.wait_ge(*A.at("c_lo", c - 2))
                for part, (c0, n) in enumerate(((0, NLAT), (NLAT, P))):
                    eng.wait_ge(*A.at("filled", ("cT", c, part)))
                    b = A.bank(("cT", c, part))
                    act(c_f[:, c % 2, c0:c0 + n], ps[:, b, 0:n], ACT.Silu, bias=lnb[:, c:c + 1], scale=lng[:, c:c + 1]).then_inc(*A.drained(("cT", c, part)))
                eng.wait_ge(*A.at("drained", ("cT", c, 1)))
                act(c_hi[:, c, :], c_f[:, c % 2, :], ACT.Copy).then_inc(*A.up("a_c", "c_hi", c))
            for j in range(N_CO):
                hi(U_CO + j + 2)
                for b8 in (2 * j, 2 * j + 1):
                    eng.wait_ge(*A.at("merged", b8))
                    act(m_hi[:, b8, :], m_t[:, b8, :], ACT.Copy).then_inc(*A.up("a_m", "m_hi", b8))
            eng.wait_ge(*A.at("filled", ("co", KC - 1, 1)))
            eng.wait_ge(*A.at("m_lo", KC - 1))
            for i in range(2):
                eng.dma_start(g1_row[:, i, :], mod_d[i:i + 1, G1:G1 + D].broadcast_to([P, D])).then_inc(*A.up("rows_in", by=16))
            eng.dma_start(h_in[:, :, :], A_hs).then_inc(*A.up("rows_in", "h_in", by=16))
            for i in range(2):
                eng.dma_start(a2_row[:, i, :], mod_d[i:i + 1, SC2:SC2 + D].broadcast_to([P, D])).then_inc(*A.up("rows_in", by=16))
                eng.dma_start(b2_row[:, i, :], mod_d[i:i + 1, SH2:SH2 + D].broadcast_to([P, D])).then_inc(*A.up("rows_in", by=16))
            eng.dma_start(n2_row[:, :], io["norm2_g"][bass.ds(l, 1), :].broadcast_to([P, D])).then_inc(*A.up("rows_in", "n2_in", by=16))
            for nh in range(2):
                hi(U_OUT + 2 * nh + 2)
                hi(U_OUT + 2 * nh + 3)
            for t in range(NT):
                eng.wait_ge(*A.at("h_a", t))
                if t >= 2:
                    eng.wait_ge(*A.at("ss2", t - 2))
                act(junk2[:, t % 2, :], h_a[:, t, :], ACT.Square, accum_out=ssq[:, t:t + 1]).then_inc(*A.up("a_ss", "ss2", t))
            eng.wait_ge(*A.at("ss2", NT - 1))
            act(std[:, 0:NT], ssq[:, 0:NT], ACT.Sqrt, bias=eps[:, :], scale=1.0 / D).then_inc(*A.up("a_ss", "std2"))
            eng.dma_start(ha_d.rearrange("(t p) d -> p t d", p=P), h_a[:, :, :]).then_inc(*A.up("ha_out", "ha_out", by=16))
            for k in range(2):
                hi_expert(U_MOE + k)
            def u2t(t):
                for i in range(2):
                    eng.wait_ge(*A.at("filled", ("u2T", t, i)))
                    b = A.bank(("u2T", t, i))
                    if t >= 2 and i == 0:
                        eng.wait_ge(*A.at("u2t_used", t - 2))
                    act(u2_t[:, t % 2, 4 * i:4 * i + 4, :].rearrange("p c n -> p (c n)"), ps[:, b, :], ACT.Copy).then_inc(*A.drained(("u2T", t, i)))

            for t in range(NT):
                u2t(t)
            eng.wait_ge(*A.at("u2", NT - 1))
            eng.dma_start(u2_d.rearrange("(t p) d -> p t d", p=P), u2[:, :, :]).then_inc(*A.up("u2_st", "u2_out", by=16))
            eng.wait_ge(*A.at("lg_shift"))
            act(lg[:, :, :], lg[:, :, :], ACT.Exp).then_inc(*A.up("a_rt", "lg_exp"))
            hi_expert(U_MOE + 2)
            eng.wait_ge(*A.at("starts"))
            eng.wait_ge(*A.at("u2_out"))
            eng.wait_ge(*A.at("filled", ("router",)))
            eng.wait_ge(*A.at("rank"))
            eng.sem_inc(sems("passed_A"), 1)
            g0 = eng.value_load(start_i[0:1, NE + 1:NE + 2], min_val=1, max_val=DEPTH * MAXT)
            n0 = eng.value_load(start_i[0:1, NE + 2:NE + 3], min_val=0, max_val=DEPTH * MAXT)

            def xt_hi_of(g):
                eng.wait_ge(sems("xt_full"), g)
                act(xt_hi[:, :, :].rearrange("p (a c) n -> p a (c n)", a=2), ps[:, 0:2, :], ACT.Copy).then_inc(sems("xt_hi"), 1)

            def y_of(n):
                eng.wait_ge(sems("y_full"), n)
                eng.wait_ge(sems("y_sent"), 16 * n)
                act(ye[:, :].rearrange("p (a n) -> p a n", a=2), ps[:, 4:6, :], ACT.Copy).then_inc(sems("y_drained"), 1)

            eng.wait_ge(*A.at("ha_out"))
            xt_hi_of(g0)
            for e in range(NE):
                lo = eng.value_load(start_i[0:1, e:e + 1], min_val=0, max_val=MAXT - 2)
                hi_g = eng.value_load(start_i[0:1, e + 1:e + 2], min_val=0, max_val=MAXT - 2)
                if e == 1:
                    for j in (10, 11):
                        eng.wait_ge(*A.at("mod_out", j))
                    for i in range(2):
                        eng.dma_start(g2_row[:, i, :], mod_d[i:i + 1, G2:G2 + D].broadcast_to([P, D])).then_inc(*A.up("g2_in", "g2_in", i, by=16))
                if e + 1 < NE:
                    if e >= 1:
                        eng.wait_ge(sems("gu_full"), n0 + lo + 1)
                        eng.wait_ge(*A.at("w_lo", U_MOE + 3 * (e - 1) + 2))
                    hi_expert(U_MOE + 3 * (e + 1))
                    hi_expert(U_MOE + 3 * (e + 1) + 1)
                    if e >= 1:
                        eng.wait_ge(sems("y_full"), n0 + lo + 1)
                    hi_expert(U_MOE + 3 * (e + 1) + 2)
                else:
                    eng.wait_ge(*A.at("w_lo", U_MOE + 3 * (e - 1) + 2))
                    eng.wait_ge(sems("y_full"), n0 + lo + 1)
                    eng.dma_start(ha_in[:, :, :], ha_d.rearrange("(t p) d -> p t d", p=P)).then_inc(*A.up("ha_in", "ha_in", by=16))
                with eng.Fori(lo, hi_g) as j:
                    g, n = g0 + j, n0 + j + 1
                    y_of(n)
                    eng.wait_ge(sems("gu_full"), n + 1)
                    act(sg[:, :], ps[:, 2, 0:DE], ACT.Silu).then_inc(sems("sg_ready"), 1)
                    eng.wait_ge(sems("ht_full"), n)
                    act(ht_hi[:, :, :].rearrange("p c n -> p (c n)"), ps[:, 3, 0:2 * P], ACT.Copy).then_inc(sems("ht_hi"), 1)
                    xt_hi_of(g + 1)
            y_of(n0 + hi_g + 1)
            eng.wait_ge(sems("xt_split"), g0 + hi_g)
            eng.wait_ge(sems("xe_landed"), 16 * (g0 + l + hi_g + 1))
            eng.wait_ge(sems("y_sent"), 16 * (n0 + hi_g + 2))
            for t in range(NT):
                eng.dma_start(y_in[:, t, :, :], y_d.rearrange("(x t p) d -> t p x d", p=P, x=2)[t]).then_inc(*A.up(f"y_in{t}", "y_in", t, by=16))

    @block.vector
    def _(eng):
        V = Counts(ledger, sems)
        v = nc.vector
        ledger.section = "before"
        v.memset(tbase[:, 0:1], 1.0).then_inc(*V.up("v_pre"))
        v.memset(tbase[:, 1:2], 0.0).then_inc(*V.up("v_pre", "tbase"))
        eng.sem_inc(*V.up("v_lo", by=4))
        eng.wait_ge(*V.at("x_in"))
        eng.sem_inc(*V.up("v_h", by=NT))
        ledger.section = "layer"
        with eng.Fori(0, DEPTH) as l:
            V.l = l

            def lo(n):
                eng.wait_ge(*V.at("w_hi", n))
                ins = v.tensor_tensor(expert_half(n, 0), raw_of(n), expert_half(n, 1).bitcast(F32), ALU.subtract)
                ins.then_inc(*V.up("v_lo", "w_lo", n))

            eng.wait_ge(*V.at("std1"))
            v.reciprocal(rstd[:, 0:NT], std[:, 0:NT]).then_inc(*V.step())
            eng.wait_ge(*V.at("v", V.steps))
            for t in range(NT):
                ins = v.tensor_scalar(xn[:, t, :], h_cur[:, t, :], rstd[:, t:t + 1], None, ALU.mult)
                ins.then_inc(*V.up("v_xn", *(("xn",) if t == NT - 1 else ())))
            def modulation(j):
                eng.wait_ge(*V.at("filled", ("ada", j)))
                b = V.bank(("ada", j))
                eng.wait_ge(*V.at("ada_bias", j))
                if j >= 2:
                    eng.wait_ge(*V.at("mod_out", j - 2))
                v.tensor_tensor(mrow[:, j % 2, :], ps[0:2, b, :], adab[:, j % 2, :], ALU.add).then_inc(*V.drained(("ada", j)))

            for j in range(4):
                modulation(j)
            eng.wait_ge(*V.at("filled", ("mcol",)))
            b = V.bank(("mcol",))
            eng.wait_ge(*V.at("n1_loaded"))
            v.tensor_copy(mcol[:, :, :, :].rearrange("p a b c -> p (a b c)"), ps[:, b, 0:32]).then_inc(*V.drained(("mcol",)))
            eng.wait_ge(*V.at("drained", ("mcol",)))
            v.tensor_scalar(mcol[:, :, 1, :], mcol[:, :, 1, :], 1.0, None, ALU.add).then_inc(*V.step())
            eng.wait_ge(*V.at("v", V.steps))
            for i in range(2):
                ins = v.tensor_tensor(mcol[:, i, 1, :], mcol[:, i, 1, :], n1col[:, :], ALU.mult)
                ins.then_inc(*V.up("v_acol", *(("acol",) if i == 1 else ())))
            eng.wait_ge(*V.at("acol"))
            for c in range(KC):
                for part, (c0, n) in enumerate(((0, NLAT), (NLAT, P))):
                    eng.wait_ge(*V.at("u_hi", c, part))
                    eng.wait_ge(*V.at("filled", ("uT", c, part)))
                    b = V.bank(("uT", c, part))
                    if c >= 2:
                        eng.wait_ge(*V.at("u_lo", c - 2, part))
                    v.tensor_scalar(u_tmp[:, c % 2, c0:c0 + n], ps[:, b, 0:n], mcol[:, part, 1, c:c + 1],
                                               mcol[:, part, 0, c:c + 1], ALU.mult, ALU.add).then_inc(*V.drained(("uT", c, part)))
                    eng.wait_ge(*V.at("drained", ("uT", c, part)))
                    ins = v.tensor_tensor(u_lo[:, c, c0:c0 + n], u_tmp[:, c % 2, c0:c0 + n],
                                          u_hi[:, c, c0:c0 + n].bitcast(F32), ALU.subtract)
                    ins.then_inc(*V.up("v_u", "u_lo", c, part))
            ALIAS(("u_lo_all",), ("u_lo", KC - 1, 1))
            eng.wait_ge(*V.at("small_loaded"))
            for x in range(2):
                for a in range(2):
                    for y in range(2):
                        v.tensor_copy(gp[:, x, a * 32 + y * 16:a * 32 + y * 16 + 16],
                                             gq[:, x, a * 32 + (1 - y) * 16:a * 32 + (1 - y) * 16 + 16]).then_inc(*V.step())
                        k = V.steps
            eng.wait_ge(*V.at("v", k))
            for x, rr in ((0, rq), (1, rk)):
                v.tensor_tensor(rr[:, 0, :, :], cosr[:, :, :], gq[:, x:x + 1, :].broadcast_to([P, LT, DH]), ALU.mult).then_inc(*V.step())
                v.tensor_tensor(rr[:, 1, :, :], sinr[:, :, :], gp[:, x:x + 1, :].broadcast_to([P, LT, DH]), ALU.mult).then_inc(*V.step())
                k_rope = V.steps

            def normed(x3, t, h0, nh, rr, gain, name):
                n = nh * DH
                v.tensor_tensor(x3, x3, hrs[:, t, h0:h0 + nh].unsqueeze(2).broadcast_to([P, nh, DH]), ALU.mult).then_inc(*V.step())
                eng.wait_ge(*V.at("v", V.steps))
                if t == LT:
                    v.tensor_tensor(x3, x3, gq[:, gain:gain + 1, :].broadcast_to([P, nh, DH]), ALU.mult).then_inc(*V.up("v_rope", name, t))
                    return
                x4 = x3.rearrange("p h (a y i) -> p h a y i", a=2, y=2)
                r4 = rot[:, 0:n].rearrange("p (h a y i) -> p h a y i", h=nh, a=2, y=2)
                s4 = rr[:, 1, t, :].rearrange("p (a y i) -> p a y i", a=2, y=2)
                for a in range(2):
                    for y in range(2):
                        v.tensor_tensor(r4[:, :, a, y, :], x4[:, :, a, 1 - y, :],
                                        s4[:, a, y, :].unsqueeze(1).broadcast_to([P, nh, 16]), ALU.mult).then_inc(*V.step())
                eng.wait_ge(*V.at("v", V.steps))
                v.tensor_tensor(x3, x3, rr[:, 0, t:t + 1, :].broadcast_to([P, nh, DH]), ALU.mult).then_inc(*V.step())
                eng.wait_ge(*V.at("v", V.steps))
                v.tensor_tensor(x3, x3, rot[:, 0:n].rearrange("p (h d) -> p h d", h=nh), ALU.add).then_inc(*V.up("v_rope", name, t))

            for nu in range(2):
                for t in range(NT):
                    eng.wait_ge(*V.at("drained", ("qkv", nu, t)))
                    half = slice((t % 2) * 512, (t % 2) * 512 + 512)
                    if nu or t >= 2:
                        eng.wait_ge(*V.at("v", V.steps))
                    v.tensor_tensor(sq[:, half], q_tok[:, t, nu * 512:(nu + 1) * 512], q_tok[:, t, nu * 512:(nu + 1) * 512], ALU.mult).then_inc(*V.step())
                    eng.wait_ge(*V.at("v", V.steps))
                    v.tensor_reduce(hss[:, t, nu * 8:nu * 8 + 8], sq[:, half].rearrange("p (h d) -> p h d", d=DH), axis=AX.X, op=ALU.add).then_inc(*V.step())
            ALIAS(("q_hss",), ("v", V.steps))
            eng.wait_ge(*V.at("q_hstd"))
            v.reciprocal(hrs[:, :, 0:NH], hrs[:, :, 0:NH]).then_inc(*V.step())
            eng.wait_ge(*V.at("v", V.steps))
            eng.wait_ge(*V.at("v", k_rope))
            for t in range(NT):
                if t:
                    eng.wait_ge(*V.at("q_done", t - 1))
                normed(q_tok[:, t, :].rearrange("p (h d) -> p h d", d=DH), t, 0, NH, rq, 0, "q_done")
            ALIAS(("q_ready",), ("q_done", LT))
            for t in range(NT):
                eng.wait_ge(*V.at("drained", ("qkv", 2, t)))
                place = slice((t % 4) * KVW, (t % 4 + 1) * KVW)
                if t >= 4:
                    eng.wait_ge(*V.at("v", V.steps))
                v.tensor_tensor(sq[:, place], kr[:, t + 1, :], kr[:, t + 1, :], ALU.mult).then_inc(*V.step())
                eng.wait_ge(*V.at("v", V.steps))
                v.tensor_reduce(hss[:, t, NH:NH + NKV], sq[:, place].rearrange("p (h d) -> p h d", d=DH), axis=AX.X, op=ALU.add).then_inc(*V.step())
            ALIAS(("k_hss",), ("v", V.steps))
            eng.wait_ge(*V.at("v_hi"))
            v.tensor_tensor(v_hl[:, :, :, DH:2 * DH], vr[:, :, :].rearrange("p b (g d) -> p b g d", g=NKV),
                            v_hl[:, :, :, 0:DH].bitcast(F32), ALU.subtract).then_inc(*V.up("v_v", "v_lo_half"))
            eng.wait_ge(*V.at("k_hstd"))
            v.reciprocal(hrs[:, :, NH:NH + NKV], hrs[:, :, NH:NH + NKV]).then_inc(*V.step())
            eng.wait_ge(*V.at("v", V.steps))
            for t in range(NT):
                eng.wait_ge(*V.at(*(("k_done", t - 1) if t else ("q_done", LT))))
                normed(kr[:, t + 1, :].rearrange("p (h d) -> p h d", d=DH), t, NH, NKV, rk, 1, "k_done")
            ALIAS(("k_ready",), ("k_done", LT))
            v.memset(glu[:, :, 0:PAD], 0.0).then_inc(*V.step())
            v.memset(glu[:, :, PAD + NLAT:PAD + NLAT + 2 * PAD], 0.0).then_inc(*V.step())
            v.memset(glu[:, :, CW - PAD:CW], 0.0).then_inc(*V.step())
            k_pad = V.steps
            for j in range(CCH):
                for i in range(2):
                    eng.wait_ge(*V.at("filled", ("ga", j, i)))
                    b = V.bank(("ga", j, i))
                    eng.wait_ge(*V.at("drained", ("gb", j, i)))
                    if i == 0:
                        v.tensor_tensor(glu[:, j, PAD:PAD + HALF], ps[:, b, 0:HALF], sgb[:, j % 2, 0:HALF], ALU.mult).then_inc(*V.drained(("ga", j, i)))
                    else:
                        n = NLAT - HALF
                        v.tensor_tensor(glu[:, j, PAD + HALF:PAD + NLAT], ps[:, b, 0:n], sgb[:, j % 2, HALF:NLAT], ALU.mult).then_inc(*V.step())
                        v.tensor_tensor(glu[:, j, PAD + CTX0:PAD + CTX0 + P], ps[:, b, n:HALF], sgb[:, j % 2, NLAT:NTOK], ALU.mult).then_inc(*V.drained(("ga", j, i)))
                ALIAS(("glu", j), ("drained", ("ga", j, 1)))
            for g2 in range(NKV // 2):
                for part, (c0, n) in enumerate(((0, 512), (512, 256))):
                    eng.wait_ge(*V.at("filled", ("kT", g2, part)))
                    b = V.bank(("kT", g2, part))
                    for x in range(2):
                        for y in range(2):
                            eng.wait_ge(*V.at("k_hi", g2, part, 1, 1))
                            ins = v.tensor_tensor(k_lo[y * DH:(y + 1) * DH, 2 * g2 + x, c0:c0 + n], ps[x * DH:(x + 1) * DH, b, 0:n],
                                                  k_hi[y * DH:(y + 1) * DH, 2 * g2 + x, c0:c0 + n].bitcast(F32), ALU.subtract)
                            if x == 1 and y == 1:
                                ins.then_inc(*V.drained(("kT", g2, part)))
                            else:
                                ins.then_inc(*V.step())

            def q_lo(h2):
                for part, (c0, n) in enumerate(((0, NLAT), (NLAT, P))):
                    eng.wait_ge(*V.at("filled", ("qT", h2, part)))
                    b = V.bank(("qT", h2, part))
                    eng.wait_ge(*V.at("q_hi", h2, part, 1))
                    for x in range(2):
                        ins = v.scalar_tensor_tensor(out=q_st[DH:P, x, c0:c0 + n], in0=ps[x * DH:(x + 1) * DH, b, 0:n], scalar=DH ** -0.5,
                                                     in1=q_st[0:DH, x, c0:c0 + n].bitcast(F32), op0=ALU.mult, op1=ALU.subtract)
                        if x == 1:
                            ins.then_inc(*V.drained(("qT", h2, part)))
                        else:
                            ins.then_inc(*V.step())
                for x in range(2):
                    ALIAS(("q_st", 2 * h2 + x), ("drained", ("qT", h2, 1)))

            def maxima(h, t):
                if h >= NH:
                    return
                eng.wait_ge(*V.at("filled", ("S", h, t, 0)))
                b0 = V.bank(("S", h, t, 0))
                eng.wait_ge(*V.at("filled", ("S", h, t, 1)))
                v.tensor_reduce(nmax[:, h % 2, t:t + 1], ps[:, b0:b0 + 2, 0:HALF], axis=AX.XY, op=ALU.max, negate=True).then_inc(*V.up("v_max", "nmax", h, t))

            def ctx_maximum(h):
                if h >= NH:
                    return
                eng.wait_ge(*V.at("filled", ("Sc", h)))
                b = V.bank(("Sc", h))
                v.tensor_reduce(cmax[:, h % 2:h % 2 + 1], ps[:, b, 0:P], axis=AX.X, op=ALU.max, negate=True).then_inc(*V.up("v_max", "cmax", h))

            def normalise(h, tiles):
                if h >= NH:
                    return
                t0, t1 = tiles[0], tiles[-1] + 1
                eng.wait_ge(*V.at("drained", ("S", h, t1 - 1, 0)))
                v.reciprocal(rsum[:, h % 2, t0:t1], rsum[:, h % 2, t0:t1]).then_inc(*V.step())
                eng.wait_ge(*V.at("v", V.steps))
                for t in tiles:
                    ins = v.tensor_scalar(probs[:, h % 2, t, :], probs[:, h % 2, t, :], rsum[:, h % 2, t:t + 1], None, ALU.mult)
                    ins.then_inc(*V.up("v_p", *(("probs", h) if t == LT - 1 else ())))

            def ctx_normalise(h):
                if h >= NH:
                    return
                eng.wait_ge(*V.at("drained", ("Sc", h)))
                v.reciprocal(csum[:, h % 2:h % 2 + 1], csum[:, h % 2:h % 2 + 1]).then_inc(*V.step())
                eng.wait_ge(*V.at("v", V.steps))
                v.tensor_scalar(ctxp[:, h % 2, :], ctxp[:, h % 2, :], csum[:, h % 2:h % 2 + 1], None, ALU.mult).then_inc(*V.up("v_p", "ctx_probs", h))

            def probs_lo(h, kc):
                eng.wait_ge(*V.at("pt_hi", h, kc))
                eng.wait_ge(*V.at("filled", ("PT", h, kc)))
                b = V.bank(("PT", h, kc))
                k = (h * NT + kc) % 3
                v.tensor_tensor(pt_lo[:, k, :], ps[:, b, :], pt_hi[:, k, :].bitcast(F32), ALU.subtract).then_inc(*V.drained(("PT", h, kc)))

            def ctx_lo(h):
                eng.wait_ge(*V.at("cpt_hi", h))
                eng.wait_ge(*V.at("filled", ("PTc", h)))
                b = V.bank(("PTc", h))
                v.tensor_tensor(cpt_lo[:, h % 2, :], ps[:, b, 0:P], cpt_hi[:, h % 2, :].bitcast(F32), ALU.subtract).then_inc(*V.drained(("PTc", h)))

            def ctx_output(h):
                x = h % 2
                eng.wait_ge(*V.at("oc_half", h))
                eng.wait_ge(*V.at("filled", ("Oc", h)))
                b = V.bank(("Oc", h))
                v.tensor_tensor(o_t[x * DH:(x + 1) * DH, LT, h // 2, :], ps[0:DH, b, 0:P], oscb[:, :], ALU.add).then_inc(*V.drained(("Oc", h)))

            def output(h):
                x = h % 2
                eng.wait_ge(*V.at("o_half", h))
                eng.wait_ge(*V.at("filled", ("O", h)))
                b = V.bank(("O", h))
                v.tensor_tensor(o_t[x * DH:(x + 1) * DH, 0:LT, h // 2, :],
                                ps[0:DH, b, :].rearrange("p (t n) -> p t n", t=LT), osb[:, :].rearrange("p (t n) -> p t n", t=LT), ALU.add).then_inc(*V.drained(("O", h)))

            q_lo(0)
            for t in range(LT):
                maxima(0, t)
            ctx_maximum(0)
            normalise(0, range(LT))
            ctx_normalise(0)
            for h in range(NH):
                if h + 1 < NH and (h + 1) % 2 == 0:
                    q_lo((h + 1) // 2)
                probs_lo(h, 0)
                probs_lo(h, 1)
                if h % 2 == 0 and 2 <= h <= 12:
                    modulation(3 + h // 2)
                if h:
                    ctx_output(h - 1)
                maxima(h + 1, 0)
                probs_lo(h, 2)
                maxima(h + 1, 1)
                probs_lo(h, 3)
                maxima(h + 1, 2)
                probs_lo(h, 4)
                maxima(h + 1, 3)
                ctx_maximum(h + 1)
                normalise(h + 1, range(0, 2))
                normalise(h + 1, range(2, LT))
                ctx_normalise(h + 1)
                ctx_lo(h)
                output(h)
            ctx_output(NH - 1)
            for k in range(KC):
                eng.wait_ge(*V.at("o_hi", k))
                v.tensor_tensor(o_lo[:, k, :].rearrange("p (t n) -> p t n", t=NT), o_t[:, :, k, :],
                                      o_hi[:, k, :].rearrange("p (t n) -> p t n", t=NT).bitcast(F32), ALU.subtract).then_inc(*V.up("v_oh", *(("o_split",) if k == KC - 1 else ())))
            eng.wait_ge(*V.at("o_split"))
            eng.wait_ge(*V.at("drained", ("ga", CCH - 1, 1)))
            eng.wait_ge(*V.at("v", k_pad))
            taps = [(k, c) for k in range(TAPS) for c in range(CCH)]
            tap_step = {}
            share = -(-len(taps) // (KC - 2))

            def conv_norm():
                for t in range(NT):
                    eng.wait_ge(*V.at("filled", ("cvT", t)))
                    b = V.bank(("cvT", t))
                    v.bn_stats(bst[:, t, :], ps[:, b, :]).then_inc(*V.step())
                    k = V.steps
                eng.wait_ge(*V.at("v", k))
                eng.sem_inc(sems("passed_V"), 1)
                for t in range(NT):
                    v.bn_aggr(bag[:, t, :], bst[:, t, :]).then_inc(*V.up("v_bn", *(("cv_var",) if t == NT - 1 else ())))
                eng.wait_ge(*V.at("cstd"))
                v.reciprocal(rstd[:, 0:NT], std[:, 0:NT]).then_inc(*V.step())
                eng.wait_ge(*V.at("v", V.steps))
                for t in range(NT):
                    eng.wait_ge(*V.at("filled", ("cvT", t)))
                    b = V.bank(("cvT", t))
                    v.tensor_scalar(cn[:, t, :], ps[:, b, :], bag[:, t, 0:1], rstd[:, t:t + 1], ALU.subtract, ALU.mult).then_inc(*V.drained(("cvT", t)))
                for t in range(NT):
                    eng.wait_ge(*V.at("drained", ("cvT", t)))
                ins = v.memset(ssq[:, 7:8], 0.0)
                ins.then_inc(*V.up("v_cn", "cn"))

            for b8 in range(KC):
                for k, c in taps[b8 * share:(b8 + 1) * share]:
                    src = glu[:, c, k:k + CO]
                    if k == 0:
                        ins = v.tensor_scalar(cv[:, c, :], src, convw[:, c, 0:1], convb[:, c:c + 1], ALU.mult, ALU.add)
                    else:
                        eng.wait_ge(*V.at("v", tap_step[(k - 1, c)]))
                        ins = v.scalar_tensor_tensor(out=cv[:, c, :], in0=src, scalar=convw[:, c, k:k + 1], in1=cv[:, c, :],
                                                     op0=ALU.mult, op1=ALU.add)
                    ins.then_inc(*V.step())
                    tap_step[(k, c)] = V.steps
                for i in range(2):
                    eng.wait_ge(*V.at("filled", ("ao", b8, i)))
                    b = V.bank(("ao", b8, i))
                    eng.wait_ge(*V.at("drained", ("gta", b8, i)))
                    v.tensor_tensor(m_t[:, b8, i * HALF:(i + 1) * HALF], ps[:, b, 0:HALF], sga[:, i * HALF:(i + 1) * HALF], ALU.mult).then_inc(*V.drained(("ao", b8, i)))
                if b8 == KC - 2:
                    ALIAS(("cv",), ("v", tap_step[(TAPS - 1, CCH - 1)]))
                    conv_norm()
            for c in range(CCH):
                eng.wait_ge(*V.at("c_hi", c))
                v.tensor_tensor(c_lo[:, c, :], c_f[:, c % 2, :], c_hi[:, c, :].bitcast(F32), ALU.subtract).then_inc(*V.up("v_c", "c_lo", c))
            def m_lo_of(b8):
                eng.wait_ge(*V.at("m_hi", b8))
                v.tensor_tensor(m_lo[:, b8, :], m_t[:, b8, :], m_hi[:, b8, :].bitcast(F32), ALU.subtract).then_inc(*V.up("v_m", "m_lo", b8))

            for b8 in range(KC):
                for i in range(2):
                    h0 = i * HALF
                    eng.wait_ge(*V.at("filled", ("co", b8, i)))
                    b = V.bank(("co", b8, i))
                    if b8 >= 2:
                        eng.wait_ge(*V.at("merged", b8 - 2))
                    v.tensor_tensor(m_tmp[:, b8 % 2, h0:h0 + HALF], ps[:, b, 0:HALF], sgc[:, b8, h0:h0 + HALF], ALU.mult).then_inc(*V.drained(("co", b8, i)))
                eng.wait_ge(*V.at("drained", ("co", b8, 0)))
                eng.wait_ge(*V.at("drained", ("co", b8, 1)))
                v.tensor_tensor(m_t[:, b8, :], m_t[:, b8, :], m_tmp[:, b8 % 2, :], ALU.add).then_inc(*V.up("v_m2", "merged", b8))
                if b8 >= 1:
                    m_lo_of(b8 - 1)
            m_lo_of(KC - 1)
            eng.wait_ge(*V.at("n2_in"))
            eng.wait_ge(*V.at("m_lo", KC - 1))
            for i in range(2):
                v.scalar_tensor_tensor(out=a2_row[:, i, :], in0=a2_row[:, i, :], scalar=1.0, in1=n2_row[:, :], op0=ALU.add, op1=ALU.mult).then_inc(*V.step())
                k = V.steps
            for nh in range(2):
                cols = slice(nh * 512, (nh + 1) * 512)
                for t in range(NT):
                    eng.wait_ge(*V.at("filled", ("wo", nh, t)))
                    b = V.bank(("wo", nh, t))
                    v.tensor_tensor(h_a[:, t, cols], ps[:, b, :], g1_row[:, t // LT, cols], ALU.mult).then_inc(*V.drained(("wo", nh, t)))
                for t in range(NT):
                    eng.wait_ge(*V.at("drained", ("wo", nh, t)))
                    v.tensor_tensor(h_a[:, t, cols], h_a[:, t, cols], h_in[:, t, cols], ALU.add).then_inc(*V.up("v_ha", *(("h_a", t) if nh else ("h_a0", t))))
            eng.wait_ge(*V.at("std2"))
            v.reciprocal(rstd[:, 0:NT], std[:, 0:NT]).then_inc(*V.step())
            eng.wait_ge(*V.at("v", V.steps))
            eng.wait_ge(*V.at("h_a", NT - 1))
            for t in range(NT):
                v.scalar_tensor_tensor(out=u2[:, t, :], in0=h_a[:, t, :], scalar=rstd[:, t:t + 1], in1=a2_row[:, t // LT, :],
                                                     op0=ALU.mult, op1=ALU.mult).then_inc(*V.step())
                eng.wait_ge(*V.at("v", V.steps))
                v.tensor_tensor(u2[:, t, :], u2[:, t, :], b2_row[:, t // LT, :], ALU.add).then_inc(*V.up("v_u2", "u2", t))
            eng.wait_ge(*V.at("filled", ("router",)))
            b = V.bank(("router",))
            lgp = ps[:, b, 0:NT * NE].rearrange("p (t e) -> p t e", e=NE)
            bc = lambda x: x.unsqueeze(2).broadcast_to([P, NT, NE])
            v.tensor_reduce(ssq[:, 0:NT], lgp, axis=AX.X, op=ALU.max).then_inc(*V.step())
            eng.wait_ge(*V.at("v", V.steps))
            v.tensor_tensor(lg[:, :, :], lgp, bc(ssq[:, 0:NT]), ALU.subtract).then_inc(*V.drained(("router",)))
            ALIAS(("lg_shift",), ("drained", ("router",)))
            eng.wait_ge(*V.at("lg_exp"))
            v.tensor_reduce(ssq[:, 0:NT], lg[:, :, :], axis=AX.X, op=ALU.add).then_inc(*V.step())
            eng.wait_ge(*V.at("v", V.steps))
            v.reciprocal(ssq[:, 0:NT], ssq[:, 0:NT]).then_inc(*V.step())
            eng.wait_ge(*V.at("v", V.steps))
            v.tensor_tensor(lg[:, :, :], lg[:, :, :], bc(ssq[:, 0:NT]), ALU.mult).then_inc(*V.step())
            eng.wait_ge(*V.at("v", V.steps))
            v.tensor_tensor(sel[:, :, :], lg[:, :, :], rb[:, :].unsqueeze(1).broadcast_to([P, NT, NE]), ALU.add).then_inc(*V.step())
            eng.wait_ge(*V.at("v", V.steps))
            s4 = sel[:, :, :].rearrange("p t (g e) -> p t g e", e=EPG)
            for t in range(NT):
                v.tensor_tensor(pair[:, t, :, 0:3], s4[:, t, :, 0:3], s4[:, t, :, 1:4], ALU.add).then_inc(*V.step())
                v.tensor_tensor(pair[:, t, :, 3:5], s4[:, t, :, 0:2], s4[:, t, :, 2:4], ALU.add).then_inc(*V.step())
                v.tensor_tensor(pair[:, t, :, 5:6], s4[:, t, :, 0:1], s4[:, t, :, 3:4], ALU.add).then_inc(*V.step())
            v.memset(g8[:, :, NG:8], -1e30).then_inc(*V.step())
            k = V.steps
            eng.wait_ge(*V.at("v", k))
            v.tensor_reduce(g8[:, :, 0:NG], pair[:, :, :, :], axis=AX.X, op=ALU.max).then_inc(*V.step())
            eng.wait_ge(*V.at("v", V.steps))
            eng.sem_inc(sems("passed_V"), 1)
            for t in range(NT):
                v.max(top8[:, t, :], g8[:, t, :]).then_inc(*V.step())
                k = V.steps
            eng.wait_ge(*V.at("v", k))
            eng.sem_inc(sems("passed_V"), 1)
            for t in range(NT):
                v.max_index(idx8[:, t, :], top8[:, t, :], g8[:, t, :]).then_inc(*V.step())
                k = V.steps
            eng.wait_ge(*V.at("v", k))
            v.tensor_copy(ef[:, :, 0:1], idx8[:, :, 0:1]).then_inc(*V.step())
            eng.wait_ge(*V.at("v", V.steps))
            v.tensor_tensor(tmp16[:, :, :], grpof[:, :].unsqueeze(1).broadcast_to([P, NT, NE]),
                                          bc(ef[:, :, 0]), ALU.is_equal).then_inc(*V.step())
            eng.wait_ge(*V.at("v", V.steps))
            v.tensor_scalar(tmp16[:, :, :], tmp16[:, :, :], 1e30, -1e30, ALU.mult, ALU.add).then_inc(*V.step())
            eng.wait_ge(*V.at("v", V.steps))
            v.tensor_tensor(sel[:, :, :], sel[:, :, :], tmp16[:, :, :], ALU.add).then_inc(*V.step())
            eng.wait_ge(*V.at("v", V.steps))
            eng.wait_ge(*V.at("v", V.steps))
            eng.sem_inc(sems("passed_V"), 1)
            for t in range(NT):
                v.max(top8[:, t, :], sel[:, t, :]).then_inc(*V.step())
                k = V.steps
            eng.wait_ge(*V.at("v", k))
            eng.sem_inc(sems("passed_V"), 1)
            for t in range(NT):
                v.max_index(idx8[:, t, :], top8[:, t, :], sel[:, t, :]).then_inc(*V.step())
                k = V.steps
            eng.wait_ge(*V.at("v", k))
            v.tensor_copy(ef[:, :, :], idx8[:, :, :]).then_inc(*V.step())
            eng.wait_ge(*V.at("v", V.steps))
            iot3 = iot[:, :].unsqueeze(1).broadcast_to([P, NT, NE])
            for x in range(2):
                v.tensor_tensor(msk[:, x, :, :], iot3, bc(ef[:, :, x]), ALU.is_equal).then_inc(*V.step())
                k = V.steps
            eng.wait_ge(*V.at("v", k))
            v.tensor_tensor(cnt[:, :, :], msk[:, 0, :, :], msk[:, 1, :, :], ALU.add).then_inc(*V.up("v_mask", "mask"))
            for x in range(2):
                v.tensor_tensor(tmp16[:, :, :], msk[:, x, :, :], lg[:, :, :], ALU.mult).then_inc(*V.step())
                eng.wait_ge(*V.at("v", V.steps))
                v.tensor_reduce(wsel[:, x, :], tmp16[:, :, :], axis=AX.X, op=ALU.add).then_inc(*V.step())
                eng.wait_ge(*V.at("v", V.steps))
            v.tensor_tensor(ssq[:, 0:NT], wsel[:, 0, :], wsel[:, 1, :], ALU.add).then_inc(*V.step())
            eng.wait_ge(*V.at("v", V.steps))
            v.reciprocal(ssq[:, 0:NT], ssq[:, 0:NT]).then_inc(*V.step())
            eng.wait_ge(*V.at("v", V.steps))
            v.tensor_tensor(wsel[:, :, :], wsel[:, :, :], ssq[:, 0:NT].unsqueeze(1).broadcast_to([P, 2, NT]), ALU.mult).then_inc(*V.step())
            eng.wait_ge(*V.at("v", V.steps))
            eng.wait_ge(*V.at("filled", ("place",)))
            b = V.bank(("place",))
            v.tensor_copy(pos[:, :, :].rearrange("p t e -> p (t e)"), ps[:, b, 0:NT * NE]).then_inc(*V.step())
            eng.wait_ge(*V.at("filled", ("place",)))
            v.tensor_copy(cnt[:, :, :].rearrange("p t e -> p (t e)"), ps[:, b, 256:256 + NT * NE]).then_inc(*V.drained(("place",)))
            eng.wait_ge(*V.at("drained", ("place",)))
            for t in range(1, NT):
                if t == 1:
                    v.tensor_copy(sca[:, 0, :], cnt[:, 0, :]).then_inc(*V.step())
                    eng.wait_ge(*V.at("v", V.steps))
                else:
                    v.tensor_tensor(sca[:, 0, :], sca[:, 0, :], cnt[:, t - 1, :], ALU.add).then_inc(*V.step())
                    eng.wait_ge(*V.at("v", V.steps))
                v.tensor_tensor(pos[:, t, :], pos[:, t, :], sca[:, 0, :], ALU.add).then_inc(*V.step())
                eng.wait_ge(*V.at("v", V.steps))
            v.tensor_tensor(sca[:, 0, :], sca[:, 0, :], cnt[:, NT - 1, :], ALU.add).then_inc(*V.step())
            eng.wait_ge(*V.at("v", V.steps))
            v.tensor_scalar(sca[:, 1, :], sca[:, 0, :], float(P), 1.0, ALU.is_gt, ALU.add).then_inc(*V.step())
            eng.wait_ge(*V.at("v", V.steps))
            for k in range(2, NT):
                v.tensor_scalar(sca[:, 2, :], sca[:, 0, :], float(k * P), None, ALU.is_gt).then_inc(*V.step())
                eng.wait_ge(*V.at("v", V.steps))
                v.tensor_tensor(sca[:, 1, :], sca[:, 1, :], sca[:, 2, :], ALU.add).then_inc(*V.step())
                eng.wait_ge(*V.at("v", V.steps))
            src = 1
            for d in (1, 2, 4, 8):
                dst = 3 if src != 3 else 2
                v.tensor_copy(sca[:, dst, 0:d], sca[:, src, 0:d]).then_inc(*V.step())
                v.tensor_tensor(sca[:, dst, d:NE], sca[:, src, d:NE], sca[:, src, 0:NE - d], ALU.add).then_inc(*V.step())
                eng.wait_ge(*V.at("v", V.steps))
                src = dst
            v.memset(start[:, 0:1], 0.0).then_inc(*V.step())
            v.tensor_copy(start[:, NE + 1:NE + 3], tbase[:, :]).then_inc(*V.step())
            v.tensor_copy(start[:, 1:NE + 1], sca[:, src, :]).then_inc(*V.step())
            eng.wait_ge(*V.at("v", V.steps))
            v.tensor_copy(start_i[:, :], start[:, :]).then_inc(*V.up("v_start", "starts"))
            v.tensor_scalar(sca[:, 0, :], start[:, 0:NE], float(P), None, ALU.mult).then_inc(*V.step())
            eng.wait_ge(*V.at("v", V.steps))
            v.tensor_tensor(pos[:, :, :], pos[:, :, :], sca[:, 0:1, :].broadcast_to([P, NT, NE]), ALU.add).then_inc(*V.step())
            eng.wait_ge(*V.at("v", V.steps))
            for x in range(2):
                v.tensor_tensor(tmp16[:, :, :], msk[:, x, :, :], pos[:, :, :], ALU.mult).then_inc(*V.step())
                eng.wait_ge(*V.at("v", V.steps))
                v.tensor_reduce(slot[:, x, :], tmp16[:, :, :], axis=AX.X, op=ALU.add).then_inc(*V.step())
                eng.wait_ge(*V.at("v", V.steps))
            v.tensor_copy(slot_u[:, :, :], slot[:, :, :]).then_inc(*V.step())
            for x in range(2):
                v.tensor_copy(rows[:, x, :, 0], tokid[:, :]).then_inc(*V.step())
                v.tensor_scalar(rows[:, x, :, 1], tokid[:, :], float(x * NTOK), None, ALU.add).then_inc(*V.step())
                v.tensor_copy(rows[:, x, :, 2].bitcast(F32), wsel[:, x, :]).then_inc(*V.step())
                v.memset(rows[:, x, :, 3], 0).then_inc(*V.step())
                k = V.steps
            v.tensor_tensor(tbase[:, 1:2], start[:, NE:NE + 1], start[:, NE + 2:NE + 3], ALU.add).then_inc(*V.step())
            v.scalar_tensor_tensor(out=tbase[:, 0:1], in0=start[:, NE:NE + 1], scalar=1.0, in1=start[:, NE + 1:NE + 2], op0=ALU.add, op1=ALU.add).then_inc(*V.step())
            k2 = V.steps
            ALIAS(("rank",), ("v", k2))
            eng.wait_ge(*V.at("v", k2))

            modulation(10)
            modulation(11)
            eng.wait_ge(*V.at("u2_out"))
            eng.sem_inc(sems("passed_V"), 1)
            g0 = eng.value_load(start_i[0:1, NE + 1:NE + 2], min_val=1, max_val=DEPTH * MAXT)
            n0 = eng.value_load(start_i[0:1, NE + 2:NE + 3], min_val=0, max_val=DEPTH * MAXT)

            def xt_lo_of(g):
                eng.wait_ge(sems("xt_hi"), g)
                v.tensor_tensor(xt_lo[:, :, :].rearrange("p (a c) n -> p a (c n)", a=2), ps[:, 0:2, :],
                                xt_hi[:, :, :].rearrange("p (a c) n -> p a (c n)", a=2).bitcast(F32), ALU.subtract).then_inc(sems("xt_split"), 1)

            eng.wait_ge(*V.at("tab_in"))
            xt_lo_of(g0)
            for e in range(NE):
                s = eng.value_load(start_i[0:1, e:e + 1], min_val=0, max_val=MAXT - 2)
                s2 = eng.value_load(start_i[0:1, e + 1:e + 2], min_val=0, max_val=MAXT - 2)
                if e + 1 < NE:
                    for k in range(2):
                        lo(U_MOE + 3 * (e + 1) + k)
                with eng.Fori(s, s2) as j:
                    g, n = g0 + j, n0 + j + 1
                    eng.wait_ge(sems("gu_full"), n + 1)
                    v.tensor_copy(wrow[:, :], tab[:, bass.ds(j, 1), 2].bitcast(F32)).then_inc(sems("w_row"), 1)
                    eng.wait_ge(sems("w_row"), n)
                    eng.wait_ge(sems("sg_ready"), n)
                    v.scalar_tensor_tensor(out=hx[:, :], in0=ps[:, 2, DE:2 * DE], scalar=wrow[:, :], in1=sg[:, :],
                                           op0=ALU.mult, op1=ALU.mult).then_inc(sems("h_ready"), 1)
                    eng.wait_ge(sems("ht_hi"), n)
                    v.tensor_tensor(ht_lo[:, :, :].rearrange("p c n -> p (c n)"), ps[:, 3, 0:2 * P],
                                    ht_hi[:, :, :].rearrange("p c n -> p (c n)").bitcast(F32), ALU.subtract).then_inc(sems("ht_split"), 1)
                    xt_lo_of(g + 1)
                if e + 1 < NE:
                    lo(U_MOE + 3 * (e + 1) + 2)
            eng.wait_ge(*V.at("g2_in", 1))
            eng.wait_ge(*V.at("ha_in"))
            for t in range(NT):
                eng.wait_ge(*V.at("y_in", t))
                v.tensor_tensor(y_in[:, t, 0, :], y_in[:, t, 0, :], y_in[:, t, 1, :], ALU.add).then_inc(*V.step())
                eng.wait_ge(*V.at("v", V.steps))
                v.tensor_tensor(y_in[:, t, 0, :], y_in[:, t, 0, :], g2_row[:, t // LT, :], ALU.mult).then_inc(*V.step())
                eng.wait_ge(*V.at("v", V.steps))
                v.tensor_tensor(h_cur[:, t, :], ha_in[:, t, :], y_in[:, t, 0, :], ALU.add).then_inc(*V.up("v_h", "h", t))
        V.l = None
        ledger.section = "after"
        eng.wait_ge(*V.at("fin_std"))
        v.reciprocal(rstd[:, 0:NT], std[:, 0:NT]).then_inc(*V.up("v_fin", "fin_rstd"))
        eng.wait_ge(*V.at("fin_rstd"))
        eng.wait_ge(*V.at("fin_in"))
        for t in range(NT):
            v.scalar_tensor_tensor(out=xn[:, t, :], in0=h_cur[:, t, :], scalar=rstd[:, t:t + 1], in1=fin_row[:, :],
                                         op0=ALU.mult, op1=ALU.mult).then_inc(*V.up("v_fin", "y", t))

    @block.scalar
    def _(eng):
        A = Counts(ledger, sems)
        ledger.section = "after"
        for t in range(NT):
            eng.wait_ge(*A.at("h", t))
            if t >= 2:
                eng.wait_ge(*A.at("fin_ss", t - 2))
            nc.scalar.activation(junk2[:, t % 2, :], h_cur[:, t, :], ACT.Square, accum_out=ssq[:, t:t + 1]).then_inc(*A.up("a_fin", "fin_ss", t))
        eng.wait_ge(*A.at("fin_ss", NT - 1))
        nc.scalar.activation(std[:, 0:NT], ssq[:, 0:NT], ACT.Sqrt, bias=eps[:, :], scale=1.0 / D).then_inc(*A.up("a_fin", "fin_std"))

    @block.gpsimd
    def _(eng):
        G = Counts(ledger, sems)
        g_ = nc.gpsimd
        ledger.section = "before"
        def dma(dst, src, sem, *event):
            eng.dma_start(dst, src).then_inc(*G.up(sem, *event, by=16))
        dma(craw[:, :, :], io["c_cols"], "g_in", "c_loaded")
        dma(h_cur[:, :, :], io["x_all"].rearrange("(t p) d -> p t d", p=P), "x_in", "x_in")
        dma(wr[:, :, :], io["w_router"].rearrange("(c p) e -> p c e", p=P), "g_in2")
        dma(rb[:, :], io["router_bias"].rearrange("(a e) -> a e", a=1).broadcast_to([P, NE]), "g_in2")
        dma(cosr[:, :, :], io["cos"].rearrange("(t p) d -> p t d", p=P), "g_in2")
        dma(sinr[:, :, :], io["sin"].rearrange("(t p) d -> p t d", p=P), "g_in2", "wr_loaded")
        g_.memset(eps[:, :], EPS).then_inc(*G.up("g_c", "eps"))
        g_.memset(ident[:, :], 0.0).then_inc(*G.up("g_c", "id0"))
        g_.memset(ones[:, :], 1.0).then_inc(*G.up("g_c", "ones"))
        g_.memset(tri[:, :], 1.0).then_inc(*G.up("g_c", "tri0"))
        g_.memset(ye[:, :], 0.0).then_inc(*G.up("g_c"))
        eng.wait_ge(*G.at("tri0"))
        eng.sem_inc(sems("passed_G"), 1)
        g_.affine_select(out=tri[:, :], in_=tri[:, :], compare_op=ALU.is_ge, fill=0.0, base=-1, pattern=[[1, P]], channel_multiplier=-1).then_inc(*G.up("g_c", "tri"))
        g_.affine_select(out=ident[:, :], in_=ident[:, :], compare_op=ALU.not_equal, fill=1.0, base=0, pattern=[[-1, P]], channel_multiplier=1).then_inc(*G.up("g_c", "ident_g"))
        g_.iota(iot[:, :], pattern=[[1, NE]], base=0, channel_multiplier=0, allow_small_or_imprecise_dtypes=True).then_inc(*G.up("g_c"))
        g_.iota(grpof[:, :], pattern=[[1, NG], [0, EPG]], base=0, channel_multiplier=0, allow_small_or_imprecise_dtypes=True).then_inc(*G.up("g_c"))
        g_.iota(tokid[:, :], pattern=[[P, NT]], base=0, channel_multiplier=1, allow_small_or_imprecise_dtypes=True).then_inc(*G.up("g_c"))
        g_.memset(blank[:, :, :], 0).then_inc(*G.up("g_c", "blank0"))
        eng.wait_ge(*G.at("blank0"))
        eng.sem_inc(sems("passed_G"), 1)
        g_.memset(blank[:, :, 1:2], SKIP).then_inc(*G.up("g_c", "blank1"))
        eng.wait_ge(*G.at("blank1"))
        eng.sem_inc(sems("passed_G"), 1)
        g_.memset(mrt[:, :], 0.0).then_inc(*G.up("g_c", "ident"))
        for t in range(NT):
            dma(h_d[t * P:(t + 1) * P, :], io["x_all"][t * P:(t + 1) * P, :], "h_st")
        for g in (slice(0, 1), slice(1, MAXT)):
            eng.dma_start(tab_d.rearrange("(p g) f -> p g f", p=P)[:, g, :], blank[:, g, :]).then_inc(sems("y_sent"), 16)
        ledger.section = "layer"
        with eng.Fori(0, DEPTH) as l:
            G.l = l
            def bias(j):
                if j >= 2:
                    eng.wait_ge(*G.at("drained", ("ada", j - 2)))
                    eng.sem_inc(sems("passed_G"), 1)
                for i in range(2):
                    dma(adab[i:i + 1, j % 2, :], io["b_ada"][bass.ds(l, 1), j * 512:(j + 1) * 512], f"ada_b{j % 2}", *(("ada_bias", j) if i else ()))

            def modulation(j):
                eng.wait_ge(*G.at("drained", ("ada", j)))
                eng.sem_inc(sems("passed_G"), 1)
                dma(mod_d[:, j * 512:(j + 1) * 512], mrow[:, j % 2, :], f"mod_st{j % 2}", "mod_out", j)

            bias(0)
            bias(1)
            dma(n1col[:, :], io["n1_cols"][l], "g_n1", "n1_loaded")


            for j in range(4):
                modulation(j)
                if j + 2 < 4:
                    bias(j + 2)
            eng.wait_ge(*G.at("mod_out", 2))
            eng.sem_inc(sems("passed_G"), 1)
            eng.wait_ge(*G.at("mod_out", 3))
            eng.sem_inc(sems("passed_G"), 1)
            for i in range(2):
                dma(mrt[i * 16:(i + 1) * 16, :], mod_d[i, 0:2 * D].rearrange("(r p) -> r p", p=P), "mrt", *(("mrt",) if i else ()))
            def lo(n):
                eng.wait_ge(*G.at("w_hi", n))
                if n >= U_MOE:
                    g_.tensor_tensor(expert_half(n, 0), raw_of(n), expert_half(n, 1).bitcast(F32), ALU.subtract).then_inc(*G.up("g_lo", "w_lo", n))
                    return
                k = size(n)
                g_.tensor_tensor(w_lo[:, n % 2, 0:k], raw[:, n % 2, 0:k], w_hi[:, n % 2, 0:k].bitcast(F32), ALU.subtract).then_inc(*G.up("g_lo", "w_lo", n))

            for n in range(U_QKV, U_QKV + 2):
                lo(n)
            for x, name in enumerate(("q_norm_g", "k_norm_g")):
                dma(gq[:, x, :], io[name][bass.ds(l, 1), :].broadcast_to([P, DH]), "g_small")
            dma(convw[:, :, :], io["conv_w_t"][l], "g_small")
            dma(convb[:, :], io["conv_b_cols"][l], "g_small")
            dma(lng[:, :], io["ln_g_cols"][l], "g_small")
            dma(lnb[:, :], io["ln_b_cols"][l], "g_small", "small_loaded")
            eng.wait_ge(*G.at("u_lo", KC - 1, 1))
            eng.sem_inc(sems("passed_G"), 1)
            eng.wait_ge(*G.at("std1"))
            eng.sem_inc(sems("passed_G"), 1)
            dma(kr[:, 0, :], io["cache_k"][0, l].rearrange("s h d -> s (h d)"), "cache")
            dma(vr[:, 0, :], io["cache_v"][0, l].rearrange("s h d -> s (h d)"), "cache", "cache_loaded")
            eng.wait_ge(sems("y_sent"), 32)
            eng.sem_inc(sems("passed_G"), 1)
            dma(tab_d.rearrange("(p g) f -> p g f", p=P), blank[:, :, :], "g_blank", "blanked")

            for n in range(U_QKV + 2, U_ADA2):
                lo(n)
            eng.wait_ge(*G.at("h_stored", NT - 1, previous=True))
            eng.sem_inc(sems("passed_G"), 1)
            eng.wait_ge(*G.at(*used(U_ADA2 - 1)))
            eng.sem_inc(sems("passed_G"), 1)
            bias(4)
            bias(5)
            eng.wait_ge(*G.at("k_done", LT))
            eng.sem_inc(sems("passed_G"), 1)
            dma(out["new_k"][0, l].rearrange("s h d -> s (h d)"), kr[:, 5, :], "out_kv")
            dma(out["new_v"][0, l].rearrange("s h d -> s (h d)"), vr[:, 5, :], "out_kv", "kv_out")
            eng.wait_ge(*G.at("kv_out"))
            eng.sem_inc(sems("passed_G"), 1)
            g_.memset(ssq[:, 6:7], 0.0).then_inc(*G.up("g_c", "kv_free"))
            for j in range(4, 10):
                modulation(j)
                if j + 2 < 10:
                    bias(j + 2)
            eng.wait_ge(*G.at("mod_out", 8))
            eng.wait_ge(*G.at("mod_out", 9))
            for n in range(U_GATE, U_ADA3):
                lo(n)
            eng.wait_ge(*G.at(*used(U_ADA3 - 1)))
            eng.sem_inc(sems("passed_G"), 1)
            bias(10)
            bias(11)
            for n in range(U_MOE, U_MOE + 2):
                lo(n)
            eng.wait_ge(*G.at("rank"))
            eng.sem_inc(sems("passed_G"), 1)
            eng.wait_ge(*G.at("blanked"))
            eng.sem_inc(sems("passed_G"), 1)
            for x in range(2):
                for t in range(NT):
                    eng.indirect_dma_start(out=tab_d, out_offset=bass.IndirectOffsetOnAxis(ap=slot_u[:, x, t:t + 1], axis=0),
                                                 in_=rows[:, x, t, :], in_offset=None, bounds_check=MAXT * P - 1, oob_is_err=False).then_inc(*G.up("tab_st", "tab_row", x, t, by=16))
            eng.wait_ge(*G.at("tab_row", 1, NT - 1))
            eng.sem_inc(sems("passed_G"), 1)
            dma(tab[:, :, :], tab_d.rearrange("(g p) f -> p g f", p=P), "tab_ld", "tab_in")
            lo(U_MOE + 2)
            eng.wait_ge(*G.at("tab_in"))
            eng.sem_inc(sems("passed_G"), 1)
            eng.wait_ge(*G.at("u2_out"))
            eng.sem_inc(sems("passed_G"), 1)
            eng.wait_ge(*G.at("ha_out"))
            eng.sem_inc(sems("passed_G"), 1)
            modulation(10)
            modulation(11)
            g0 = eng.value_load(start_i[0:1, NE + 1:NE + 2], min_val=1, max_val=DEPTH * MAXT)
            n0 = eng.value_load(start_i[0:1, NE + 2:NE + 3], min_val=0, max_val=DEPTH * MAXT)

            def wait_apart(sem, value):
                eng.wait_ge(sems(sem), value)
                eng.sem_inc(sems("passed_G"), 1)

            def gather(j):
                at_j = tab[:, bass.ds(j, 1), 0] if not isinstance(j, int) else tab[:, j:j + 1, 0]
                g_.tensor_copy(gidx[:, :], at_j).then_inc(sems("g_idx"), 1)
                wait_apart("g_idx", g0 + l + j)
                eng.indirect_dma_start(out=xe[:, :], out_offset=None, in_=u2_d,
                                       in_offset=bass.IndirectOffsetOnAxis(ap=gidx[:, :], axis=0),
                                       bounds_check=NTOK - 1, oob_is_err=False).then_inc(sems("xe_landed"), 16)

            gather(0)
            wait_apart("xt_full", g0)
            gather(1)
            for e in range(NE):
                s = eng.value_load(start_i[0:1, e:e + 1], min_val=0, max_val=MAXT - 2)
                s2 = eng.value_load(start_i[0:1, e + 1:e + 2], min_val=0, max_val=MAXT - 2)
                with eng.Fori(s, s2) as j:
                    g, n = g0 + j, n0 + j + 1
                    wait_apart("xt_full", g + 1)
                    gather(j + 2)
                    wait_apart("y_sent", 16 * (n + 1))
                    g_.tensor_copy(sidx[:, :], tab[:, bass.ds(j, 1), 1]).then_inc(sems("s_idx"), 1)
                    eng.wait_ge(sems("s_idx"), n)
                    wait_apart("y_drained", g + 1)
                    eng.indirect_dma_start(out=y_d, out_offset=bass.IndirectOffsetOnAxis(ap=sidx[:, :], axis=0),
                                           in_=ye[:, :], in_offset=None,
                                           bounds_check=2 * NTOK - 1, oob_is_err=False).then_inc(sems("y_sent"), 16)
            for t in range(NT):
                eng.wait_ge(*G.at("h", t))
                eng.sem_inc(sems("passed_G"), 1)
                dma(h_d[t * P:(t + 1) * P, :], h_cur[:, t, :], "h_st", "h_stored", t)
        ledger.section = "after"
        G.l = None
        dma(fin_row[:, :], io["final_norm_g"].rearrange("(a e) -> a e", a=1).broadcast_to([P, D]), "fin_ld", "fin_in")
        for t in range(NT):
            eng.wait_ge(*G.at("y", t))
            eng.sem_inc(sems("passed_G"), 1)
            if t < LT:
                dma(out["y_sample"][0, t * P:(t + 1) * P, :], xn[:, t, :], "out_y", "y_out", t)
            else:
                dma(out["y_prompt"][0, :, :], xn[:, t, :], "out_y", "y_out", t)
        eng.wait_ge(*G.at("h_stored", NT - 1))
        eng.sem_inc(sems("passed_G"), 1)
        eng.wait_ge(*G.at("y_out", NT - 1))
        eng.sem_inc(sems("passed_G"), 1)
        eng.wait_ge(*G.at("kv_out"))
        eng.sem_inc(sems("passed_G"), 1)


_OUTS = [("y_prompt", (1, P, D)), ("y_sample", (1, NLAT, D)), ("new_k", (1, DEPTH, P, NKV, DH)), ("new_v", (1, DEPTH, P, NKV, DH))]


def tables():
    f = np.float32
    grid_w, axis = 64, DH // 2
    row = np.repeat(np.arange(NLAT // grid_w), grid_w).astype(f)
    col = np.tile(np.arange(grid_w), NLAT // grid_w).astype(f)
    inv = (f(1.0) / (f(10000.0) ** (np.arange(0, axis, 2, dtype=f) / f(axis)))).astype(f)
    ar, ac = row[:, None] * inv[None, :], col[:, None] * inv[None, :]
    cos = np.concatenate([np.cos(ar), np.cos(ar), np.cos(ac), np.cos(ac)], axis=-1).astype(f)
    sin = np.concatenate([-np.sin(ar), np.sin(ar), -np.sin(ac), np.sin(ac)], axis=-1).astype(f)
    return cos, sin


def kernel(**inputs):
    from concourse import bacc
    from concourse.bass_utils import run_bass_kernel_spmd

    a = {k: np.asarray(v) for k, v in inputs.items()}

    def cols(x):
        return np.ascontiguousarray(np.swapaxes(x.reshape(*x.shape[:-1], -1, P), -1, -2))

    cos, sin = tables()
    arrays = {
        "x_all": np.concatenate([a["x_sample"][0], a["x_prompt"][0]], axis=0),
        "c_cols": np.ascontiguousarray(np.stack([cols(a["c"][0]), cols(a["c_ctx"])], axis=1)),
        "n1_cols": cols(a["norm1_g"]),
        "conv_w_t": np.ascontiguousarray(a["conv_w"].reshape(DEPTH, TAPS, CCH, P).transpose(0, 3, 2, 1)),
        "conv_b_cols": cols(a["conv_b"]), "ln_g_cols": cols(a["conv_ln_g"]), "ln_b_cols": cols(a["conv_ln_b"]),
        "cos": cos, "sin": sin,
    }
    for name in ("cache_k", "cache_v", "w_ada", "b_ada", "w_in", "q_norm_g", "k_norm_g", "w_attn_o", "w_conv_o", "w_out",
                 "norm2_g", "w_router", "router_bias", "w_gate", "w_up", "w_down", "final_norm_g"):
        arrays[name] = np.ascontiguousarray(a[name])

    def program(ledger):
        nc = bacc.Bacc("TRN2", target_bir_lowering=False, num_devices=1)
        io = {k: nc.dram_tensor(f"in_{k}", x.shape, mybir.dt.from_np(x.dtype), kind="ExternalInput").ap() for k, x in arrays.items()}
        out = {k: nc.dram_tensor(f"out_{k}", s, F32, kind="ExternalOutput").ap() for k, s in _OUTS}
        build(nc, io, out, ledger)
        return nc

    counted = Ledger()
    program(counted)
    counted.order_drains()
    nc = program(Ledger(counted))
    r = run_bass_kernel_spmd(nc, [{f"in_{k}": x for k, x in arrays.items()}], core_ids=[0])
    return tuple(r.results[0][f"out_{k}"] for k, _ in _OUTS)
```
